# Optimizing a Trainium2 kernel written in Bass

```python
import math
import jax
import jax.numpy as jnp
from jax import lax
import numpy as np
import jax, jax.numpy as jnp

D_MODEL = 1024
BATCH = 1
SEQ = 256
DEPTH = 2

HEAD_DIM = 64
Q_BLOCK = 128
GLA_HEADS = 4
GLA_DK = 64
GLA_DV = 128
GLA_GATE_RANK = 16
GLA_GATE_TAU = 16.0
GLA_CHUNK = 64
DSA_HEADS = 8
IDX_HEADS = 8
IDX_DIM = 64
DSA_TOPK_MAX = 256
FOX_HEADS = 8
FORGET_BIAS_MEAN = 2.0
DIL_HEADS = 8
DIL_PATTERNS = ((128, 1), (512, 4), (2048, 16))
REL_BUCKETS = 32
REL_MAX_DIST = 2048
REL_HEADS = 8
D_FF = 2816
N_EXPERTS = 8
TOP_K = 2
D_FF_EXPERT = 3584
ALPHA = (2 * DEPTH) ** 0.25
BETA = (8 * DEPTH) ** -0.25
LN_EPS = 1e-5

AB_SPLITS = (GLA_HEADS * GLA_DK, GLA_HEADS * GLA_DK, GLA_HEADS * GLA_DV, GLA_HEADS * GLA_DV, GLA_GATE_RANK,
             DSA_HEADS * HEAD_DIM, DSA_HEADS * HEAD_DIM, DSA_HEADS * HEAD_DIM,
             IDX_HEADS * IDX_DIM, IDX_DIM, IDX_HEADS)
CD_SPLITS = (FOX_HEADS * HEAD_DIM, FOX_HEADS * HEAD_DIM, FOX_HEADS * HEAD_DIM, FOX_HEADS,
             DIL_HEADS * HEAD_DIM, DIL_HEADS * HEAD_DIM, DIL_HEADS * HEAD_DIM)
W_AB = sum(AB_SPLITS)
W_CD = sum(CD_SPLITS)
MIX_AB = GLA_HEADS * GLA_DV + DSA_HEADS * HEAD_DIM
MIX_CD = (FOX_HEADS + DIL_HEADS) * HEAD_DIM


def _split(y, sizes):
    idx = [int(v) for v in np.cumsum(sizes)[:-1]]
    return jnp.split(y, idx, axis=-1)

def _layernorm(x, g, b):
    xf = x.astype(jnp.float32)
    mu = jnp.mean(xf, axis=-1, keepdims=True)
    var = jnp.mean(jnp.square(xf - mu), axis=-1, keepdims=True)
    return ((xf - mu) * lax.rsqrt(var + LN_EPS) * g + b).astype(x.dtype)

def _rel_bucket(dist):
    max_exact = REL_BUCKETS // 2
    d = jnp.maximum(dist, 0)
    df = jnp.maximum(d, 1).astype(jnp.float32)
    large = max_exact + (jnp.log(df / max_exact) / math.log(REL_MAX_DIST / max_exact)
                         * (REL_BUCKETS - max_exact)).astype(jnp.int32)
    large = jnp.minimum(large, REL_BUCKETS - 1)
    return jnp.where(d < max_exact, d, large)

def _gla(q, k, v, g_log):
    B, L, H, dk = q.shape
    dv = v.shape[-1]
    C = GLA_CHUNK
    n = L // C

    def to_chunks(t):
        return t.reshape(B, n, C, H, t.shape[-1]).transpose(1, 0, 3, 2, 4)

    qc, kc, vc, gc = (to_chunks(q * dk ** -0.5), to_chunks(k), to_chunks(v), to_chunks(g_log))
    causal = jnp.tril(jnp.ones((C, C), dtype=bool))[None, None, :, :, None]

    def step(S, inp):
        qi, ki, vi, gi = inp
        G = jnp.cumsum(gi.astype(jnp.float32), axis=2)
        o_inter = jnp.einsum('bhck,bhkv->bhcv', qi * jnp.exp(G), S)
        diff = G[:, :, :, None, :] - G[:, :, None, :, :]
        decay = jnp.exp(jnp.where(causal, diff, -jnp.inf))
        A = jnp.einsum('bhtk,bhsk,bhtsk->bhts', qi, ki, decay)
        o_intra = jnp.einsum('bhts,bhsv->bhtv', A, vi)
        G_last = G[:, :, -1:, :]
        S_new = (jnp.exp(G_last[:, :, 0, :, None]) * S
                 + jnp.einsum('bhsk,bhsv->bhkv', ki * jnp.exp(G_last - G), vi))
        return S_new, o_inter + o_intra

    S0 = jnp.zeros((B, H, dk, dv), jnp.float32)
    _, o = lax.scan(step, S0, (qc, kc, vc, gc))
    return o.transpose(1, 0, 3, 2, 4).reshape(B, L, H, dv).astype(v.dtype)

def _dsa(q, k, v, q_idx, k_idx, w_idx, rel_table):
    B, L, H, dh = q.shape
    topk = min(DSA_TOPK_MAX, L // 4)
    pos = jnp.arange(L)
    gather = jax.vmap(lambda t, i: t[i])

    def block(i):
        q0 = i * Q_BLOCK
        tq = q0 + jnp.arange(Q_BLOCK)
        qib = lax.dynamic_slice_in_dim(q_idx, q0, Q_BLOCK, axis=1)
        wib = lax.dynamic_slice_in_dim(w_idx, q0, Q_BLOCK, axis=1)
        s = jnp.einsum('bqhd,bkd->bhqk', qib, k_idx).astype(jnp.float32)
        score = jnp.einsum('bqh,bhqk->bqk', wib.astype(jnp.float32), jax.nn.relu(s))
        causal = pos[None, :] <= tq[:, None]
        score = jnp.where(causal[None], score, -jnp.inf)
        _, sel = lax.top_k(score, topk)
        valid = sel <= tq[None, :, None]
        ksel = gather(k, sel)
        vsel = gather(v, sel)
        qb = lax.dynamic_slice_in_dim(q, q0, Q_BLOCK, axis=1)
        logits = jnp.einsum('bqhd,bqkhd->bhqk', qb, ksel).astype(jnp.float32) * dh ** -0.5
        bias = rel_table[_rel_bucket(tq[None, :, None] - sel)]
        logits = logits + bias.transpose(0, 3, 1, 2).astype(jnp.float32)
        logits = jnp.where(valid[:, None], logits, -jnp.inf)
        p = jax.nn.softmax(logits, axis=-1)
        return jnp.einsum('bhqk,bqkhd->bqhd', p.astype(v.dtype), vsel)

    out = lax.map(block, jnp.arange(L // Q_BLOCK))
    return out.transpose(1, 0, 2, 3, 4).reshape(B, L, H, dh)

def _fox(q, k, v, log_f):
    B, L, H, dh = q.shape
    F = jnp.cumsum(log_f, axis=1).transpose(0, 2, 1)
    pos = jnp.arange(L)

    def block(i):
        q0 = i * Q_BLOCK
        tq = q0 + jnp.arange(Q_BLOCK)
        qb = lax.dynamic_slice_in_dim(q, q0, Q_BLOCK, axis=1)
        Fq = lax.dynamic_slice_in_dim(F, q0, Q_BLOCK, axis=2)
        logits = (jnp.einsum('bqhd,bkhd->bhqk', qb, k).astype(jnp.float32) * dh ** -0.5
                  + Fq[..., None] - F[:, :, None, :])
        causal = pos[None, :] <= tq[:, None]
        logits = jnp.where(causal[None, None], logits, -jnp.inf)
        p = jax.nn.softmax(logits, axis=-1)
        return jnp.einsum('bhqk,bkhd->bqhd', p.astype(v.dtype), v)

    out = lax.map(block, jnp.arange(L // Q_BLOCK))
    return out.transpose(1, 0, 2, 3, 4).reshape(B, L, H, dh)

def _dilated(q, k, v, rel_table):
    B, L, H, dh = q.shape

    def block(i):
        q0 = i * Q_BLOCK
        tq = q0 + jnp.arange(Q_BLOCK)
        qb = lax.dynamic_slice_in_dim(q, q0, Q_BLOCK, axis=1)
        outs, log_den = [], []
        for window, dil in DIL_PATTERNS:
            offs = dil * jnp.arange(window // dil + 1)
            idx = tq[:, None] - offs[None, :]
            valid = idx >= 0
            idxc = jnp.maximum(idx, 0)
            ksel = k[:, idxc]
            vsel = v[:, idxc]
            bias = rel_table[_rel_bucket(offs)].T.astype(jnp.float32)
            lg = (jnp.einsum('bqhd,bqjhd->bhqj', qb, ksel).astype(jnp.float32) * dh ** -0.5
                  + bias[None, :, None, :])
            lg = jnp.where(valid[None, None], lg, -jnp.inf)
            m = jnp.max(lg, axis=-1, keepdims=True)
            e = jnp.exp(lg - m)
            s = jnp.sum(e, axis=-1, keepdims=True)
            outs.append(jnp.einsum('bhqj,bqjhd->bhqd', e, vsel.astype(jnp.float32)) / s)
            log_den.append(m + jnp.log(s))
        wts = jax.nn.softmax(jnp.stack(log_den, 0), axis=0)
        o = jnp.sum(wts * jnp.stack(outs, 0), axis=0)
        return o.transpose(0, 2, 1, 3).astype(v.dtype)

    out = lax.map(block, jnp.arange(L // Q_BLOCK))
    return out.transpose(1, 0, 2, 3, 4).reshape(B, L, H, dh)

def _mixer_ab(x, w_in, w_gate, b_gate, g_norm, w_out, rel_table):
    B, L, _ = x.shape
    y = x @ w_in
    qa, ka, va, ra, ga, qb, kb, vb, qi, ki, wi = _split(y, AB_SPLITS)
    g_log = jax.nn.log_sigmoid((ga @ w_gate + b_gate).astype(jnp.float32)) / GLA_GATE_TAU
    oa = _gla(qa.reshape(B, L, GLA_HEADS, GLA_DK), ka.reshape(B, L, GLA_HEADS, GLA_DK),
              va.reshape(B, L, GLA_HEADS, GLA_DV), g_log.reshape(B, L, GLA_HEADS, GLA_DK))
    of = oa.astype(jnp.float32)
    of = of * lax.rsqrt(jnp.mean(jnp.square(of), axis=-1, keepdims=True) + LN_EPS) * g_norm
    oa = of.astype(x.dtype) * jax.nn.silu(ra.reshape(B, L, GLA_HEADS, GLA_DV))
    ob = _dsa(qb.reshape(B, L, DSA_HEADS, HEAD_DIM), kb.reshape(B, L, DSA_HEADS, HEAD_DIM),
              vb.reshape(B, L, DSA_HEADS, HEAD_DIM), qi.reshape(B, L, IDX_HEADS, IDX_DIM), ki, wi, rel_table)
    o = jnp.concatenate([oa.reshape(B, L, -1), ob.reshape(B, L, -1)], axis=-1)
    return o @ w_out

def _mixer_cd(x, w_in, b_forget, w_out, rel_table):
    B, L, _ = x.shape
    y = x @ w_in
    qc, kc, vc, fc, qd, kd, vd = _split(y, CD_SPLITS)
    log_f = jax.nn.log_sigmoid((fc + b_forget).astype(jnp.float32))
    oc = _fox(qc.reshape(B, L, FOX_HEADS, HEAD_DIM), kc.reshape(B, L, FOX_HEADS, HEAD_DIM),
              vc.reshape(B, L, FOX_HEADS, HEAD_DIM), log_f)
    od = _dilated(qd.reshape(B, L, DIL_HEADS, HEAD_DIM), kd.reshape(B, L, DIL_HEADS, HEAD_DIM),
                  vd.reshape(B, L, DIL_HEADS, HEAD_DIM), rel_table)
    o = jnp.concatenate([oc.reshape(B, L, -1), od.reshape(B, L, -1)], axis=-1)
    return o @ w_out

def _swiglu(x, w1, w3, w2):
    return (jax.nn.silu(x @ w1) * (x @ w3)) @ w2

def _moe(x, w_router, w1, w3, w2):
    logits = (x @ w_router).astype(jnp.float32)
    top_v, top_i = lax.top_k(logits, TOP_K)
    gates = jax.nn.softmax(top_v, axis=-1)
    combine = jnp.sum(jax.nn.one_hot(top_i, N_EXPERTS, dtype=jnp.float32) * gates[..., None], axis=-2)
    combine = combine.astype(x.dtype)
    y = jnp.zeros_like(x)
    for e in range(N_EXPERTS):
        y = y + _swiglu(x, w1[e], w3[e], w2[e]) * combine[..., e:e + 1]
    return y

def first_inputs(seed: int = 0) -> dict:
    key = jax.random.key(seed)
    ks = iter(jax.random.split(key, 32))
    n_e = (DEPTH + 1) // 2
    n_o = DEPTH // 2

    def nrm(shape, scale):
        return jax.random.normal(next(ks), shape, jnp.float32) * scale

    return {
        "x": nrm((BATCH, SEQ, D_MODEL), 1.0),
        "ln_g": 1.0 + nrm((DEPTH, 2, D_MODEL), 0.02),
        "ln_b": nrm((DEPTH, 2, D_MODEL), 0.02),
        "rel_table": nrm((REL_BUCKETS, REL_HEADS), 0.2),
        "w_in_ab": nrm((n_e, D_MODEL, W_AB), D_MODEL ** -0.5),
        "w_gate_a": nrm((n_e, GLA_GATE_RANK, GLA_HEADS * GLA_DK), GLA_GATE_RANK ** -0.5),
        "b_gate_a": nrm((n_e, GLA_HEADS * GLA_DK), 0.1),
        "g_norm_a": 1.0 + nrm((n_e, GLA_DV), 0.02),
        "w_out_ab": nrm((n_e, MIX_AB, D_MODEL), MIX_AB ** -0.5 * BETA),
        "w_in_cd": nrm((n_o, D_MODEL, W_CD), D_MODEL ** -0.5),
        "b_forget": FORGET_BIAS_MEAN + nrm((n_o, FOX_HEADS), 0.1),
        "w_out_cd": nrm((n_o, MIX_CD, D_MODEL), MIX_CD ** -0.5 * BETA),
        "w1_dense": nrm((n_e, D_MODEL, D_FF), D_MODEL ** -0.5),
        "w3_dense": nrm((n_e, D_MODEL, D_FF), D_MODEL ** -0.5),
        "w2_dense": nrm((n_e, D_FF, D_MODEL), D_FF ** -0.5 * BETA),
        "w_router": nrm((n_o, D_MODEL, N_EXPERTS), D_MODEL ** -0.5),
        "w1_moe": nrm((n_o, N_EXPERTS, D_MODEL, D_FF_EXPERT), D_MODEL ** -0.5),
        "w3_moe": nrm((n_o, N_EXPERTS, D_MODEL, D_FF_EXPERT), D_MODEL ** -0.5),
        "w2_moe": nrm((n_o, N_EXPERTS, D_FF_EXPERT, D_MODEL), D_FF_EXPERT ** -0.5 * BETA),
    }

def first_block(x, ln_g, ln_b, rel_table, w_in_ab, w_gate_a, b_gate_a, g_norm_a, w_out_ab,
              w_in_cd, b_forget, w_out_cd, w1_dense, w3_dense, w2_dense,
              w_router, w1_moe, w3_moe, w2_moe):
    for layer in range(DEPTH):
        j = layer // 2
        if layer % 2 == 0:
            mix = _mixer_ab(x, w_in_ab[j], w_gate_a[j], b_gate_a[j], g_norm_a[j], w_out_ab[j], rel_table)
        else:
            mix = _mixer_cd(x, w_in_cd[j], b_forget[j], w_out_cd[j], rel_table)
        x = _layernorm(ALPHA * x + mix, ln_g[layer, 0], ln_b[layer, 0])
        if layer % 2 == 0:
            ffn = _swiglu(x, w1_dense[j], w3_dense[j], w2_dense[j])
        else:
            ffn = _moe(x, w_router[j], w1_moe[j], w3_moe[j], w2_moe[j])
        x = _layernorm(ALPHA * x + ffn, ln_g[layer, 1], ln_b[layer, 1])
    return x


DEPTH_2 = 1

ATTN_HEADS = 8
ATTN_WIDTH = ATTN_HEADS * HEAD_DIM
CONV_GROUPS = 8
CONV_CH = D_MODEL - ATTN_WIDTH
MIX_WIDTH = ATTN_WIDTH + CONV_CH
IN_COLS = 3 * ATTN_WIDTH + 2 * CONV_CH
CONV_KERNEL = 31
MOBA_BLOCK = 256
MOBA_TOPK = 3
Q_CHUNK = 128
NUM_BUCKETS = 32
MAX_DISTANCE = 128
D_FF_2 = -(-8 * D_MODEL // (3 * 256)) * 256
RMS_EPS = 1e-6
NEG_INF = -1e30
ATTN_SCALE = HEAD_DIM ** -0.5


def rms_norm(x, g):
    xf = x.astype(jnp.float32)
    y = xf * lax.rsqrt(jnp.mean(xf * xf, axis=-1, keepdims=True) + RMS_EPS)
    return (y * g.astype(jnp.float32)).astype(x.dtype)

def t5_bucket(dist):
    max_exact = NUM_BUCKETS // 2
    d = jnp.maximum(dist, 1).astype(jnp.float32)
    large = max_exact + (jnp.log(d / max_exact) / math.log(MAX_DISTANCE / max_exact)
                         * (NUM_BUCKETS - max_exact)).astype(jnp.int32)
    large = jnp.minimum(large, NUM_BUCKETS - 1)
    return jnp.where(dist < max_exact, dist, large)

def moba_attention(q, k, v, rel_bias):
    B, H, S, Dh = q.shape
    nb = -(-S // MOBA_BLOCK)
    s_pad = nb * MOBA_BLOCK
    n_sel = max(1, min(MOBA_TOPK, nb - 1))
    nq = S // Q_CHUNK
    pad = ((0, 0), (0, 0), (0, s_pad - S), (0, 0))
    k_blocks = jnp.pad(k, pad).reshape(B, H, nb, MOBA_BLOCK, Dh)
    v_blocks = jnp.pad(v, pad).reshape(B, H, nb, MOBA_BLOCK, Dh)

    k_mean = jnp.mean(k_blocks.astype(jnp.float32), axis=3)
    gate = jnp.einsum('bhsd,bhnd->bhsn', q.astype(jnp.float32), k_mean)
    q_block = jnp.arange(S, dtype=jnp.int32) // MOBA_BLOCK
    fully_past = jnp.arange(nb, dtype=jnp.int32)[None, :] < q_block[:, None]
    gate = jnp.where(fully_past, gate, NEG_INF)
    _, sel = lax.top_k(gate, n_sel)
    sel = sel.astype(jnp.int32)

    bias_ht = rel_bias.T.astype(jnp.float32)
    head_ix = jnp.arange(H)
    offs = jnp.arange(MOBA_BLOCK, dtype=jnp.int32)
    rank_ix = jnp.arange(n_sel, dtype=jnp.int32)

    q_c = q.reshape(B, H, nq, Q_CHUNK, Dh).transpose(0, 2, 1, 3, 4).reshape(B * nq, H, Q_CHUNK, Dh)
    sel_c = sel.reshape(B, H, nq, Q_CHUNK, n_sel).transpose(0, 2, 1, 3, 4).reshape(B * nq, H, Q_CHUNK, n_sel)
    b_ids = jnp.repeat(jnp.arange(B, dtype=jnp.int32), nq)
    c_ids = jnp.tile(jnp.arange(nq, dtype=jnp.int32), B)

    def chunk(args):
        qc, sc, b, c = args
        kb = k_blocks[b]
        vb = v_blocks[b]
        t = c * Q_CHUNK + jnp.arange(Q_CHUNK, dtype=jnp.int32)
        own = (c * Q_CHUNK) // MOBA_BLOCK
        k_sel = kb[head_ix[:, None, None], sc]
        v_sel = vb[head_ix[:, None, None], sc]
        s_sel = jnp.einsum('hqd,hqnkd->hqnk', qc, k_sel).astype(jnp.float32) * ATTN_SCALE
        dist_sel = t[None, :, None, None] - (sc[..., None] * MOBA_BLOCK + offs)
        s_sel = s_sel + bias_ht[head_ix[:, None, None, None], t5_bucket(jnp.maximum(dist_sel, 0))]
        valid = (rank_ix < own)[None, None, :, None]
        s_sel = jnp.where(valid, s_sel, NEG_INF)
        k_own = kb[:, own]
        v_own = vb[:, own]
        s_own = jnp.einsum('hqd,hkd->hqk', qc, k_own).astype(jnp.float32) * ATTN_SCALE
        dist_own = t[:, None] - (own * MOBA_BLOCK + offs)[None, :]
        s_own = s_own + bias_ht[:, t5_bucket(jnp.maximum(dist_own, 0))]
        s_own = jnp.where((dist_own >= 0)[None], s_own, NEG_INF)
        logits = jnp.concatenate([s_sel.reshape(H, Q_CHUNK, n_sel * MOBA_BLOCK), s_own], axis=-1)
        p = jax.nn.softmax(logits, axis=-1).astype(v.dtype)
        p_sel = p[..., :n_sel * MOBA_BLOCK].reshape(H, Q_CHUNK, n_sel, MOBA_BLOCK)
        p_own = p[..., n_sel * MOBA_BLOCK:]
        return (jnp.einsum('hqnk,hqnkd->hqd', p_sel, v_sel)
                + jnp.einsum('hqk,hkd->hqd', p_own, v_own))

    out = lax.map(chunk, (q_c, sel_c, b_ids, c_ids))
    return out.reshape(B, nq, H, Q_CHUNK, Dh).transpose(0, 1, 3, 2, 4).reshape(B, S, H * Dh)

def conformer_conv(a, g, w_dw, b_dw, ln_g, ln_b):
    C = a.shape[-1]
    u = a * jax.nn.sigmoid(g)
    u = lax.conv_general_dilated(u, w_dw[:, None, :], window_strides=(1,),
                                 padding=((CONV_KERNEL - 1, 0),),
                                 dimension_numbers=('NWC', 'WIO', 'NWC'),
                                 feature_group_count=C) + b_dw
    uf = u.astype(jnp.float32)
    mu = jnp.mean(uf, axis=-1, keepdims=True)
    var = jnp.mean(jnp.square(uf - mu), axis=-1, keepdims=True)
    un = (uf - mu) * lax.rsqrt(var + LN_EPS) * ln_g.astype(jnp.float32) + ln_b.astype(jnp.float32)
    return jax.nn.silu(un).astype(a.dtype)

def second_inputs(seed: int = 0) -> dict:
    key = jax.random.key(seed)
    ks = jax.random.split(key, 16)
    f32 = jnp.float32
    nrm = lambda k, shape, scale: jax.random.normal(k, shape, f32) * scale
    return {
        'x': jax.random.normal(ks[0], (BATCH, SEQ, D_MODEL), f32),
        'mix_norm_g': 1.0 + nrm(ks[1], (DEPTH_2, D_MODEL), 0.02),
        'w_in': nrm(ks[2], (DEPTH_2, D_MODEL, IN_COLS), D_MODEL ** -0.5),
        'rel_bias': nrm(ks[3], (NUM_BUCKETS, ATTN_HEADS), 0.5),
        'conv_w': nrm(ks[4], (DEPTH_2, CONV_KERNEL, CONV_CH), CONV_KERNEL ** -0.5),
        'conv_b': nrm(ks[5], (DEPTH_2, CONV_CH), 0.02),
        'conv_ln_g': 1.0 + nrm(ks[6], (DEPTH_2, CONV_CH), 0.02),
        'conv_ln_b': nrm(ks[7], (DEPTH_2, CONV_CH), 0.02),
        'w_out': nrm(ks[8], (DEPTH_2, MIX_WIDTH, D_MODEL), MIX_WIDTH ** -0.5),
        'ffn_norm_g': 1.0 + nrm(ks[9], (DEPTH_2, D_MODEL), 0.02),
        'w_gate': nrm(ks[10], (DEPTH_2, D_MODEL, D_FF_2), D_MODEL ** -0.5),
        'w_up': nrm(ks[11], (DEPTH_2, D_MODEL, D_FF_2), D_MODEL ** -0.5),
        'w_down': nrm(ks[12], (DEPTH_2, D_FF_2, D_MODEL), D_FF_2 ** -0.5),
        'final_norm_g': 1.0 + nrm(ks[13], (D_MODEL,), 0.02),
    }

def second_block(x, mix_norm_g, w_in, rel_bias, conv_w, conv_b, conv_ln_g, conv_ln_b,
              w_out, ffn_norm_g, w_gate, w_up, w_down, final_norm_g):
    B, S, _ = x.shape
    splits = [ATTN_WIDTH, 2 * ATTN_WIDTH, 3 * ATTN_WIDTH, 3 * ATTN_WIDTH + CONV_CH]

    def heads(t):
        return t.reshape(B, S, ATTN_HEADS, HEAD_DIM).transpose(0, 2, 1, 3)

    h = x
    for l in range(DEPTH_2):
        u = rms_norm(h, mix_norm_g[l])
        proj = u @ w_in[l]
        q, k, v, glu_a, glu_g = jnp.split(proj, splits, axis=-1)
        attn_out = moba_attention(heads(q), heads(k), heads(v), rel_bias)
        conv_out = conformer_conv(glu_a, glu_g, conv_w[l], conv_b[l],
                                  conv_ln_g[l], conv_ln_b[l])
        mixed = jnp.concatenate([attn_out, conv_out], axis=-1)
        h = h + mixed @ w_out[l]
        u = rms_norm(h, ffn_norm_g[l])
        h = h + (jax.nn.silu(u @ w_gate[l]) * (u @ w_up[l])) @ w_down[l]
    return rms_norm(h, final_norm_g)


def setup_inputs(seed=0):
    out = dict(first_inputs(seed))
    for name, value in second_inputs(seed + 1).items():
        if name != "x":
            out[name + "_2"] = value
    return out


def reference(
    x, ln_g, ln_b, rel_table, w_in_ab, w_gate_a, b_gate_a, g_norm_a, w_out_ab, w_in_cd,
    b_forget, w_out_cd, w1_dense, w3_dense, w2_dense, w_router, w1_moe, w3_moe, w2_moe,
    mix_norm_g_2, w_in_2, rel_bias_2, conv_w_2, conv_b_2, conv_ln_g_2, conv_ln_b_2, w_out_2,
    ffn_norm_g_2, w_gate_2, w_up_2, w_down_2, final_norm_g_2,
):
    x = first_block(
        x, ln_g, ln_b, rel_table, w_in_ab, w_gate_a, b_gate_a, g_norm_a, w_out_ab, w_in_cd,
        b_forget, w_out_cd, w1_dense, w3_dense, w2_dense, w_router, w1_moe, w3_moe, w2_moe,
    )
    return second_block(
        x, mix_norm_g_2, w_in_2, rel_bias_2, conv_w_2, conv_b_2, conv_ln_g_2, conv_ln_b_2,
        w_out_2, ffn_norm_g_2, w_gate_2, w_up_2, w_down_2, final_norm_g_2,
    )


_drawn_inputs = setup_inputs


def setup_inputs(seed=0):
    import zlib

    import numpy as np

    out = dict(_drawn_inputs(seed))
    spreads = {}
    factors = {'b_gate_a': 4.054,
     'g_norm_a': 8.0,
     'b_forget': 33.664,
     'mix_norm_g_2': 5.167,
     'conv_b_2': 9.813,
     'conv_ln_g_2': 18.81,
     'conv_ln_b_2': 19.562,
     'ffn_norm_g_2': 3.972,
     'final_norm_g_2': 7.738}
    for name, (base, spread) in spreads.items():
        noise = np.random.default_rng([zlib.crc32(name.encode()), seed]).standard_normal(out[name].shape)
        drawn = base * np.exp(spread * noise) if base else spread * noise
        out[name] = jnp.asarray(drawn.astype(out[name].dtype))
    for name, factor in factors.items():
        out[name] = (out[name] * factor).astype(out[name].dtype)
    return out
```

```python
import concourse.bass as bass
from concourse import mybir
from contextlib import ExitStack

F32 = mybir.dt.float32
I32 = mybir.dt.int32
U32 = mybir.dt.uint32
ALU = mybir.AluOpType
ACT = mybir.ActivationFunctionType
AX = mybir.AxisListType

P = 128
T = 256
TT = T // P
D = 1024
KT = D // P
H = 8
HD = 64
TOPK = 64
F_DENSE = 2816
F_MOE = 3584
FC = 256
NE = 8
UNITS = 6
UW = 2048
ALPHA = 4.0 ** 0.25
NEG = -1e30
TAKEN = -3e38
REL = 384
CONV = 31
LN_EPS = 1e-5
RMS_EPS = 1e-6
LN_AT = [32, 32, 64, 64, 80, 80, 96]
STEPS_ROUTER = 36
STEPS_CONV = 50
CONSTS = 16 * 18

AB = dict(qa=0, ka=256, va=512, ra=1024, ga=1536, qb=1552, kb=2064, vb=2576, qi=3088, ki=3600, wi=3664)
CD = dict(qc=0, kc=512, vc=1024, fc=1536, qd=1544, kd=2056, vd=2568)
B2 = dict(q=0, k=512, v=1024, a=1536, g=2048)
AB_ORDER = [AB["qi"], AB["qi"] + 256, AB["qa"], AB["ka"], AB["va"], AB["va"] + 256, AB["ra"], AB["ra"] + 256,
            AB["qb"], AB["qb"] + 256, AB["kb"], AB["kb"] + 256, AB["vb"], AB["vb"] + 256]
CD_ORDER = [CD[n] + 256 * i for n in ("qc", "kc", "vc", "qd", "kd", "vd") for i in range(2)]
B2_ORDER = [B2[n] + 256 * i for n in ("a", "g", "q", "k", "v") for i in range(2)]


def build(nc, x_in, ln_g, ln_b, rel_table, w_in_ab, w_gate_a, b_gate_a, g_norm_a, w_out_ab, w_in_cd,
          b_forget, w_out_cd, w1_dense, w3_dense, w2_dense, w_router, w1_moe, w3_moe, w2_moe,
          mix_norm_g_2, w_in_2, rel_bias_2, conv_w_2, conv_b_2, conv_ln_g_2, conv_ln_b_2, w_out_2,
          ffn_norm_g_2, w_gate_2, w_up_2, w_down_2, final_norm_g_2,
          c_ident, c_cum, c_causal, c_iota, c_onehot, c_rowadd, c_rowsel, out):
    ctx = ExitStack()
    with ctx:
        def sb(name, shape, dt=F32):
            return ctx.enter_context(nc.sbuf_tensor(name, shape, dt))

        def sem(name):
            return ctx.enter_context(nc.semaphore(name))

        ring = sb("ring", [P, UNITS, UW])
        x = sb("x", [P, TT, D])
        u = sb("u", [P, TT, D])
        xT = sb("xT", [P, KT, T])
        lnw = sb("lnw", [P, 2, 2, D])
        y = sb("y", [P, TT, D])
        ident = sb("ident", [P, P])
        cum = sb("cum", [P, TT, T])
        causal = sb("causal", [P, T])
        iota = sb("iota", [P, P])
        rowsel = sb("rowsel", [8, 8, P])
        ones = sb("ones", [P, P])
        rel = sb("rel", [32, 2, H])
        bias = sb("bias", [P, 3, H, T])
        wsm = sb("wsm", [P, KT, 160])
        wfc = sb("wfc", [P, KT, 8])
        wrt = sb("wrt", [P, KT, NE])
        wgate = sb("wgate", [16, 256])
        bgate = sb("bgate", [1, 256])
        bforget = sb("bforget", [1, 8])
        gnorm = sb("gnorm", [P, P])
        convw = sb("convw", [32, 512])
        cw = sb("cw", [P, 4, 32])
        convln = sb("convln", [P, 2, 512])
        tq = sb("tq", [P, 4, T])
        tk = sb("tk", [P, 4, T])
        nv = sb("nv", [P, TT, 512])
        ta = sb("ta", [P, 4, T])
        tb = sb("tb", [P, 4, T])
        nw = sb("nw", [P, TT, 512])
        nr = sb("nr", [P, TT, 512])
        kiT = sb("kiT", [P, T])
        gaT = sb("gaT", [16, T])
        wi = sb("wi", [P, TT, 8])
        score = sb("score", [P, TT, T])
        lg = sb("lg", [P, 2, 512])
        pr = sb("pr", [P, 2, 512])
        pT = sb("pT", [P, 2, 512])
        gnat = sb("gnat", [P, TT, T])
        gT = sb("gT", [P, 2, T])
        ngc = sb("ngc", [P, 2, 8])
        gA = sb("gA", [P, 4, 384])
        small = sb("small", [P, 256])
        rstd_t = sb("rstd", [P, 8])
        topi = sb("topi", [P, 8], U32)
        trip_i = sb("trip_i", [1, 1], I32)
        half = sb("half", [P, 8])
        table = sb("table", [P, 2 * NE + 1, 6])
        cur = sb("cur", [P, 6])
        disp = sb("disp", [P, TT, P])
        dispT = sb("dispT", [P, T])
        slotg = sb("slotg", [P, 1])
        hT = sb("hT", [P, 2, 2, T])
        hs = sb("hs", [P, 2, T])
        psum = ctx.enter_context(nc.psum_tensor("psum", [P, 8, 512], F32))
        bank = [psum[:, i, :] for i in range(8)]

        def pair_banks(i, n):
            return psum[:, 2 * (i % 2):2 * (i % 2) + 2, 0:n]

        rel_dram = nc.dram_tensor("rel_scratch", (3, P, H, REL), F32, kind="Internal").ap()

        uf = u.rearrange("p t d -> p (t d)")
        onehot = uf[0:32, 0:2 * REL].rearrange("p (a n) -> p a n", a=2)
        relrow = uf[0:8, 2 * REL:5 * REL].rearrange("p (a n) -> p a n", a=3)
        rowadd = gA.rearrange("p h n -> p (h n)")[0:1, 0:3 * REL].rearrange("p (a n) -> p a n", a=3)
        gz = pr[:, 0, :].rearrange("p (t n) -> p t n", t=2)
        ga_ = pr[:, 1, :].rearrange("p (t n) -> p t n", t=2)
        yf = y.rearrange("p t d -> p (t d)")
        gq, gk, gqo = (yf[:, 512 * i:512 * i + 512].rearrange("p (c t) -> p c t", c=2) for i in range(3))
        gko = hT.rearrange("p c f t -> p (c f t)")[:, 0:768].rearrange("p (c t) -> p c t", c=2)

        negmax = small[:, 0:4]
        rsum = small[:, 8:40]
        rinv = small[:, 240:256]
        stat = small[:, 40:64]
        mv = small[:, 64:72]
        top8 = small[:, 76:84]
        ms = small[:, 84:92]
        e2 = small[:, 92:100]
        rstd8 = rstd_t[:, 0:8]
        rstd = rstd_t[:, 0:2]
        comb = small[:, 100:116]
        chosen = small[:, 116:132]
        slot = small[:, 132:148]
        oh2 = small[:, 148:164]
        rl = small[:, 164:180]
        topf = small[:, 180:188]
        trip_f = small[:, 188:190]
        lf = small[:, 192:208]
        flz = small[:, 208:224]
        fla = small[:, 224:240]
        nfT = gnat[0:8, 0, :]

        landed = [[sem(f"unit{i}_landed_{s}") for i in range(UNITS)] for s in range(2)]
        used = [sem("units_used_0"), sem("units_used_1")]
        consts_in = sem("consts_in")
        filled = sem("fills_done")
        x_in_sem = sem("x_in")
        small_in = sem("small_in")
        ln_in = [sem("norm_weights_a"), sem("norm_weights_b")]
        rel_out = sem("rel_rows_out")
        rel_in = [sem(f"rel_bias_in_{i}") for i in range(3)]
        rel_ready = sem("rel_row_ready")
        tr_done = sem("transposed")
        tr_evac = sem("transposed_copied")
        step_done = sem("step_done")
        step_evac = sem("step_copied")
        idx_scores = sem("indexer_scores")
        idx_relu = sem("indexer_relu")
        idx_acc = sem("indexer_summed")
        mask_ready = sem("key_mask_ready")
        ls_a = sem("log_sigmoid_parts")
        ls_b = sem("log_sigmoid_ready")
        gla_neg = sem("gla_negated")
        gla_exp = sem("gla_exponentials")
        gla_ops = sem("gla_operands")
        gla_A = sem("gla_products")
        gla_Am = sem("gla_products_masked")
        gla_o = sem("gla_out")
        gla_sq = sem("gla_squares")
        gla_done = sem("gla_normed")
        a_scores = sem("scores_ready")
        a_max = sem("max_ready")
        a_exp = sem("probs_ready")
        a_tr = sem("probs_transposed")
        a_pT = sem("probs_copied")
        a_pv = sem("probs_used")
        a_done = sem("heads_normed")
        mix_done = sem("mixer_out_ready")
        sums_done = sem("sums_ready")
        sums_evac = sem("sums_copied")
        x_ready = sem("norm_ready")
        rs_ask = sem("variance_ready")
        rs_got = sem("rstd_ready")
        up_done = [sem("hidden_ready_0"), sem("hidden_ready_1")]
        silu_done = [sem("silu_ready_0"), sem("silu_ready_1")]
        h_ready = [sem("gated_ready_0"), sem("gated_ready_1")]
        down_done = [sem("down_done_0"), sem("down_done_1")]
        route_ready = sem("routes_ready")
        trip_ready = sem("trip_ready")
        cur_ready = sem("expert_columns_ready")
        disp_ready = sem("dispatch_ready")
        xe_done = sem("gathered")
        xe_ready = sem("gathered_copied")
        ye_ready = sem("expert_out_scaled")
        sc_done = sem("scattered")
        sc_added = sem("scattered_added")
        pt_done = sem("dispatch_transposed")
        pt_ready = sem("dispatch_copied")
        moe_done = sem("moe_done")
        rms_sq = sem("squares_ready")
        x2_ready = sem("residual_ready")
        gate_ask = sem("gate_logits_ready")
        gate_got = sem("gate_exps_ready")
        conv_in = sem("conv_in_ready")
        conv_done = sem("conv_done")
        conv_n = sem("conv_normed")
        conv_out = sem("conv_out")
        fin = sem("final_ready")
        stored = sem("stored")
        v_chain = sem("vector_chain")
        a_chain = sem("scalar_chain")
        g_chain = sem("pool_chain")

        def by_rows(w):
            return w.rearrange("(k p) n -> p k n", p=P)

        win = [by_rows(w_in_ab[0]), by_rows(w_in_cd[0]), by_rows(w_in_2[0])]
        wout = [by_rows(w_out_ab[0]), by_rows(w_out_cd[0]), by_rows(w_out_2[0])]

        def as_cols(i):
            return ring[:, i, :].rearrange("p (k n) -> p k n", k=KT)

        def as_rows(i):
            return ring[:, i, :].rearrange("p (k n) -> p k n", k=2)

        class Place:
            def __init__(self):
                self.s, self.n = 0, 0

            def second(self):
                self.s, self.n = 1, 0

            def unit(self):
                return self.n % UNITS

            def landed_at(self, rounds=0):
                return 16 * (self.n // UNITS + 1) + rounds * 16

        block = ctx.enter_context(nc.Block())

        @block.sync
        def _(sp):
            at = Place()

            def load(dst_of, src, shift=0, free=True):
                i = at.unit()
                if at.n >= UNITS:
                    sp.wait_ge(used[at.s], at.n - UNITS + 1 + shift)
                sp.dma_start(dst_of(i), src).then_inc(landed[at.s][i], 16)
                at.n += 1

            def ffn(w1, w3, w2):
                w1, w3, w2 = by_rows(w1), by_rows(w3), by_rows(w2)

                def up(c):
                    load(as_cols, w1[:, :, bass.ds(c * FC, FC)], shift)
                    load(as_cols, w3[:, :, bass.ds(c * FC, FC)], shift)

                def down(c):
                    load(as_rows, w2[:, bass.ds(c * 2, 2), :], shift)

                shift = 0
                up(0)
                up(1)
                down(0)
                with sp.Fori(0, 4) as r:
                    shift = r * 6
                    up(r * 2 + 2)
                    down(r * 2 + 1)
                    up(r * 2 + 3)
                    down(r * 2 + 2)
                at.n += 18
                shift = 0
                up(10)
                down(9)
                down(10)

            sp.dma_start(x[:, :, :], x_in[0].rearrange("(a p) d -> p a d", p=P)).then_inc(x_in_sem, 16)
            sp.dma_start(ident[:, :], c_ident).then_inc(x_in_sem, 16)
            sp.dma_start(wsm[:, :, 0:16], win[0][:, :, AB["ga"]:AB["ga"] + 16]).then_inc(small_in, 16)
            sp.dma_start(wsm[:, :, 16:80], win[0][:, :, AB["ki"]:AB["ki"] + 64]).then_inc(small_in, 16)
            sp.dma_start(wsm[:, :, 80:144], win[0][:, :, AB["ki"]:AB["ki"] + 64]).then_inc(small_in, 16)
            sp.dma_start(wsm[:, :, 144:152], win[0][:, :, AB["wi"]:AB["wi"] + 8]).then_inc(small_in, 16)
            for col in AB_ORDER:
                load(as_cols, win[0][:, :, col:col + 256])
            for j in range(4):
                load(as_rows, wout[0][:, 2 * j:2 * j + 2, :])
            ffn(w1_dense[0], w3_dense[0], w2_dense[0])
            for col in CD_ORDER:
                load(as_cols, win[1][:, :, col:col + 256])
            for j in range(4):
                load(as_rows, wout[1][:, 2 * j:2 * j + 2, :])

            m1 = w1_moe[0].rearrange("e (k p) n -> e p k n", p=P)
            m3 = w3_moe[0].rearrange("e (k p) n -> e p k n", p=P)
            m2 = w2_moe[0].rearrange("e (k p) n -> e p k n", p=P)

            def expert(e, shift):
                for c in range(F_MOE // FC + 1):
                    if c < F_MOE // FC:
                        load(as_cols, m1[bass.ds(e, 1), :, :, c * FC:(c + 1) * FC].rearrange("a p k n -> p (a k) n"), shift)
                        load(as_cols, m3[bass.ds(e, 1), :, :, c * FC:(c + 1) * FC].rearrange("a p k n -> p (a k) n"), shift)
                    if c > 0:
                        load(as_rows, m2[bass.ds(e, 1), :, 2 * c - 2:2 * c, :].rearrange("a p k n -> p (a k) n"), shift)

            start = at.n
            with sp.Fori(0, NE) as e:
                expert(e, e * 42)
            at.n = start
            sp.wait_ge(trip_ready, 1)
            trips = sp.value_load(trip_i[0:1, 0:1], min_val=NE, max_val=2 * NE)
            with sp.If(trips > NE):
                with sp.Fori(0, NE) as e:
                    expert(e, e * 42 + NE * 42)
            sp.wait_ge(moe_done, 1)
            at.second()
            for col in B2_ORDER:
                load(as_cols, win[2][:, :, col:col + 256])
            for j in range(4):
                load(as_rows, wout[2][:, 2 * j:2 * j + 2, :])
            ffn(w_gate_2[0], w_up_2[0], w_down_2[0])
            sp.wait_ge(fin, 2)
            sp.dma_start(out[0].rearrange("(a p) d -> p a d", p=P), u[:, :, :]).then_inc(stored, 16)
            sp.wait_ge(stored, 16)

        @block.tensor
        def _(pe):
            at = Place()
            steps = [0]
            trs = [0]
            sums = [0]

            def arrived(rounds=0):
                pe.wait_ge(landed[at.s][at.unit()], at.landed_at(rounds))
                return at.unit()

            freed = [0]

            def release(ins=None):
                if ins is None:
                    freed[0] += 1
                else:
                    ins.then_inc(used[at.s], 1)
                at.n += 1

            def first_of(ins):
                if freed[0]:
                    ins.then_inc(used[at.s], freed[0])
                    freed[0] = 0

            def step_bank():
                j = steps[0]
                steps[0] += 1
                if j >= 2:
                    pe.wait_ge(step_evac, j - 1)
                return bank[6 + j % 2]

            def proj_transposed():
                ps = step_bank()
                w = as_cols(arrived())
                for c in range(2):
                    for k in range(KT):
                        last = pe.matmul(ps[:, c * T:(c + 1) * T], w[:, k, c * P:(c + 1) * P], xT[:, k, :],
                                         start=(k == 0), stop=(k == KT - 1))
                        first_of(last)
                last.then_inc(step_done, 1)
                release()

            def proj_natural():
                ps = step_bank()
                w = as_cols(arrived())
                for t in range(TT):
                    for k in range(KT):
                        last = pe.matmul(ps[:, t * 256:(t + 1) * 256], xT[:, k, t * P:(t + 1) * P], w[:, k, :],
                                         start=(k == 0), stop=(k == KT - 1))
                        first_of(last)
                last.then_inc(step_done, 1)
                release()

            def narrow(w, added=None):
                ps = step_bank()
                for t in range(TT):
                    o = ps[:, t * 8:(t + 1) * 8]
                    for k in range(KT):
                        last = pe.matmul(o, xT[:, k, t * P:(t + 1) * P], w(k),
                                         start=(k == 0), stop=(k == KT - 1 and added is None))
                    if added is not None:
                        last = pe.matmul(o, ones[0:1, :], added, start=False, stop=True)
                last.then_inc(step_done, 1)

            def transposes(src):
                for g in range(4):
                    for k in (2 * g, 2 * g + 1):
                        for t in range(TT):
                            last = pe.transpose(bank[g][:, (k % 2) * T + t * P:(k % 2) * T + (t + 1) * P],
                                                src[:, t, k * P:(k + 1) * P], ident[:, :])
                            first_of(last)
                    last.then_inc(tr_done, 1)
                trs[0] += 4
                pe.wait_ge(tr_evac, trs[0])

            def attention(a, q, k, v, masked=False, forget=False):
                def scores(g):
                    i = g - 8 * a
                    t, hp, n = i // 4, i % 4, P * (i // 4 + 1)
                    if g >= 2:
                        pe.wait_ge(a_max, g - 1)
                    for hh in range(2):
                        rows = slice(HD * hh, HD * hh + HD)
                        o = bank[2 * (g % 2) + hh][:, 0:n]
                        more = masked or forget
                        last = pe.matmul(o, q[rows, hp, t * P:(t + 1) * P], k[rows, hp, 0:n],
                                         start=True, stop=not more)
                        if masked:
                            last = pe.matmul(o, ident[:, :], score[:, t, 0:n], start=False, stop=True)
                        if forget:
                            last = pe.matmul(o, rowsel[:, 2 * hp + hh, :], nfT[:, 0:n], start=False, stop=True)
                    last.then_inc(a_scores, 1)

                def turn(g):
                    t = (g - 8 * a) // 4
                    pe.wait_ge(a_exp, g + 1)
                    if g >= 2:
                        pe.wait_ge(a_pT, g - 1)
                    for hh in range(2):
                        for s in range(t + 1):
                            last = pe.transpose(bank[6 + g % 2][:, (2 * hh + s) * P:(2 * hh + s + 1) * P],
                                                pr[:, g % 2, hh * T + s * P:hh * T + (s + 1) * P], ident[:, :])
                    last.then_inc(a_tr, 1)

                def values(g):
                    i = g - 8 * a
                    t, hp = i // 4, i % 4
                    pe.wait_ge(a_pT, g + 1)
                    if hp == 0 and a > 0:
                        pe.wait_ge(a_done, 2 * (a - 1) + t + 1)
                    for hh in range(2):
                        h = 2 * hp + hh
                        for s in range(t + 1):
                            last = pe.matmul(bank[4 + t][:, h * HD:(h + 1) * HD],
                                             pT[:, g % 2, (2 * hh + s) * P:(2 * hh + s + 1) * P],
                                             v[:, s, h * HD:(h + 1) * HD], start=(s == 0), stop=(s == t))
                    last.then_inc(a_pv, 1)

                for g in range(8 * a, 8 * a + 10):
                    if g < 8 * a + 8:
                        scores(g)
                    if 8 * a < g <= 8 * a + 8:
                        turn(g - 1)
                    if g >= 8 * a + 2:
                        values(g - 2)

            def out_projection():
                pe.wait_ge(step_evac, steps[0])
                for j in range(4):
                    w = as_rows(arrived())
                    for kk in range(2):
                        for t in range(TT):
                            for n in range(2):
                                k = 2 * j + kk
                                last = pe.matmul(bank[4 + 2 * t + n][:, :], xT[:, k, t * P:(t + 1) * P],
                                                 w[:, kk, n * 512:(n + 1) * 512], start=(k == 0), stop=(k == KT - 1))
                                first_of(last)
                    if j == 3:
                        last.then_inc(sums_done, 1)
                    release()
                sums[0] += 1

            def up(s, ft, n, shift=0, rounds=0):
                w1, w3 = as_cols(arrived(rounds)), None
                for f in range(2):
                    ps = bank[(ft + f) % 4]
                    if ft + f >= 4:
                        pe.wait_ge(h_ready[s], ft + f - 3 + shift)
                    for k in range(KT):
                        last = pe.matmul(ps[:, 0:n], w1[:, k, f * P:(f + 1) * P], xT[:, k, 0:n],
                                         start=(k == 0), stop=(k == KT - 1))
                        first_of(last)
                    if f == 1:
                        last.then_inc(used[at.s], 1)
                    if f == 0:
                        at.n += 1
                        w3 = as_cols(arrived(rounds))
                    for k in range(KT):
                        last = pe.matmul(ps[:, T:T + n], w3[:, k, f * P:(f + 1) * P], xT[:, k, 0:n],
                                         start=(k == 0), stop=(k == KT - 1))
                    last.then_inc(up_done[s], 1)
                release()

            def down(s, c, tiles, first, final, shift=0, rounds=0):
                w = as_rows(arrived(rounds))
                pe.wait_ge(h_ready[s], 2 * c + 2 + shift)
                for f in range(2):
                    for t in range(tiles):
                        for n in range(2):
                            last = pe.matmul(bank[4 + 2 * t + n][:, :], hT[:, c % 2, f, t * P:(t + 1) * P],
                                             w[:, f, n * 512:(n + 1) * 512],
                                             start=first and f == 0, stop=final and f == 1)
                            first_of(last)
                last.then_inc(down_done[s], 1)
                release()

            def ffn(s):
                pe.wait_ge(sums_evac, sums[0])
                up(s, 0, T)
                up(s, 2, T)
                down(s, 0, TT, True, False)
                with pe.Fori(0, 4) as r:
                    up(s, 4, T, r * 4, r)
                    down(s, 1, TT, False, False, r * 4, r)
                    up(s, 6, T, r * 4, r)
                    down(s, 2, TT, False, False, r * 4, r)
                at.n += 18
                up(s, 20, T)
                down(s, 9, TT, False, False)
                down(s, 10, TT, False, True)
                sums[0] += 1

            pe.wait_ge(x_in_sem, 32)
            pe.wait_ge(filled, 3)
            transposes(x)
            pe.wait_ge(small_in, 64)
            ps = step_bank()
            for k in range(KT):
                pe.matmul(ps[0:16, 0:T], wsm[:, k, 0:16], xT[:, k, :], start=(k == 0), stop=(k == KT - 1))
            for k in range(KT):
                last = pe.matmul(ps[:, T:2 * T], wsm[:, k, 16:144], xT[:, k, :], start=(k == 0), stop=(k == KT - 1))
            last.then_inc(step_done, 1)
            narrow(lambda k: wsm[:, k, 144:152])
            proj_transposed()
            proj_transposed()
            pe.wait_ge(consts_in, CONSTS)
            pe.wait_ge(step_evac, 1)
            ps = step_bank()
            for t in range(TT):
                pe.matmul(ps[:, t * T:(t + 1) * T], gaT[:, t * P:(t + 1) * P], wgate[:, :], start=True, stop=False)
                last = pe.matmul(ps[:, t * T:(t + 1) * T], ones[0:1, :], bgate[:, :], start=False, stop=True)
            last.then_inc(step_done, 1)
            for i, w in enumerate((0, 0, 1)):
                ps = step_bank()
                pe.matmul(ps[0:8, 0:REL], rel[:, w, :], onehot[:, w, :], start=True, stop=False)
                pe.matmul(ps[0:8, 0:REL], ones[0:1, 0:8], rowadd[:, i, :], start=False, stop=True).then_inc(step_done, 1)
            for i in range(8):
                t, hp, n = i // 4, i % 4, P * (i // 4 + 1)
                if i == 0:
                    pe.wait_ge(step_evac, 4)
                if i >= 2:
                    pe.wait_ge(idx_relu, i - 1)
                for hh in range(2):
                    rows = slice(HD * hh, HD * hh + HD)
                    last = pe.matmul(bank[2 * (i % 2) + hh][:, 0:n], ta[rows, hp, t * P:(t + 1) * P],
                                     kiT[rows, 0:n], start=True, stop=True)
                last.then_inc(idx_scores, 1)
            proj_transposed()
            proj_transposed()
            pe.wait_ge(ls_b, 1)
            ps = step_bank()
            for c in range(2):
                for t in range(TT):
                    last = pe.matmul(ps[:, c * T:(c + 1) * T], gnat[:, t, c * P:(c + 1) * P], cum[:, t, :],
                                     start=(t == 0), stop=(t == 1))
            last.then_inc(step_done, 1)
            for _ in range(4):
                proj_natural()
            pe.wait_ge(idx_relu, 8)
            pe.wait_ge(gla_ops, 1)
            for h in range(4):
                r, c = slice(HD * (h % 2), HD * (h % 2) + HD), h // 2
                b_ = bank[h]
                for o, m, kk, qq in (
                    (b_[0:P, 0:64], P, gk[r, c, 0:P], gq[r, c, 0:64]),
                    (b_[64:P, 64:P], 64, gk[r, c, 64:P], gq[r, c, 64:P]),
                    (b_[0:64, 64:P], 64, gko[r, c, 0:64], gqo[r, c, 64:P]),
                    (b_[0:P, P:192], P, gko[r, c, 64:192], gqo[r, c, P:192]),
                    (b_[0:P, 192:T], P, gko[r, c, 192:320], gqo[r, c, 192:T]),
                    (b_[0:P, T:T + 64], P, gk[r, c, P:T], gq[r, c, P:192]),
                    (b_[64:P, T + 64:384], 64, gk[r, c, 192:T], gq[r, c, 192:T]),
                    (b_[0:64, T + 64:384], 64, gko[r, c, 320:384], gqo[r, c, 192:T]),
                ):
                    last = pe.matmul(o, kk, qq, start=True, stop=True)
                last.then_inc(gla_A, 1)
            proj_transposed()
            pe.wait_ge(gla_Am, 4)
            pe.wait_ge(step_evac, 13)
            for h in range(4):
                v_ = slice(h * P, (h + 1) * P)
                pe.matmul(bank[4][:, v_], gA[:, h, 0:P], nw[:, 0, v_], start=True, stop=True)
                pe.matmul(bank[5][:, v_], gA[:, h, P:T], nw[:, 0, v_], start=True, stop=False)
                last = pe.matmul(bank[5][:, v_], gA[:, h, T:384], nw[:, 1, v_], start=False, stop=True)
            last.then_inc(gla_o, 1)
            for _ in range(3):
                proj_transposed()
            for _ in range(2):
                proj_natural()
            pe.wait_ge(step_evac, steps[0])
            pe.wait_ge(mask_ready, 1)
            pe.wait_ge(gla_done, 1)
            attention(0, tq, tk, nv, masked=True)
            pe.wait_ge(a_done, 2)
            transposes(u)
            out_projection()
            pe.wait_ge(x_ready, 1)
            transposes(x)
            ffn(0)

            pe.wait_ge(x_ready, 2)
            transposes(x)
            narrow(lambda k: wfc[:, k, :], bforget[:, :])
            for _ in range(4):
                proj_transposed()
            for _ in range(2):
                proj_natural()
            pe.wait_ge(ls_b, 2)
            ps = step_bank()
            for t in range(TT):
                last = pe.matmul(ps[0:8, 0:T], lf[:, t * 8:(t + 1) * 8], cum[:, t, :], start=(t == 0), stop=(t == 1))
            last.then_inc(step_done, 1)
            for _ in range(4):
                proj_transposed()
            for _ in range(2):
                proj_natural()
            pe.wait_ge(step_evac, steps[0])
            attention(1, tq, tk, nv, forget=True)
            attention(2, ta, tb, nw)
            pe.wait_ge(a_done, 6)
            transposes(u)
            out_projection()

            pe.wait_ge(x_ready, 3)
            transposes(x)
            pe.wait_ge(sums_evac, sums[0])
            narrow(lambda k: wrt[:, k, :])
            pe.wait_ge(route_ready, 1)
            ps = step_bank()
            pe.matmul(ps[:, 0:8], cum[:, 0, 0:P], chosen[:, 0:8], start=True, stop=True)
            pe.matmul(ps[:, 8:16], cum[:, 0, P:T], chosen[:, 0:8], start=True, stop=False)
            pe.matmul(ps[:, 8:16], cum[:, 1, P:T], chosen[:, 8:16], start=False, stop=True)
            pe.matmul(ps[0:1, 16:24], ones[:, 0:1], chosen[:, 0:8], start=True, stop=False)
            pe.matmul(ps[0:1, 16:24], ones[:, 0:1], chosen[:, 8:16], start=False, stop=True).then_inc(step_done, 1)

            def gather(n):
                pe.wait_ge(disp_ready, n)
                for k in range(KT):
                    for t in range(TT):
                        last = pe.matmul(bank[6 + k // 4][:, (k % 4) * P:(k % 4 + 1) * P], x[:, t, k * P:(k + 1) * P],
                                         disp[:, t, :], start=(t == 0), stop=(t == 1))
                        first_of(last)
                    if k % 4 == 3:
                        last.then_inc(xe_done, 1)

            def turn_dispatch(n):
                pe.wait_ge(xe_ready, n * 2)
                for t in range(TT):
                    pe.transpose(bank[6][:, t * P:(t + 1) * P], disp[:, t, :], ident[:, :])
                for t in range(TT):
                    last = pe.matmul(bank[7][:, 0:1], disp[:, t, :], cur[:, 4 + t:5 + t], start=(t == 0), stop=(t == 1))
                last.then_inc(pt_done, 1)

            pe.wait_ge(step_evac, steps[0])
            gather(1)
            turn_dispatch(1)
            pe.wait_ge(trip_ready, 1)
            trips = pe.value_load(trip_i[0:1, 0:1], min_val=NE, max_val=2 * NE)
            start = at.n
            FT0, C0, NCH = 2 * (F_DENSE // FC), F_DENSE // FC, F_MOE // FC
            with pe.Fori(0, trips) as e:
                at.n = start
                for c in range(NCH + 1):
                    if c < NCH:
                        if c == 0:
                            pe.wait_ge(xe_ready, e * 2 + 2)
                        up(0, FT0 + 2 * c, P, e * (2 * NCH), e * 7)
                    if c > 0:
                        down(0, C0 + c - 1, 1, c == 1, c == NCH, e * (2 * NCH), e * 7)
                pe.wait_ge(pt_ready, e + 1)
                gather(e + 2)
                pe.wait_ge(ye_ready, e + 1)
                for t in range(TT):
                    for n in range(2):
                        pe.matmul(bank[2 * t + n][:, :], dispT[:, t * P:(t + 1) * P], y[:, 0, n * 512:(n + 1) * 512],
                                  start=True, stop=True).then_inc(sc_done, 1)
                turn_dispatch(e + 2)
                pe.wait_ge(sc_added, e * 4 + 4)
            pe.wait_ge(pt_ready, trips + 1)
            pe.nop().then_inc(moe_done, 1)
            at.second()

            pe.wait_ge(x_ready, 5)
            transposes(u)
            for i in range(4):
                if i == 0:
                    ps = step_bank()
                last = pe.transpose(ps[:, i * 32:(i + 1) * 32], convw[:, i * P:(i + 1) * P], ident[0:32, 0:32])
            last.then_inc(step_done, 1)
            for _ in range(8):
                proj_transposed()
            for _ in range(2):
                proj_natural()
            pe.wait_ge(step_evac, steps[0])
            attention(3, tq, tk, nv)
            pe.wait_ge(conv_done, 1)
            for t in range(TT):
                ps = step_bank()
                for c in range(4):
                    last = pe.transpose(ps[:, c * P:(c + 1) * P], ta[:, c, t * P:(t + 1) * P], ident[:, :])
                last.then_inc(step_done, 1)
            pe.wait_ge(a_done, 8)
            pe.wait_ge(conv_out, 2)
            transposes(u)
            out_projection()
            pe.wait_ge(x_ready, 6)
            transposes(u)
            ffn(1)

        @block.scalar
        def _(act):
            steps = [0]
            trs = [0]
            chain = [0]

            def link(ins):
                chain[0] += 1
                ins.then_inc(a_chain, 1)
                act.wait_ge(a_chain, chain[0])

            def load(dst, src):
                act.dma_start(dst, src).then_inc(consts_in, 16)

            def copy_transposed():
                for g in range(4):
                    trs[0] += 1
                    act.wait_ge(tr_done, trs[0])
                    act.activation(xT[:, 2 * g:2 * g + 2, :], bank[g].rearrange("p (k t) -> p k t", k=2),
                                   ACT.Copy).then_inc(tr_evac, 1)

            def step_out():
                j = steps[0]
                steps[0] += 1
                act.wait_ge(step_done, j + 1)
                return bank[6 + j % 2]

            def copy_step(dst, func=ACT.Copy, scale=1.0):
                act.activation(dst, step_out().rearrange("p (k t) -> p k t", k=2), func,
                               scale=scale).then_inc(step_evac, 1)

            def log_sigmoid_parts(ps, z, a):
                link(act.activation(z, ps, ACT.Copy))
                act.activation(a, z, ACT.Abs).then_inc(step_evac, 1)
                act.wait_ge(step_evac, steps[0])
                link(act.activation(a, a, ACT.Exp, scale=-1.0))
                act.activation(a, a, ACT.Ln, bias=1.0).then_inc(ls_a, 1)

            def attention(a):
                def exps(g):
                    t, hp, n = (g - 8 * a) // 4, (g - 8 * a) % 4, P * ((g - 8 * a) // 4 + 1)
                    act.wait_ge(a_max, g + 1)
                    if g >= 2:
                        act.wait_ge(a_tr, g - 1)
                    for hh in range(2):
                        col = (a % 2) * 16 + t * 8 + 2 * hp + hh
                        last = act.activation(pr[:, g % 2, hh * T:hh * T + n], lg[:, g % 2, hh * T:hh * T + n],
                                              ACT.Exp, bias=negmax[:, 2 * (g % 2) + hh:2 * (g % 2) + hh + 1],
                                              accum_out=rsum[:, col:col + 1])
                    last.then_inc(a_exp, 1)

                def copy(g):
                    t = (g - 8 * a) // 4
                    act.wait_ge(a_tr, g + 1)
                    if g >= 2:
                        act.wait_ge(a_pv, g - 1)
                    dst = pT[:, g % 2, :].rearrange("p (h s t) -> p h s t", h=2, s=2)[:, :, 0:t + 1, :]
                    src = bank[6 + g % 2].rearrange("p (h s t) -> p h s t", h=2, s=2)[:, :, 0:t + 1, :]
                    act.activation(dst, src, ACT.Copy).then_inc(a_pT, 1)

                if a >= 2:
                    act.wait_ge(a_done, 2 * (a - 1))
                for g in range(8 * a, 8 * a + 9):
                    if g < 8 * a + 8:
                        exps(g)
                    if g > 8 * a:
                        copy(g - 1)

            def silus(s, ft, shift=0, n=T):
                for f in range(2):
                    act.wait_ge(up_done[s], ft + f + 1 + shift)
                    if ft + f >= 2:
                        act.wait_ge(h_ready[s], ft + f - 1 + shift)
                    act.activation(hs[:, (ft + f) % 2, 0:n], bank[(ft + f) % 4][:, 0:n], ACT.Silu)\
                       .then_inc(silu_done[s], 1)

            def ffn(s):
                silus(s, 0)
                silus(s, 2)
                with act.Fori(0, 4) as r:
                    silus(s, 4, r * 4)
                    silus(s, 6, r * 4)
                silus(s, 20)

            load(cum[:, :, :], c_cum)
            load(causal[:, :], c_causal)
            load(iota[:, :], c_iota)
            load(onehot[:, :, :], c_onehot)
            load(rowadd[:, :, :], c_rowadd)
            load(rowsel[:, :, :], c_rowsel)
            load(rel[:, 0, :], rel_table)
            load(rel[:, 1, :], rel_bias_2)
            load(wgate[:, :], w_gate_a[0])
            load(bgate[:, :], b_gate_a)
            load(bforget[:, :], b_forget)
            load(gnorm[:, :], g_norm_a.broadcast_to([P, P]))
            load(wfc[:, :, :], win[1][:, :, CD["fc"]:CD["fc"] + 8])
            load(wrt[:, :, :], by_rows(w_router[0]))
            load(convw[0:31, :], conv_w_2[0])
            load(convw[31:32, :], conv_b_2)
            load(convln[:, 0, :], conv_ln_g_2.broadcast_to([P, 512]))
            load(convln[:, 1, :], conv_ln_b_2.broadcast_to([P, 512]))

            copy_transposed()
            ps = step_out()
            act.activation(gaT[:, :], ps[0:16, 0:T], ACT.Copy)
            act.activation(kiT[:, :], ps[:, T:2 * T], ACT.Copy).then_inc(step_evac, 1)
            act.activation(wi[:, :, :], step_out()[:, 0:16].rearrange("p (t n) -> p t n", t=2), ACT.Copy)\
               .then_inc(step_evac, 1)
            copy_step(ta[:, 0:2, :])
            copy_step(ta[:, 2:4, :])
            log_sigmoid_parts(step_out().rearrange("p (t n) -> p t n", t=2), gz[:, :, :], ga_[:, :, :])
            for i in range(3):
                act.activation(relrow[:, i, :], step_out()[0:8, 0:REL], ACT.Copy).then_inc(step_evac, 1)
            for i in range(8):
                t, n = i // 4, P * (i // 4 + 1)
                act.wait_ge(idx_scores, i + 1)
                if i >= 2:
                    act.wait_ge(idx_acc, i - 1)
                act.activation(lg[:, i % 2, :].rearrange("p (h s) -> p h s", h=2)[:, :, 0:n],
                               pair_banks(i, n), ACT.Relu)\
                   .then_inc(idx_relu, 1)
            copy_step(tb[:, 0:2, :], scale=HD ** -0.5)
            copy_step(tb[:, 2:4, :])
            copy_step(gT[:, :, :], scale=1.0 / 16.0)
            act.wait_ge(step_evac, steps[0])
            act.wait_ge(gla_neg, 1)
            for c in range(2):
                for j in range(4):
                    s_ = slice(64 * j, 64 * j + 64)
                    mid = 64 * j + 31
                    act.activation(gq[:, c, s_], gT[:, c, s_], ACT.Exp, bias=ngc[:, c, j:j + 1])
                    last = act.activation(gk[:, c, s_], gT[:, c, s_], ACT.Exp, bias=gT[:, c, mid:mid + 1], scale=-1.0)
                    if j > 0:
                        b_ = 64 * j - 1
                        act.activation(gqo[:, c, s_], gT[:, c, s_], ACT.Exp, bias=ngc[:, c, 3 + j:4 + j])
                        o = 64 * (j * (j - 1) // 2)
                        last = act.activation(gko[:, c, o:o + 64 * j], gT[:, c, 0:64 * j], ACT.Exp,
                                              bias=gT[:, c, b_:b_ + 1], scale=-1.0)
                last.then_inc(gla_exp, 1)
                copy_step(nw[:, :, c * 256:(c + 1) * 256])
            for c in range(2):
                copy_step(nr[:, :, c * 256:(c + 1) * 256], ACT.Silu)
            copy_step(tq[:, 0:2, :], scale=HD ** -0.5)
            act.wait_ge(gla_o, 1)
            for t in range(TT):
                act.activation(y[:, t, 0:512], bank[4 + t][:, :], ACT.Square).then_inc(gla_sq, 1)
            copy_step(tq[:, 2:4, :], scale=HD ** -0.5)
            copy_step(tk[:, 0:2, :])
            copy_step(tk[:, 2:4, :])
            copy_step(nv[:, :, 0:256])
            copy_step(nv[:, :, 256:512])
            attention(0)
            copy_transposed()
            copy_transposed()
            ffn(0)

            copy_transposed()
            log_sigmoid_parts(step_out()[:, 0:16], flz, fla)
            for q, k, v in ((tq, tk, nv), (ta, tb, nw)):
                copy_step(q[:, 0:2, :], scale=HD ** -0.5)
                copy_step(q[:, 2:4, :], scale=HD ** -0.5)
                copy_step(k[:, 0:2, :])
                copy_step(k[:, 2:4, :])
                copy_step(v[:, :, 0:256])
                copy_step(v[:, :, 256:512])
                if q is tq:
                    act.activation(nfT, step_out()[0:8, 0:T], ACT.Copy, scale=-1.0).then_inc(step_evac, 1)
            attention(1)
            attention(2)
            copy_transposed()
            copy_transposed()
            act.activation(rl, step_out()[:, 0:16], ACT.Copy).then_inc(step_evac, 1)
            act.wait_ge(gate_ask, 1)
            act.activation(e2[:, 2:4], e2[:, 0:2], ACT.Exp).then_inc(gate_got, 1)
            ps = step_out()
            link(act.activation(slot, ps[:, 0:16], ACT.Copy))
            act.activation(oh2[0:1, 0:8], ps[0:1, 16:24], ACT.Copy).then_inc(step_evac, 1)

            def gathered(n):
                for i in range(2):
                    act.wait_ge(xe_done, n * 2 + (i - 1))
                    act.activation(xT[:, 4 * i:4 * i + 4, 0:P], bank[6 + i].rearrange("p (k t) -> p k t", k=4),
                                   ACT.Copy).then_inc(xe_ready, 1)

            def turned(n):
                act.wait_ge(pt_done, n)
                act.activation(dispT[:, :], bank[6][:, 0:T], ACT.Copy)
                act.activation(slotg[:, :], bank[7][:, 0:1], ACT.Copy).then_inc(pt_ready, 1)

            gathered(1)
            turned(1)
            act.wait_ge(trip_ready, 1)
            trips = act.value_load(trip_i[0:1, 0:1], min_val=NE, max_val=2 * NE)
            FT0, NCH = 2 * (F_DENSE // FC), F_MOE // FC
            with act.Fori(0, trips) as e:
                for c in range(NCH):
                    silus(0, FT0 + 2 * c, e * (2 * NCH), P)
                gathered(e + 2)
                turned(e + 2)

            def squares(sem_, value):
                act.wait_ge(sem_, value)
                for t in range(TT):
                    act.activation(y[:, t, :], x[:, t, :], ACT.Square, accum_out=ms[:, t:t + 1]).then_inc(rms_sq, 1)

            squares(x_ready, 4)
            copy_transposed()
            act.activation(cw[:, :, :], step_out()[:, 0:P].rearrange("p (c j) -> p c j", c=4), ACT.Copy)\
               .then_inc(step_evac, 1)
            copy_step(ta[:, 0:2, :])
            copy_step(ta[:, 2:4, :])
            copy_step(tb[:, 0:2, :], ACT.Sigmoid)
            copy_step(tb[:, 2:4, :], ACT.Sigmoid)
            act.wait_ge(step_evac, steps[0])
            act.nop().then_inc(conv_in, 1)
            copy_step(tq[:, 0:2, :], scale=HD ** -0.5)
            copy_step(tq[:, 2:4, :], scale=HD ** -0.5)
            copy_step(tk[:, 0:2, :])
            copy_step(tk[:, 2:4, :])
            copy_step(nv[:, :, 0:256])
            copy_step(nv[:, :, 256:512])
            attention(3)
            for t in range(TT):
                act.activation(nr[:, t, :], step_out()[:, :], ACT.Copy).then_inc(step_evac, 1)
            for t in range(TT):
                act.wait_ge(conv_n, t + 1)
                act.activation(u[:, t, 512:1024], nr[:, t, :], ACT.Silu).then_inc(conv_out, 1)
            copy_transposed()
            squares(x2_ready, 1)
            copy_transposed()
            ffn(1)
            squares(x2_ready, 2)

        @block.vector
        def _(dve):
            chain = [0]
            norms = [0]

            def link(ins):
                chain[0] += 1
                ins.then_inc(v_chain, 1)
                dve.wait_ge(v_chain, chain[0])

            norms_asked = [0]

            def ask(ins):
                ins.then_inc(rs_ask, 1)
                norms_asked[0] += 1
                dve.wait_ge(rs_got, norms_asked[0])

            def norm_weights(n):
                dve.wait_ge(ln_in[n % 2], LN_AT[n])

            def add_residual(dst, alpha, done, n):
                dve.wait_ge(done, n)
                for t in range(TT):
                    for n in range(2):
                        s_ = slice(n * 512, (n + 1) * 512)
                        last = dve.scalar_tensor_tensor(dst[:, t, s_], x[:, t, s_], alpha, bank[4 + 2 * t + n][:, :],
                                                        ALU.mult, ALU.add)
                link(last)
                dve.nop().then_inc(sums_evac, 1)

            def moments(src, tiles, width):
                for t in tiles:
                    for j in range(width // 512):
                        last = dve.bn_stats(stat[:, t * 12 + 6 * j:t * 12 + 6 * j + 6], src(t)[:, j * 512:(j + 1) * 512])
                    link(last)
                    link(dve.bn_aggr(mv[:, 2 * t:2 * t + 2], stat[:, t * 12:t * 12 + 6 * (width // 512)]))
                ask(dve.tensor_scalar(e2[:, 0:2], mv[:, 1:4:2], LN_EPS, None, ALU.add))

            def layer_norm(src):
                n = norms[0]
                norms[0] += 1
                moments(lambda t: src[:, t, :], range(TT), D)
                norm_weights(n)
                w = lnw[:, n % 2]
                for t in range(TT):
                    link(dve.scalar_tensor_tensor(src[:, t, :], src[:, t, :], mv[:, 2 * t:2 * t + 1], w[:, 0, :],
                                                  ALU.subtract, ALU.mult))
                for t in range(TT):
                    last = dve.scalar_tensor_tensor(x[:, t, :], src[:, t, :], rstd[:, t:t + 1], w[:, 1, :],
                                                    ALU.mult, ALU.add)
                last.then_inc(x_ready, 1)
                dve.wait_ge(x_ready, norms[0])

            def rms_norm(dst, n_sq, signal):
                n = norms[0]
                norms[0] += 1
                dve.wait_ge(rms_sq, 2 * n_sq + 2)
                ask(dve.tensor_scalar(e2[:, 0:2], ms[:, 0:2], 1.0 / D, RMS_EPS, ALU.mult, ALU.add))
                norm_weights(n)
                for t in range(TT):
                    last = dve.scalar_tensor_tensor(dst[:, t, :], x[:, t, :], rstd[:, t:t + 1], lnw[:, n % 2, 0, :],
                                                    ALU.mult, ALU.mult)
                    if signal is fin:
                        last.then_inc(fin, 1)
                if signal is not fin:
                    last.then_inc(signal, 1)

            def pairs(ap, n):
                return ap.rearrange("p (h s) -> p h s", h=2)[:, :, 0:n]

            def attention(a, add, v_off):
                for g in range(8 * a, 8 * a + 8):
                    t, hp, n = (g - 8 * a) // 4, (g - 8 * a) % 4, P * ((g - 8 * a) // 4 + 1)
                    dve.wait_ge(a_scores, g + 1)
                    if g >= 2:
                        dve.wait_ge(a_exp, g - 1)
                    link(dve.tensor_tensor(pairs(lg[:, g % 2, :], n), pair_banks(g, n),
                                           add(hp, T - n), ALU.add))
                    dve.tensor_reduce(negmax[:, 2 * (g % 2):2 * (g % 2) + 2], pairs(lg[:, g % 2, :], n),
                                      AX.X, ALU.max, negate=True).then_inc(a_max, 1)
                for t in range(TT):
                    dve.wait_ge(a_pv, 8 * a + 4 * (t + 1))
                    r0 = (a % 2) * 16 + t * 8
                    link(dve.reciprocal(rinv[:, t * 8:t * 8 + 8], rsum[:, r0:r0 + 8]))
                    dve.tensor_tensor(u[:, t, v_off:v_off + 512].rearrange("p (h d) -> p h d", h=8),
                                      bank[4 + t].rearrange("p (h d) -> p h d", h=8),
                                      rinv[:, t * 8:t * 8 + 8].unsqueeze(2).broadcast_to([P, 8, HD]),
                                      ALU.mult).then_inc(a_done, 1)

            def relative(i):
                return lambda hp, lo: bias[:, i, 2 * hp:2 * hp + 2, lo:T]

            def gates(s, ft, shift=0, n=T):
                for f in range(2):
                    dve.wait_ge(silu_done[s], ft + f + 1 + shift)
                    c = (ft + f) // 2
                    if c >= 2 and f == 0:
                        dve.wait_ge(down_done[s], c - 1 + (shift // 2 if isinstance(shift, int) else shift_half[0]))
                    dve.tensor_tensor(hT[:, c % 2, f, 0:n], hs[:, (ft + f) % 2, 0:n], bank[(ft + f) % 4][:, T:T + n],
                                      ALU.mult).then_inc(h_ready[s], 1)

            shift_half = [0]

            def ffn(s):
                gates(s, 0)
                gates(s, 2)
                with dve.Fori(0, 4) as r:
                    shift_half[0] = r * 2
                    gates(s, 4, r * 4)
                    gates(s, 6, r * 4)
                gates(s, 20)

            dve.memset(ones[:, :], 1.0).then_inc(filled, 1)
            dve.memset(half[:, :], -0.5).then_inc(filled, 1)
            dve.memset(table[:, :, :], 0.0).then_inc(filled, 1)

            def log_sigmoid(z, a, dst, n):
                dve.wait_ge(ls_a, n)
                dve.scalar_tensor_tensor(dst, z, 0.0, a, ALU.min, ALU.subtract).then_inc(ls_b, 1)

            log_sigmoid(gz[:, :, :], ga_[:, :, :], gnat[:, :, :], 1)
            for i in range(8):
                t, hp, n = i // 4, i % 4, P * (i // 4 + 1)
                dve.wait_ge(idx_relu, i + 1)
                for hh in range(2):
                    r = lg[:, i % 2, hh * T:hh * T + n]
                    w = wi[:, t, 2 * hp + hh:2 * hp + hh + 1]
                    if hp == 0 and hh == 0:
                        last = dve.tensor_scalar(score[:, t, 0:n], r, w, None, ALU.mult)
                    else:
                        last = dve.scalar_tensor_tensor(score[:, t, 0:n], r, w, score[:, t, 0:n], ALU.mult, ALU.add)
                    link(last)
                dve.nop().then_inc(idx_acc, 1)
            dve.wait_ge(step_evac, 11)
            for c in range(2):
                dve.tensor_scalar(ngc[:, c, 0:4], gT[:, c, 31:T:64], -1.0, None, ALU.mult)
                last = dve.tensor_scalar(ngc[:, c, 4:7], gT[:, c, 63:T - 64:64], -1.0, None, ALU.mult)
            last.then_inc(gla_neg, 1)
            for t in range(TT):
                n = P * (t + 1)
                link(dve.tensor_tensor(score[:, t, 0:n], score[:, t, 0:n], causal[:, T - n:T], ALU.add))
                for _ in range(TOPK // 8):
                    link(dve.max(top8, score[:, t, 0:n]))
                    link(dve.match_replace(score[:, t, 0:n], top8, score[:, t, 0:n], TAKEN))
                link(dve.tensor_scalar(score[:, t, 0:n], score[:, t, 0:n], 10.0 * NEG * 1e7, NEG, ALU.is_gt, ALU.mult))
            dve.nop().then_inc(mask_ready, 1)
            dve.wait_ge(gla_exp, 2)
            dve.wait_ge(step_evac, 11)
            dve.tensor_tensor(gq[:, :, :], gq[:, :, :], tb[:, 0:2, :], ALU.mult)
            dve.tensor_tensor(gk[:, :, :], gk[:, :, :], tb[:, 2:4, :], ALU.mult)
            dve.tensor_tensor(gqo[:, :, 64:T], gqo[:, :, 64:T], tb[:, 0:2, 64:T], ALU.mult)
            for j in (1, 2, 3):
                o = 64 * (j * (j - 1) // 2)
                last = dve.tensor_tensor(gko[:, :, o:o + 64 * j], gko[:, :, o:o + 64 * j], tb[:, 2:4, 0:64 * j], ALU.mult)
            last.then_inc(gla_ops, 1)
            for h in range(4):
                dve.wait_ge(gla_A, h + 1)
                dve.tensor_tensor(gA[:, h, 0:T], bank[h][:, 0:T], cum[:, 0, :], ALU.mult)
                dve.tensor_tensor(gA[:, h, T:384], bank[h][:, T:384], cum[:, 1, P:T], ALU.mult).then_inc(gla_Am, 1)
            dve.wait_ge(step_evac, 15)
            for t in range(TT):
                v4 = nr[:, t, :].rearrange("p (h d) -> p h d", h=4)
                link(dve.tensor_tensor(v4, v4, gnorm[:, :].unsqueeze(1).broadcast_to([P, 4, P]), ALU.mult))
            for t in range(TT):
                dve.wait_ge(gla_sq, t + 1)
                link(dve.tensor_reduce(ms[:, 4 * t:4 * t + 4], y[:, t, 0:512].rearrange("p (h d) -> p h d", h=4),
                                       AX.X, ALU.add))
            ask(dve.tensor_scalar(e2[:, 0:8], ms[:, 0:8], 1.0 / P, LN_EPS, ALU.mult, ALU.add))
            dve.wait_ge(rel_out, 48)
            for t in range(TT):
                v4 = nr[:, t, :].rearrange("p (h d) -> p h d", h=4)
                link(dve.tensor_tensor(v4, v4, rstd8[:, 4 * t:4 * t + 4].unsqueeze(2).broadcast_to([P, 4, P]), ALU.mult))
                last = dve.tensor_tensor(u[:, t, 0:512], nr[:, t, :], bank[4 + t][:, :], ALU.mult)
            last.then_inc(gla_done, 1)
            dve.wait_ge(rel_in[0], 16)
            attention(0, relative(0), 512)
            add_residual(y, ALPHA, sums_done, 1)
            layer_norm(y)
            ffn(0)
            add_residual(y, ALPHA, down_done[0], F_DENSE // FC)
            layer_norm(y)

            log_sigmoid(flz, fla, lf, 2)
            attention(1, lambda hp, lo: causal[:, lo:T].unsqueeze(1).broadcast_to([P, 2, T - lo]), 0)
            dve.wait_ge(rel_in[1], 16)
            attention(2, relative(1), 512)
            add_residual(y, ALPHA, sums_done, 2)
            layer_norm(y)

            dve.wait_ge(step_evac, STEPS_ROUTER)
            for t in range(TT):
                s8 = slice(8 * t, 8 * t + 8)
                link(dve.max(top8, rl[:, s8]))
                link(dve.max_index(topi[:, :], top8, rl[:, s8]))
                link(dve.tensor_copy(topf, topi[:, :]))
                link(dve.tensor_scalar(e2[:, t:t + 1], top8[:, 1:2], top8[:, 0:1], None, ALU.subtract))
                link(dve.tensor_scalar(chosen[:, s8], iota[:, 0:8], topf[:, 0:1], None, ALU.is_equal))
                link(dve.tensor_scalar(oh2[:, s8], iota[:, 0:8], topf[:, 1:2], None, ALU.is_equal))
            dve.nop().then_inc(gate_ask, 1)
            dve.wait_ge(gate_got, 1)
            link(dve.tensor_scalar(ms[:, 0:2], e2[:, 2:4], 1.0, None, ALU.add))
            link(dve.reciprocal(ms[:, 2:4], ms[:, 0:2]))
            link(dve.tensor_tensor(ms[:, 4:6], e2[:, 2:4], ms[:, 2:4], ALU.mult))
            for t in range(TT):
                s8 = slice(8 * t, 8 * t + 8)
                link(dve.tensor_scalar(comb[:, s8], chosen[:, s8], ms[:, 2 + t:3 + t], None, ALU.mult))
                link(dve.scalar_tensor_tensor(comb[:, s8], oh2[:, s8], ms[:, 4 + t:5 + t], comb[:, s8], ALU.mult, ALU.add))
                link(dve.tensor_tensor(chosen[:, s8], chosen[:, s8], oh2[:, s8], ALU.add))
            for t in range(TT):
                for r in range(2):
                    e_ = slice(r * 8, r * 8 + 8)
                    s8 = slice(8 * t, 8 * t + 8)
                    dve.tensor_copy(table[:, e_, 2 + t], chosen[:, s8])
                    link(dve.tensor_copy(table[:, e_, 4 + t], comb[:, s8]))
            dve.nop().then_inc(route_ready, 1)
            dve.wait_ge(step_evac, STEPS_ROUTER + 1)
            for t in range(TT):
                for r in range(2):
                    link(dve.tensor_scalar(table[:, r * 8:r * 8 + 8, t], slot[:, 8 * t:8 * t + 8], -1.0 - P * r, None, ALU.add))
            link(dve.tensor_reduce(trip_f[0:1, 0:1], oh2[0:1, 0:8], AX.X, ALU.max))
            link(dve.tensor_scalar(trip_f[0:1, 1:2], trip_f[0:1, 0:1], P + 0.5, float(NE), ALU.is_gt, ALU.mult))
            dve.tensor_scalar(trip_i[:, :], trip_f[0:1, 1:2], float(NE), None, ALU.add).then_inc(trip_ready, 1)
            for t in range(TT):
                link(dve.tensor_scalar(u[:, t, :], x[:, t, :], ALPHA, None, ALU.mult))

            def dispatch(e):
                dve.tensor_copy(cur[:, :], table[:, bass.ds(e, 1), :].rearrange("p a n -> p (a n)")).then_inc(cur_ready, 1)
                dve.wait_ge(cur_ready, e + 1)
                for t in range(TT):
                    last = dve.tensor_scalar(disp[:, t, :], iota[:, :], cur[:, t:t + 1], cur[:, 2 + t:3 + t],
                                             ALU.is_equal, ALU.mult)
                last.then_inc(disp_ready, 1)

            dispatch(0)
            dve.wait_ge(trip_ready, 1)
            trips = dve.value_load(trip_i[0:1, 0:1], min_val=NE, max_val=2 * NE)
            FT0, NCH = 2 * (F_DENSE // FC), F_MOE // FC
            with dve.Fori(0, trips) as e:
                shift_half[0] = e * NCH
                for c in range(NCH):
                    gates(0, FT0 + 2 * c, e * (2 * NCH), P)
                    if c == 1:
                        dve.wait_ge(pt_done, e + 1)
                        dispatch(e + 1)
                dve.wait_ge(down_done[0], e * NCH + (FT0 // 2 + NCH))
                dve.tensor_scalar(y[:, 0, 0:512], bank[4][:, :], slotg[:, 0:1], None, ALU.mult)
                dve.tensor_scalar(y[:, 0, 512:1024], bank[5][:, :], slotg[:, 0:1], None, ALU.mult).then_inc(ye_ready, 1)
                for t in range(TT):
                    for n in range(2):
                        dve.wait_ge(sc_done, e * 4 + (2 * t + n + 1))
                        s_ = u[:, t, n * 512:(n + 1) * 512]
                        dve.tensor_tensor(s_, s_, bank[2 * t + n][:, :], ALU.add).then_inc(sc_added, 1)
            dve.wait_ge(sc_added, trips * 4)
            layer_norm(u)

            rms_norm(u, 0, x_ready)
            upad = gA[:, :, 0:CONV - 1 + T]
            dve.memset(upad[:, :, 0:CONV - 1], 0.0)
            dve.wait_ge(conv_in, 1)
            link(dve.tensor_tensor(upad[:, :, CONV - 1:], ta[:, :, :], tb[:, :, :], ALU.mult))
            for j in range(CONV):
                for c in range(4):
                    if j == 0:
                        last = dve.tensor_scalar(ta[:, c, :], upad[:, c, 0:T], cw[:, c, 0:1], cw[:, c, 31:32], ALU.mult, ALU.add)
                    else:
                        last = dve.scalar_tensor_tensor(ta[:, c, :], upad[:, c, j:j + T], cw[:, c, j:j + 1], ta[:, c, :],
                                                        ALU.mult, ALU.add)
                link(last)
            dve.nop().then_inc(conv_done, 1)
            dve.wait_ge(rel_in[2], 16)
            attention(3, relative(2), 0)
            dve.wait_ge(step_evac, STEPS_CONV)
            moments(lambda t: nr[:, t, :], range(TT), 512)
            for t in range(TT):
                link(dve.scalar_tensor_tensor(nr[:, t, :], nr[:, t, :], mv[:, 2 * t:2 * t + 1], convln[:, 0, :],
                                              ALU.subtract, ALU.mult))
                dve.scalar_tensor_tensor(nr[:, t, :], nr[:, t, :], rstd[:, t:t + 1], convln[:, 1, :],
                                         ALU.mult, ALU.add).then_inc(conv_n, 1)
            add_residual(x, 1.0, sums_done, 3)
            dve.nop().then_inc(x2_ready, 1)
            rms_norm(u, 1, x_ready)
            ffn(1)
            add_residual(x, 1.0, down_done[1], F_DENSE // FC)
            dve.nop().then_inc(x2_ready, 1)
            rms_norm(u, 2, fin)

        @block.gpsimd
        def _(pool):
            def weights(n, rows):
                if n >= 2:
                    pool.wait_ge(x_ready, n - 1)
                for i, r in enumerate(rows):
                    pool.dma_start(lnw[:, n % 2, i, :], r.broadcast_to([P, D])).then_inc(ln_in[n % 2], 16)

            def rstd_of(n):
                asked[0] += 1
                pool.wait_ge(rs_ask, asked[0])
                pool.tensor_tensor(rstd8[:, 0:n], e2[:, 0:n], half[:, 0:n], ALU.pow).then_inc(rs_got, 1)

            asked = [0]
            weights(0, (ln_g[0, 0:1, :], ln_b[0, 0:1, :]))
            weights(1, (ln_g[0, 1:2, :], ln_b[0, 1:2, :]))
            for i in range(3):
                pool.wait_ge(step_evac, 6 + i)
                pool.dma_start(rel_dram[i].rearrange("t h j -> h t j"),
                               relrow[:, i, :].unsqueeze(1).broadcast_to([H, P, REL])).then_inc(rel_out, 16)
            pool.wait_ge(rel_out, 48)
            for i in range(3):
                src = bass.AP(rel_dram.tensor, i * P * H * REL + P - 1, [[H * REL - 1, P], [REL, H], [1, T]])
                pool.dma_start(bias[:, i, :, :], src).then_inc(rel_in[i], 16)
            pool.wait_ge(filled, 3)
            rstd_of(8)
            rstd_of(2)
            weights(2, (ln_g[1, 0:1, :], ln_b[1, 0:1, :]))
            rstd_of(2)
            weights(3, (ln_g[1, 1:2, :], ln_b[1, 1:2, :]))
            rstd_of(2)
            weights(4, (mix_norm_g_2,))
            rstd_of(2)
            weights(5, (ffn_norm_g_2,))
            rstd_of(2)
            rstd_of(2)
            weights(6, (final_norm_g_2.rearrange("(a d) -> a d", a=1),))
            rstd_of(2)
            rstd_of(2)


def constants():
    import numpy as np

    t = np.arange(T)
    cum = (t[:, None] <= t[None, :]).astype(np.float32).reshape(TT, P, T).transpose(1, 0, 2)
    dist = np.arange(255, 255 - REL, -1)

    def bucket(furthest):
        d = np.maximum(dist, 1).astype(np.float32)
        far = 16 + (np.log(d / np.float32(16)) / np.float32(np.log(furthest / 16)) * np.float32(16)).astype(np.int32)
        return np.where(dist < 16, np.maximum(dist, 0), np.minimum(far, 31))

    onehot = np.stack([(bucket(f)[None, :] == np.arange(32)[:, None]) for f in (2048, 128)], 1).astype(np.float32)
    times = (dist <= 128).astype(int) + (dist % 4 == 0) + (dist % 16 == 0)
    past = dist >= 0
    plain = np.where(past, 0.0, NEG)
    dilated = np.where(past & (times > 0), np.log(np.maximum(times, 1)), NEG)
    rowadd = np.stack([plain, dilated, plain])[None].astype(np.float32)
    rowsel = np.zeros((8, 8, P), np.float32)
    for h in range(8):
        rowsel[h, h] = 1
    q = P + np.arange(P)
    return {
        "c_ident": np.eye(P, dtype=np.float32),
        "c_cum": np.ascontiguousarray(cum),
        "c_causal": np.where(t[None, :] <= q[:, None], 0.0, NEG).astype(np.float32),
        "c_iota": np.broadcast_to(np.arange(P, dtype=np.float32), (P, P)).copy(),
        "c_onehot": onehot,
        "c_rowadd": rowadd,
        "c_rowsel": rowsel,
    }


INS = ["x", "ln_g", "ln_b", "rel_table", "w_in_ab", "w_gate_a", "b_gate_a", "g_norm_a", "w_out_ab", "w_in_cd",
       "b_forget", "w_out_cd", "w1_dense", "w3_dense", "w2_dense", "w_router", "w1_moe", "w3_moe", "w2_moe",
       "mix_norm_g_2", "w_in_2", "rel_bias_2", "conv_w_2", "conv_b_2", "conv_ln_g_2", "conv_ln_b_2", "w_out_2",
       "ffn_norm_g_2", "w_gate_2", "w_up_2", "w_down_2", "final_norm_g_2"]


def kernel(**inputs):
    import numpy as np
    import concourse.bacc as bacc
    from concourse.bass_utils import run_bass_kernel_spmd

    nc = bacc.Bacc("TRN2", target_bir_lowering=False, num_devices=1)
    arrays, args = {}, []
    for name, a in [(n, np.ascontiguousarray(inputs[n])) for n in INS] + list(constants().items()):
        arrays[f"in_{name}"] = a
        args.append(nc.dram_tensor(f"in_{name}", a.shape, mybir.dt.from_np(a.dtype), kind="ExternalInput").ap())
    args.append(nc.dram_tensor("out_0", (1, T, D), F32, kind="ExternalOutput").ap())
    build(nc, *args)
    r = run_bass_kernel_spmd(nc, [arrays], core_ids=[0])
    return r.results[0]["out_0"]
```

```python
import concourse.bass as bass
from concourse import mybir
from contextlib import ExitStack

F32 = mybir.dt.float32
F32R = mybir.dt.float32r
I32 = mybir.dt.int32
U32 = mybir.dt.uint32
ALU = mybir.AluOpType
ACT = mybir.ActivationFunctionType
AX = mybir.AxisListType

P = 128
T = 256
TT = T // P
D = 1024
KT = D // P
H = 8
HD = 64
TOPK = 64
F_DENSE = 2816
F_MOE = 3584
FC = 256
NE = 8
UNITS = 6
UW = 2048
ALPHA = 4.0 ** 0.25
NEG = -1e30
TAKEN = -3e38
REL = 384
CONV = 31
LN_EPS = 1e-5
RMS_EPS = 1e-6
LN_AT = [32, 64, 96, 144, 144, 160, 176]
STEPS_ROUTER = 39
STEPS_CONV = 53
CONSTS = 16 * 11
NARROW = 168
NCH_D = F_DENSE // FC
NCH_M = F_MOE // FC
C_BODY = 2 * NCH_M
L_BODY = 3 * NCH_M


def stream():
    dense = "cc" + "cc" + "r" + "ccrccr" * 4 + "cc" + "r" + "r"
    return "c" * 18 + dense + "c" * 16


def stream_2():
    return "c" * 12 + "cc" + "cc" + "r" + "ccrccr" * 4 + "cc" + "r" + "r"


def expert_kinds():
    return "cc" + "ccr" * (NCH_M - 1) + "r"

AB = dict(qa=0, ka=256, va=512, ra=1024, ga=1536, qb=1552, kb=2064, vb=2576, qi=3088, ki=3600, wi=3664)
CD = dict(qc=0, kc=512, vc=1024, fc=1536, qd=1544, kd=2056, vd=2568)
B2 = dict(q=0, k=512, v=1024, a=1536, g=2048)
AB_ORDER = [AB["qi"], AB["qi"] + 256, AB["qa"], AB["ka"], AB["va"], AB["va"] + 256, AB["ra"], AB["ra"] + 256,
            AB["qb"], AB["qb"] + 256, AB["kb"], AB["kb"] + 256, AB["vb"], AB["vb"] + 256]
CD_ORDER = [CD[n] + 256 * i for n in ("qc", "kc", "vc", "qd", "kd", "vd") for i in range(2)]
B2_ORDER = [B2[n] + 256 * i for n in ("a", "g", "q", "k", "v") for i in range(2)]


def build(nc, x_in, ln_g, ln_b, rel_table, w_in_ab, w_gate_a, b_gate_a, g_norm_a, w_out_ab, w_in_cd,
          b_forget, w_out_cd, w1_dense, w3_dense, w2_dense, w_router, w1_moe, w3_moe, w2_moe,
          mix_norm_g_2, w_in_2, rel_bias_2, conv_w_2, conv_b_2, conv_ln_g_2, conv_ln_b_2, w_out_2,
          ffn_norm_g_2, w_gate_2, w_up_2, w_down_2, final_norm_g_2,
          c_ident, c_cum, c_causal, c_iota, c_onehot, c_rowadd, c_rowsel, out):
    ctx = ExitStack()
    with ctx:
        def sb(name, shape, dt=F32):
            return ctx.enter_context(nc.sbuf_tensor(name, shape, dt))

        def sem(name):
            return ctx.enter_context(nc.semaphore(name))

        ring = sb("ring", [P, UNITS, UW])
        x = sb("x", [P, TT, D])
        u = sb("u", [P, TT, D])
        wh = sb("wh", [P, 2, UW], F32R)
        wl = sb("wl", [P, 2, UW], F32R)
        xTh = sb("xTh", [P, KT, T], F32R)
        xTl = sb("xTl", [P, KT, T], F32R)
        wnh = sb("wnh", [P, KT, NARROW], F32R)
        wnl = sb("wnl", [P, KT, NARROW], F32R)
        lnw = sb("lnw", [P, 2, D])
        y = sb("y", [P, TT, D])
        ident = sb("ident", [P, P])
        cum = sb("cum", [P, TT, T])
        causal = sb("causal", [P, T])
        iota = sb("iota", [P, P])
        ones = sb("ones", [P, P])
        rel = sb("rel", [32, 2, H])
        bias = sb("bias", [P, H, T])
        bforget = sb("bforget", [8, 1])
        gnorm = sb("gnorm", [P, P])
        cw = sb("cw", [P, 4, 32])
        tq = sb("tq", [P, 4, T])
        tk = sb("tk", [P, 4, T])
        nv = sb("nv", [P, TT, 512])
        ta = sb("ta", [P, 4, T])
        tb = sb("tb", [P, 4, T])
        nw = sb("nw", [P, TT, 512])
        nr = sb("nr", [P, TT, 512])
        wgate = nw[0:16, 0, 0:256]
        bgate = nw[0:1, 1, 0:256]
        nt = tb[0:24, 0, :]
        kiT = sb("kiT", [P, T])
        wi = sb("wi", [P, TT, 8])
        score = sb("score", [P, TT, T])
        lg = sb("lg", [P, 2, 512])
        pr = sb("pr", [P, 2, 512])
        pT = sb("pT", [P, 2, 512])
        gnat = sb("gnat", [P, TT, T])
        gT = sb("gT", [P, 2, T])
        ngc = sb("ngc", [P, 2, 8])
        gA = sb("gA", [P, 4, 384])
        small = sb("small", [P, 256])
        rstd_t = sb("rstd", [P, 8])
        topi = sb("topi", [P, 8], U32)
        trip_i = sb("trip_i", [1, 1], I32)
        half = sb("half", [P, 8])
        table = sb("table", [P, 2 * NE + 1, 6])
        cur = sb("cur", [P, 6])
        slotg = sb("slotg", [P, 1])
        psum = ctx.enter_context(nc.psum_tensor("psum", [P, 8, 512], F32))
        bank = [psum[:, i, :] for i in range(8)]

        def pair_banks(i, n):
            return psum[:, 2 * (i % 2):2 * (i % 2) + 2, 0:n]

        rel_dram = nc.dram_tensor("rel_scratch", (3, P, H, REL), F32, kind="Internal").ap()

        uf = u.rearrange("p t d -> p (t d)")
        onehot = uf[0:32, 0:2 * REL].rearrange("p (a n) -> p a n", a=2)
        relrow = uf[0:8, 2 * REL:5 * REL].rearrange("p (a n) -> p a n", a=3)
        rowadd = gA.rearrange("p h n -> p (h n)")[0:1, 0:3 * REL].rearrange("p (a n) -> p a n", a=3)
        gz = pr[:, 0, :].rearrange("p (t n) -> p t n", t=2)
        ga_ = pr[:, 1, :].rearrange("p (t n) -> p t n", t=2)
        yf = y.rearrange("p t d -> p (t d)")
        gq, gk, gqo = (yf[:, 512 * i:512 * i + 512].rearrange("p (c t) -> p c t", c=2) for i in range(3))
        nvf = nv.rearrange("p t n -> p (t n)")
        gko = nvf[:, 0:768].rearrange("p (c t) -> p c t", c=2)
        wnraw = yf[:, 0:KT * NARROW].rearrange("p (k n) -> p k n", k=KT)
        gaf = gA.rearrange("p h n -> p (h n)")
        rowsel = gaf[0:8, 0:8 * P].rearrange("p (h t) -> p h t", h=8)
        convw = gT.rearrange("p c t -> p (c t)")[0:32, :]
        convg = score.rearrange("p t n -> p (t n)")
        convb = gnat.rearrange("p t n -> p (t n)")
        mixg = lg.rearrange("p a n -> p (a n)")
        hT = tq.rearrange("p (c f) t -> p c f t", c=2)
        hs = tk[:, 0:2, :]
        hn = tk[:, 2:4, :]
        disp = nv[:, 0, 0:T].rearrange("p (t j) -> p t j", t=TT)
        dispT = nv[:, 1, 0:T]

        negmax = small[:, 0:4]
        rsum = small[:, 8:40]
        rinv = small[:, 240:256]
        stat = small[:, 40:64]
        mv = small[:, 64:72]
        top8 = small[:, 76:84]
        ms = small[:, 84:92]
        e2 = small[:, 92:100]
        rstd8 = rstd_t[:, 0:8]
        rstd = rstd_t[:, 0:2]
        comb = small[:, 100:116]
        chosen = small[:, 116:132]
        slot = small[:, 132:148]
        oh2 = small[:, 148:164]
        rl = small[:, 164:180]
        topf = small[:, 180:188]
        trip_f = small[:, 188:190]
        lf = small[:, 192:208]
        flz = small[:, 208:224]
        fla = small[:, 224:240]
        nfT = gnat[0:8, 0, :]

        landed = [[sem(f"unit{i}_landed_{s}") for i in range(UNITS)] for s in range(2)]
        taken = [[sem(f"unit{i}_taken_{s}") for i in range(UNITS)] for s in range(2)]
        hi_ready = [sem("upper_halves_0"), sem("upper_halves_1")]
        split_used = [sem("halves_used_0"), sem("halves_used_1")]
        narrow_hi = sem("narrow_upper")
        narrow_lo = sem("narrow_lower")
        consts_in = sem("consts_in")
        filled = sem("fills_done")
        x_in_sem = sem("x_in")
        small_in = sem("small_in")
        ln_in = sem("norm_weights")
        late_in = sem("late_constants")
        rel_out = sem("rel_rows_out")
        rel_in = [sem(f"rel_bias_in_{i}") for i in range(3)]
        rel_ready = sem("rel_row_ready")
        tr_done = sem("transposed")
        tr_evac = sem("transposed_upper")
        tr_low = sem("transposed_lower")
        step_done = sem("step_done")
        step_evac = sem("step_copied")
        idx_scores = sem("indexer_scores")
        idx_relu = sem("indexer_relu")
        idx_acc = sem("indexer_summed")
        mask_ready = sem("key_mask_ready")
        ls_a = sem("log_sigmoid_parts")
        ls_b = sem("log_sigmoid_ready")
        gla_neg = sem("gla_negated")
        gla_exp = sem("gla_exponentials")
        gla_ops = sem("gla_operands")
        gla_A = sem("gla_products")
        gla_Am = sem("gla_products_masked")
        gla_o = sem("gla_out")
        gla_sq = sem("gla_squares")
        gla_done = sem("gla_normed")
        a_scores = sem("scores_ready")
        a_max = sem("max_ready")
        a_exp = sem("probs_ready")
        a_tr = sem("probs_transposed")
        a_pT = sem("probs_copied")
        a_pv = sem("probs_used")
        a_done = sem("heads_normed")
        mix_done = sem("mixer_out_ready")
        sums_done = sem("sums_ready")
        sums_evac = sem("sums_copied")
        x_ready = sem("norm_ready")
        rs_ask = sem("variance_ready")
        rs_got = sem("rstd_ready")
        m_up = sem("expert_hidden")
        m_silu = sem("expert_silu")
        m_gate = sem("expert_gated")
        m_tr = sem("expert_hidden_transposed")
        m_hT = sem("expert_hidden_copied")
        m_down = sem("expert_down_done")
        xe_low = sem("gathered_lower")
        up_done = [sem("hidden_ready_0"), sem("hidden_ready_1")]
        silu_done = [sem("silu_ready_0"), sem("silu_ready_1")]
        h_ready = [sem("gated_ready_0"), sem("gated_ready_1")]
        down_done = [sem("down_done_0"), sem("down_done_1")]
        route_ready = sem("routes_ready")
        trip_ready = sem("trip_ready")
        cur_ready = sem("expert_columns_ready")
        disp_ready = sem("dispatch_ready")
        xe_done = sem("gathered")
        xe_ready = sem("gathered_copied")
        ye_ready = sem("expert_out_scaled")
        sc_done = sem("scattered")
        sc_added = sem("scattered_added")
        pt_done = sem("dispatch_transposed")
        pt_ready = sem("dispatch_copied")
        moe_done = sem("moe_done")
        rms_sq = sem("squares_ready")
        x2_ready = sem("residual_ready")
        gate_ask = sem("gate_logits_ready")
        gate_got = sem("gate_exps_ready")
        conv_in = sem("conv_in_ready")
        conv_done = sem("conv_done")
        conv_n = sem("conv_normed")
        conv_out = sem("conv_out")
        fin = sem("final_ready")
        stored = sem("stored")
        v_chain = sem("vector_chain")
        a_chain = sem("scalar_chain")
        g_chain = sem("pool_chain")

        def by_rows(w):
            return w.rearrange("(k p) n -> p k n", p=P)

        win = [by_rows(w_in_ab[0]), by_rows(w_in_cd[0]), by_rows(w_in_2[0])]
        wout = [by_rows(w_out_ab[0]), by_rows(w_out_cd[0]), by_rows(w_out_2[0])]

        def as_cols(i):
            return ring[:, i, :].rearrange("p (k n) -> p k n", k=KT)

        def as_rows(i):
            return ring[:, i, :].rearrange("p (k n) -> p k n", k=2)

        KINDS = [stream(), stream_2()]
        N0 = [0, len(KINDS[0]) + 2]
        C_ALL = KINDS[0].count("c")

        class Split:
            def __init__(self):
                self.s, self.i, self.more, self.rounds = 0, 0, 0, 0
                self.at = [[n for n, k in enumerate(KINDS[s] + (expert_kinds() + "cc" if s == 0 else "")) if k == "c"]
                           for s in range(2)]

            def place(self):
                i = self.i
                n = self.at[self.s][i]
                self.i += 1
                u_ = (n + N0[self.s]) % UNITS
                return u_, self.rounds + (n // UNITS + 1), i % 2, i + self.more

            def round(self, more, rounds):
                self.more, self.rounds = more, rounds

            def second(self):
                self.s, self.i, self.more, self.rounds = 1, 0, 0, 0

        block = ctx.enter_context(nc.Block())

        @block.sync
        def _(sp):
            at = [0]
            st = [0]

            def load(dst_of, src, j=0, rounds=0):
                s_, n = st[0], at[0] + j
                i = (n + N0[s_]) % UNITS
                if n >= UNITS:
                    sp.wait_ge(taken[s_][i], rounds + n // UNITS)
                elif s_ == 1:
                    last = N0[1] - 1 - (N0[1] - 1 - i) % UNITS
                    sp.wait_ge(taken[0][i], trips * (L_BODY // UNITS) + (last // UNITS + 1))
                sp.dma_start(dst_of(i), src).then_inc(landed[s_][i], 16)

            def load_all(units, rounds=None):
                for j, (form, src) in enumerate(units):
                    if rounds is None:
                        load(form, src)
                        at[0] += 1
                    else:
                        load(form, src, j, rounds)

            def cols(w, c):
                return as_cols, w[:, :, bass.ds(c, 256)]

            def rows(w, k):
                return as_rows, w[:, bass.ds(k, 2), :]

            def ffn(w1, w3, w2):
                w1, w3, w2 = by_rows(w1), by_rows(w3), by_rows(w2)

                def up(c):
                    return [cols(w1, c * FC), cols(w3, c * FC)]

                def down(c):
                    return [rows(w2, c * 2)]

                load_all(up(0) + up(1) + down(0))
                with sp.Fori(0, 4) as r_:
                    load_all(up(r_ * 2 + 2) + down(r_ * 2 + 1) + up(r_ * 2 + 3) + down(r_ * 2 + 2), r_)
                at[0] += 6 * 4
                load_all(up(10) + down(9) + down(10))

            sp.dma_start(x[:, :, :], x_in[0].rearrange("(a p) d -> p a d", p=P)).then_inc(x_in_sem, 16)
            sp.dma_start(ident[:, :], c_ident).then_inc(x_in_sem, 16)
            for c, src in ((0, win[0][:, :, AB["ga"]:AB["ga"] + 16]), (16, win[0][:, :, AB["wi"]:AB["wi"] + 8]),
                           (24, win[0][:, :, AB["ki"]:AB["ki"] + 64]), (88, win[0][:, :, AB["ki"]:AB["ki"] + 64]),
                           (152, win[1][:, :, CD["fc"]:CD["fc"] + 8]), (160, by_rows(w_router[0]))):
                sp.dma_start(wnraw[:, :, c:c + src.shape[2]], src).then_inc(small_in, 16)
            load_all([cols(win[0], c) for c in AB_ORDER])
            load_all([rows(wout[0], 2 * j) for j in range(4)])
            ffn(w1_dense[0], w3_dense[0], w2_dense[0])
            load_all([cols(win[1], c) for c in CD_ORDER])
            load_all([rows(wout[1], 2 * j) for j in range(4)])

            m1 = w1_moe[0].rearrange("e (k p) n -> e p k n", p=P)
            m3 = w3_moe[0].rearrange("e (k p) n -> e p k n", p=P)
            m2 = w2_moe[0].rearrange("e (k p) n -> e p k n", p=P)

            def expert(e, passes):
                def part(form, w, k, n):
                    return form, w[bass.ds(e, 1), :, k, n].rearrange("a p k n -> p (a k) n")

                units = []
                for c in range(NCH_M + 1):
                    if c < NCH_M:
                        n = slice(c * FC, (c + 1) * FC)
                        units += [part(as_cols, m1, slice(0, KT), n), part(as_cols, m3, slice(0, KT), n)]
                    if c > 0:
                        units += [part(as_rows, m2, slice(2 * c - 2, 2 * c), slice(0, D))]
                load_all(units, passes * (L_BODY // UNITS))

            with sp.Fori(0, NE) as e:
                expert(e, e)
            sp.wait_ge(trip_ready, 1)
            trips = sp.value_load(trip_i[0:1, 0:1], min_val=NE, max_val=2 * NE)
            with sp.If(trips > NE):
                with sp.Fori(0, NE) as e:
                    expert(e, e + NE)
            for j in range(2):
                load(*cols(win[2], B2_ORDER[j]), j, trips * (L_BODY // UNITS))
            st[0], at[0] = 1, 0
            load_all([cols(win[2], c) for c in B2_ORDER[2:]])
            load_all([rows(wout[2], 2 * j) for j in range(4)])
            ffn(w_gate_2[0], w_up_2[0], w_down_2[0])
            sp.wait_ge(fin, 2)
            sp.dma_start(out[0].rearrange("(a p) d -> p a d", p=P), u[:, :, :]).then_inc(stored, 16)
            sp.wait_ge(stored, 16)

        @block.tensor
        def _(pe):
            halves = Split()
            raw = [0]
            steps = [0]
            trs = [0]
            sums = [0]
            freed = []

            def first_of(ins):
                if freed:
                    ins.then_inc(freed.pop(), 1)

            def split_unit(form):
                u_, loads, i, n = halves.place()
                pe.wait_ge(taken[halves.s][u_], loads)
                w_h, w_l = wh[:, i, :], wl[:, i, :]
                if form == "cols":
                    return (w_h.rearrange("p (k n) -> p k n", k=KT), w_l.rearrange("p (k n) -> p k n", k=KT))
                return (w_h.rearrange("p (k n) -> p k n", k=2), w_l.rearrange("p (k n) -> p k n", k=2))

            def split_done():
                freed.append(split_used[halves.s])

            def raw_unit(n, rounds=0):
                i = (n + N0[halves.s]) % UNITS
                pe.wait_ge(landed[halves.s][i], 16 * (n // UNITS + 1) + rounds)
                return as_rows(i), taken[halves.s][i]

            def thirds(o, ws, xs, first, final, turned=False):
                a, b_ = (ws, xs) if not turned else (xs, ws)
                last = pe.matmul(o, a[0], b_[0], start=first, stop=False)
                first_of(last)
                pe.matmul(o, a[0], b_[1], start=False, stop=False)
                return pe.matmul(o, a[1], b_[0], start=False, stop=final)

            def step_bank():
                j = steps[0]
                steps[0] += 1
                if j >= 2:
                    pe.wait_ge(step_evac, j - 1)
                return bank[6 + j % 2]

            def proj_transposed():
                ps = step_bank()
                h_, l_ = split_unit("cols")
                for c in range(2):
                    n = slice(c * P, (c + 1) * P)
                    for k in range(KT):
                        last = thirds(ps[:, c * T:(c + 1) * T], (h_[:, k, n], l_[:, k, n]), (xTh[:, k, :], xTl[:, k, :]),
                                      k == 0, k == KT - 1)
                last.then_inc(step_done, 1)
                split_done()

            def proj_natural():
                ps = step_bank()
                h_, l_ = split_unit("cols")
                for t in range(TT):
                    m = slice(t * P, (t + 1) * P)
                    for k in range(KT):
                        last = thirds(ps[:, t * 256:(t + 1) * 256], (h_[:, k, :], l_[:, k, :]), (xTh[:, k, m], xTl[:, k, m]),
                                      k == 0, k == KT - 1, turned=True)
                last.then_inc(step_done, 1)
                split_done()

            def narrow(c0, n):
                ps = step_bank()
                for k in range(KT):
                    last = thirds(ps[0:n, 0:T], (wnh[:, k, c0:c0 + n], wnl[:, k, c0:c0 + n]), (xTh[:, k, :], xTl[:, k, :]),
                                  k == 0, k == KT - 1)
                last.then_inc(step_done, 1)
                pe.wait_ge(step_evac, steps[0])
                ps = step_bank()
                for t in range(TT):
                    last = pe.transpose(ps[:, t * n:(t + 1) * n], nt[0:n, t * P:(t + 1) * P], ident[0:n, 0:n])
                last.then_inc(step_done, 1)

            def transposes(src):
                for g in range(4):
                    for k in (2 * g, 2 * g + 1):
                        for t in range(TT):
                            last = pe.transpose(bank[g][:, (k % 2) * T + t * P:(k % 2) * T + (t + 1) * P],
                                                src[:, t, k * P:(k + 1) * P], ident[:, :])
                            first_of(last)
                    last.then_inc(tr_done, 1)
                trs[0] += 4
                pe.wait_ge(tr_low, trs[0])

            def attention(a, q, k, v, masked=False, forget=False):
                def scores(g):
                    i = g - 8 * a
                    t, hp, n = i // 4, i % 4, P * (i // 4 + 1)
                    if g >= 2:
                        pe.wait_ge(a_max, g - 1)
                    for hh in range(2):
                        rows = slice(HD * hh, HD * hh + HD)
                        o = bank[2 * (g % 2) + hh][:, 0:n]
                        more = masked or forget
                        last = pe.matmul(o, q[rows, hp, t * P:(t + 1) * P], k[rows, hp, 0:n],
                                         start=True, stop=not more)
                        if g == 8 * a and hh == 0:
                            first_of(last)
                        if masked:
                            last = pe.matmul(o, ident[:, :], score[:, t, 0:n], start=False, stop=True)
                        if forget:
                            last = pe.matmul(o, rowsel[:, 2 * hp + hh, :], nfT[:, 0:n], start=False, stop=True)
                    last.then_inc(a_scores, 1)

                def turn(g):
                    t = (g - 8 * a) // 4
                    pe.wait_ge(a_exp, g + 1)
                    if g >= 2:
                        pe.wait_ge(a_pT, g - 1)
                    for hh in range(2):
                        for s in range(t + 1):
                            last = pe.transpose(bank[6 + g % 2][:, (2 * hh + s) * P:(2 * hh + s + 1) * P],
                                                pr[:, g % 2, hh * T + s * P:hh * T + (s + 1) * P], ident[:, :])
                    last.then_inc(a_tr, 1)

                def values(g):
                    i = g - 8 * a
                    t, hp = i // 4, i % 4
                    pe.wait_ge(a_pT, g + 1)
                    if hp == 0 and a > 0:
                        pe.wait_ge(a_done, 2 * (a - 1) + t + 1)
                    for hh in range(2):
                        h = 2 * hp + hh
                        for s in range(t + 1):
                            last = pe.matmul(bank[4 + t][:, h * HD:(h + 1) * HD],
                                             pT[:, g % 2, (2 * hh + s) * P:(2 * hh + s + 1) * P],
                                             v[:, s, h * HD:(h + 1) * HD], start=(s == 0), stop=(s == t))
                    last.then_inc(a_pv, 1)

                for g in range(8 * a, 8 * a + 10):
                    if g < 8 * a + 8:
                        scores(g)
                    if 8 * a < g <= 8 * a + 8:
                        turn(g - 1)
                    if g >= 8 * a + 2:
                        values(g - 2)

            def out_projection():
                pe.wait_ge(step_evac, steps[0])
                for j in range(4):
                    h_, l_ = split_unit("rows")
                    for kk in range(2):
                        k = 2 * j + kk
                        for t in range(TT):
                            m = slice(t * P, (t + 1) * P)
                            for n in range(2):
                                c = slice(n * 512, (n + 1) * 512)
                                last = thirds(bank[4 + 2 * t + n][:, :], (h_[:, kk, c], l_[:, kk, c]),
                                              (xTh[:, k, m], xTl[:, k, m]), k == 0, k == KT - 1, turned=True)
                    if j == 3:
                        last.then_inc(sums_done, 1)
                    split_done()
                sums[0] += 1

            def up(s, ft, shift=0):
                for w in range(2):
                    h_, l_ = split_unit("cols")
                    for f in range(2):
                        ps = bank[(ft + f) % 4]
                        if w == 0 and ft + f >= 4:
                            pe.wait_ge(h_ready[s], ft + f - 3 + shift)
                        m = slice(f * P, (f + 1) * P)
                        for k in range(KT):
                            last = thirds(ps[:, w * T:(w + 1) * T], (h_[:, k, m], l_[:, k, m]), (xTh[:, k, :], xTl[:, k, :]),
                                          k == 0, k == KT - 1)
                        if w == 1:
                            last.then_inc(up_done[s], 1)
                    split_done()

            def down(s, c, n0, first, final, shift=0, rounds=0):
                w, used = raw_unit(n0, rounds)
                pe.wait_ge(h_ready[s], 2 * c + 2 + shift)
                for f in range(2):
                    for t in range(TT):
                        for n in range(2):
                            last = pe.matmul(bank[4 + 2 * t + n][:, :], hT[:, c % 2, f, t * P:(t + 1) * P],
                                             w[:, f, n * 512:(n + 1) * 512],
                                             start=first and f == 0, stop=final and f == 1)
                            first_of(last)
                last.then_inc(down_done[s], 1)
                freed.append(used)

            def ffn(s, n0):
                pe.wait_ge(sums_evac, sums[0])
                up(s, 0)
                up(s, 2)
                down(s, 0, n0 + 4, True, False)
                i0 = halves.i
                with pe.Fori(0, 4) as r:
                    halves.round(r * 4, r)
                    up(s, 4, r * 4)
                    down(s, 1, n0 + 7, False, False, r * 4, r * 16)
                    up(s, 6, r * 4)
                    down(s, 2, n0 + 10, False, False, r * 4, r * 16)
                halves.round(0, 0)
                halves.i = i0 + 16
                up(s, 20)
                down(s, 9, n0 + 31, False, False)
                down(s, 10, n0 + 32, False, True)
                sums[0] += 1

            pe.wait_ge(x_in_sem, 32)
            pe.wait_ge(filled, 3)
            transposes(x)
            pe.wait_ge(narrow_lo, 1)
            ps = step_bank()
            for k in range(KT):
                last = thirds(ps[:, 0:T], (wnh[:, k, 24:152], wnl[:, k, 24:152]), (xTh[:, k, :], xTl[:, k, :]),
                              k == 0, k == KT - 1)
            last.then_inc(step_done, 1)
            narrow(0, 24)
            proj_transposed()
            proj_transposed()
            pe.wait_ge(consts_in, CONSTS)
            ps = step_bank()
            for t in range(TT):
                first_of(pe.matmul(ps[:, t * T:(t + 1) * T], nt[0:16, t * P:(t + 1) * P], wgate[:, :],
                                   start=True, stop=False))
                last = pe.matmul(ps[:, t * T:(t + 1) * T], ones[0:1, :], bgate[:, :], start=False, stop=True)
            last.then_inc(step_done, 1)
            for i, w in enumerate((0, 0, 1)):
                ps = step_bank()
                pe.matmul(ps[0:8, 0:REL], rel[:, w, :], onehot[:, w, :], start=True, stop=False)
                pe.matmul(ps[0:8, 0:REL], ones[0:1, 0:8], rowadd[:, i, :], start=False, stop=True).then_inc(step_done, 1)
            for i in range(8):
                t, hp, n = i // 4, i % 4, P * (i // 4 + 1)
                if i == 0:
                    pe.wait_ge(step_evac, 5)
                if i >= 2:
                    pe.wait_ge(idx_relu, i - 1)
                for hh in range(2):
                    rows = slice(HD * hh, HD * hh + HD)
                    last = pe.matmul(bank[2 * (i % 2) + hh][:, 0:n], ta[rows, hp, t * P:(t + 1) * P],
                                     kiT[rows, 0:n], start=True, stop=True)
                last.then_inc(idx_scores, 1)
            proj_transposed()
            proj_transposed()
            pe.wait_ge(ls_b, 1)
            ps = step_bank()
            for c in range(2):
                for t in range(TT):
                    last = pe.matmul(ps[:, c * T:(c + 1) * T], gnat[:, t, c * P:(c + 1) * P], cum[:, t, :],
                                     start=(t == 0), stop=(t == 1))
                    first_of(last)
            last.then_inc(step_done, 1)
            for _ in range(4):
                proj_natural()
            pe.wait_ge(idx_relu, 8)
            pe.wait_ge(gla_ops, 1)
            for h in range(4):
                r, c = slice(HD * (h % 2), HD * (h % 2) + HD), h // 2
                b_ = bank[h]
                for o, m, kk, qq in (
                    (b_[0:P, 0:64], P, gk[r, c, 0:P], gq[r, c, 0:64]),
                    (b_[64:P, 64:P], 64, gk[r, c, 64:P], gq[r, c, 64:P]),
                    (b_[0:64, 64:P], 64, gko[r, c, 0:64], gqo[r, c, 64:P]),
                    (b_[0:P, P:192], P, gko[r, c, 64:192], gqo[r, c, P:192]),
                    (b_[0:P, 192:T], P, gko[r, c, 192:320], gqo[r, c, 192:T]),
                    (b_[0:P, T:T + 64], P, gk[r, c, P:T], gq[r, c, P:192]),
                    (b_[64:P, T + 64:384], 64, gk[r, c, 192:T], gq[r, c, 192:T]),
                    (b_[0:64, T + 64:384], 64, gko[r, c, 320:384], gqo[r, c, 192:T]),
                ):
                    last = pe.matmul(o, kk, qq, start=True, stop=True)
                    first_of(last)
                last.then_inc(gla_A, 1)
            proj_transposed()
            pe.wait_ge(gla_Am, 4)
            pe.wait_ge(step_evac, 14)
            for h in range(4):
                v_ = slice(h * P, (h + 1) * P)
                first_of(pe.matmul(bank[4][:, v_], gA[:, h, 0:P], nw[:, 0, v_], start=True, stop=True))
                pe.matmul(bank[5][:, v_], gA[:, h, P:T], nw[:, 0, v_], start=True, stop=False)
                last = pe.matmul(bank[5][:, v_], gA[:, h, T:384], nw[:, 1, v_], start=False, stop=True)
            last.then_inc(gla_o, 1)
            for _ in range(3):
                proj_transposed()
            for _ in range(2):
                proj_natural()
            pe.wait_ge(step_evac, steps[0])
            pe.wait_ge(mask_ready, 1)
            pe.wait_ge(gla_done, 1)
            attention(0, tq, tk, nv, masked=True)
            pe.wait_ge(a_done, 2)
            transposes(u)
            out_projection()
            pe.wait_ge(x_ready, 1)
            transposes(x)
            ffn(0, 18)

            pe.wait_ge(x_ready, 2)
            transposes(x)
            narrow(152, 8)
            for _ in range(4):
                proj_transposed()
            for _ in range(2):
                proj_natural()
            pe.wait_ge(ls_b, 2)
            ps = step_bank()
            for t in range(TT):
                last = pe.matmul(ps[0:8, 0:T], lf[:, t * 8:(t + 1) * 8], cum[:, t, :], start=(t == 0), stop=(t == 1))
                if t == 0:
                    first_of(last)
            last.then_inc(step_done, 1)
            for _ in range(4):
                proj_transposed()
            for _ in range(2):
                proj_natural()
            pe.wait_ge(step_evac, steps[0])
            pe.wait_ge(late_in, 16)
            attention(1, tq, tk, nv, forget=True)
            attention(2, ta, tb, nw)
            pe.wait_ge(a_done, 6)
            transposes(u)
            out_projection()

            pe.wait_ge(x_ready, 3)
            transposes(x)
            pe.wait_ge(sums_evac, sums[0])
            narrow(160, 8)
            pe.wait_ge(route_ready, 1)
            ps = step_bank()
            pe.matmul(ps[:, 0:8], cum[:, 0, 0:P], chosen[:, 0:8], start=True, stop=True)
            pe.matmul(ps[:, 8:16], cum[:, 0, P:T], chosen[:, 0:8], start=True, stop=False)
            pe.matmul(ps[:, 8:16], cum[:, 1, P:T], chosen[:, 8:16], start=False, stop=True)
            pe.matmul(ps[0:1, 16:24], ones[:, 0:1], chosen[:, 0:8], start=True, stop=False)
            pe.matmul(ps[0:1, 16:24], ones[:, 0:1], chosen[:, 8:16], start=False, stop=True).then_inc(step_done, 1)

            def gather(n):
                pe.wait_ge(disp_ready, n)
                for k in range(KT):
                    for t in range(TT):
                        last = pe.matmul(bank[6 + k // 4][:, (k % 4) * P:(k % 4 + 1) * P], x[:, t, k * P:(k + 1) * P],
                                         disp[:, t, :], start=(t == 0), stop=(t == 1))
                        first_of(last)
                    if k % 4 == 3:
                        last.then_inc(xe_done, 1)

            def turn_dispatch(n):
                pe.wait_ge(xe_low, n * 2)
                for t in range(TT):
                    first_of(pe.transpose(bank[6][:, t * P:(t + 1) * P], disp[:, t, :], ident[:, :]))
                for t in range(TT):
                    last = pe.matmul(bank[7][:, 0:1], disp[:, t, :], cur[:, 4 + t:5 + t], start=(t == 0), stop=(t == 1))
                last.then_inc(pt_done, 1)

            pe.wait_ge(step_evac, steps[0])
            gather(1)
            turn_dispatch(1)
            pe.wait_ge(trip_ready, 1)
            trips = pe.value_load(trip_i[0:1, 0:1], min_val=NE, max_val=2 * NE)

            def expert_up(c, w, e, turn=None):
                h_, l_ = split_unit("cols")
                if w == 0:
                    if c >= 2:
                        pe.wait_ge(m_gate, e * NCH_M + (c - 1))
                for k in range(KT):
                    if k == 5 and turn is not None:
                        expert_turn(turn, e)
                    last = thirds(bank[c % 2][:, w * FC:(w + 1) * FC], (h_[:, k, :], l_[:, k, :]),
                                  (xTh[:, k, 0:P], xTl[:, k, 0:P]), k == 0, k == KT - 1, turned=True)
                if w == 1:
                    last.then_inc(m_up, 1)
                split_done()

            def expert_turn(c, e):
                pe.wait_ge(m_gate, e * NCH_M + (c + 1))
                if c >= 2:
                    pe.wait_ge(m_hT, e * NCH_M + (c - 1))
                for f in range(2):
                    last = pe.transpose(bank[2 + c % 2][:, f * P:(f + 1) * P], hn[:, c % 2, f * P:(f + 1) * P], ident[:, :])
                    first_of(last)
                last.then_inc(m_tr, 1)

            n_m = len(KINDS[0])

            def expert_down(c, e):
                at_ = [n for n, k in enumerate(expert_kinds()) if k == "r"][c]
                w, used = raw_unit(n_m + at_, e * (16 * L_BODY // UNITS))
                pe.wait_ge(m_hT, e * NCH_M + (c + 1))
                for f in range(2):
                    for n in range(2):
                        last = pe.matmul(bank[4 + n][:, :], hT[:, c % 2, f, 0:P], w[:, f, n * 512:(n + 1) * 512],
                                         start=(c == 0 and f == 0), stop=(c == NCH_M - 1 and f == 1))
                        first_of(last)
                last.then_inc(m_down, 1)
                freed.append(used)

            assert halves.i == C_ALL
            assert not freed
            with pe.Fori(0, trips) as e:
                halves.i = C_ALL
                halves.round(e * C_BODY, e * (L_BODY // UNITS))
                pe.wait_ge(xe_low, e * 2 + 2)
                for c in range(NCH_M):
                    expert_up(c, 0, e, c - 1 if c > 0 else None)
                    if c > 0:
                        expert_down(c - 1, e)
                    expert_up(c, 1, e)
                pe.wait_ge(pt_ready, e + 1)
                gather(e + 2)
                expert_turn(NCH_M - 1, e)
                expert_down(NCH_M - 1, e)
                pe.wait_ge(ye_ready, e + 1)
                for t in range(TT):
                    for n in range(2):
                        last = pe.matmul(bank[2 * t + n][:, :], dispT[:, t * P:(t + 1) * P], y[:, 0, n * 512:(n + 1) * 512],
                                         start=True, stop=True)
                        last.then_inc(sc_done, 1)
                turn_dispatch(e + 2)
                pe.wait_ge(sc_added, e * 4 + 4)
            pe.wait_ge(pt_ready, trips + 1)

            pe.wait_ge(x_ready, 5)
            transposes(u)
            pe.wait_ge(late_in, 80)
            for i in range(4):
                if i == 0:
                    ps = step_bank()
                last = pe.transpose(ps[:, i * 32:(i + 1) * 32], convw[:, i * P:(i + 1) * P], ident[0:32, 0:32])
            last.then_inc(step_done, 1)
            halves.i = C_ALL
            halves.round(trips * C_BODY, 0)
            for _ in range(2):
                proj_transposed()
            halves.second()
            for _ in range(6):
                proj_transposed()
            for _ in range(2):
                proj_natural()
            pe.wait_ge(step_evac, steps[0])
            attention(3, tq, tk, nv)
            pe.wait_ge(conv_done, 1)
            for t in range(TT):
                ps = step_bank()
                for c in range(4):
                    last = pe.transpose(ps[:, c * P:(c + 1) * P], ta[:, c, t * P:(t + 1) * P], ident[:, :])
                last.then_inc(step_done, 1)
            pe.wait_ge(a_done, 8)
            pe.wait_ge(conv_out, 2)
            transposes(u)
            out_projection()
            pe.wait_ge(x_ready, 6)
            transposes(u)
            ffn(1, 12)

        @block.scalar
        def _(act):
            steps = [0]
            trs = [0]
            chain = [0]

            def link(ins):
                chain[0] += 1
                ins.then_inc(a_chain, 1)
                act.wait_ge(a_chain, chain[0])

            def load(dst, src):
                act.dma_start(dst, src).then_inc(consts_in, 16)

            halves = Split()

            def upper(after=None, count=0):
                u_, loads, i, n = halves.place()
                s_ = halves.s
                act.wait_ge(landed[s_][u_], loads * 16)
                if after is not None:
                    act.wait_ge(after, count)
                elif not isinstance(n, int) or n >= 2:
                    act.wait_ge(split_used[s_], n - 1)
                act.activation(wh[:, i, :], ring[:, u_, :], ACT.Copy).then_inc(hi_ready[s_], 1)

            def copy_transposed():
                for g in range(4):
                    trs[0] += 1
                    act.wait_ge(tr_done, trs[0])
                    act.activation(xTh[:, 2 * g:2 * g + 2, :], bank[g].rearrange("p (k t) -> p k t", k=2),
                                   ACT.Copy).then_inc(tr_evac, 1)

            def step_out():
                j = steps[0]
                steps[0] += 1
                act.wait_ge(step_done, j + 1)
                return bank[6 + j % 2]

            def copy_step(dst, func=ACT.Copy, scale=1.0):
                act.activation(dst, step_out().rearrange("p (k t) -> p k t", k=2), func,
                               scale=scale).then_inc(step_evac, 1)

            def log_sigmoid_parts(ps, z, a):
                link(act.activation(z, ps, ACT.Copy))
                act.activation(a, z, ACT.Abs).then_inc(step_evac, 1)
                act.wait_ge(step_evac, steps[0])
                link(act.activation(a, a, ACT.Exp, scale=-1.0))
                act.activation(a, a, ACT.Ln, bias=1.0).then_inc(ls_a, 1)

            def attention(a):
                def exps(g):
                    t, hp, n = (g - 8 * a) // 4, (g - 8 * a) % 4, P * ((g - 8 * a) // 4 + 1)
                    act.wait_ge(a_max, g + 1)
                    if g >= 2:
                        act.wait_ge(a_tr, g - 1)
                    for hh in range(2):
                        col = (a % 2) * 16 + t * 8 + 2 * hp + hh
                        last = act.activation(pr[:, g % 2, hh * T:hh * T + n], lg[:, g % 2, hh * T:hh * T + n],
                                              ACT.Exp, bias=negmax[:, 2 * (g % 2) + hh:2 * (g % 2) + hh + 1],
                                              accum_out=rsum[:, col:col + 1])
                    last.then_inc(a_exp, 1)

                def copy(g):
                    t = (g - 8 * a) // 4
                    act.wait_ge(a_tr, g + 1)
                    if g >= 2:
                        act.wait_ge(a_pv, g - 1)
                    dst = pT[:, g % 2, :].rearrange("p (h s t) -> p h s t", h=2, s=2)[:, :, 0:t + 1, :]
                    src = bank[6 + g % 2].rearrange("p (h s t) -> p h s t", h=2, s=2)[:, :, 0:t + 1, :]
                    act.activation(dst, src, ACT.Copy).then_inc(a_pT, 1)

                if a >= 2:
                    act.wait_ge(a_done, 2 * (a - 1))
                for g in range(8 * a, 8 * a + 9):
                    if g < 8 * a + 8:
                        exps(g)
                    if g > 8 * a:
                        copy(g - 1)

            def silus(s, ft, shift=0, more=True):
                if more:
                    upper()
                for f in range(2):
                    act.wait_ge(up_done[s], ft + f + 1 + shift)
                    if ft + f >= 2:
                        act.wait_ge(h_ready[s], ft + f - 1 + shift)
                    act.activation(hs[:, (ft + f) % 2, :], bank[(ft + f) % 4][:, 0:T], ACT.Silu)\
                       .then_inc(silu_done[s], 1)
                if more:
                    upper()

            def ffn(s):
                silus(s, 0)
                silus(s, 2)
                i0 = halves.i
                with act.Fori(0, 4) as r:
                    halves.round(r * 4, r)
                    silus(s, 4, r * 4)
                    silus(s, 6, r * 4)
                halves.round(0, 0)
                halves.i = i0 + 16
                silus(s, 20, more=s == 0)

            load(cum[:, :, :], c_cum)
            load(causal[:, :], c_causal)
            load(iota[:, :], c_iota)
            load(onehot[:, :, :], c_onehot)
            load(rowadd[:, :, :], c_rowadd)
            load(rel[:, 0, :], rel_table)
            load(rel[:, 1, :], rel_bias_2)
            load(wgate[:, :], w_gate_a[0])
            load(bgate[:, :], b_gate_a)
            load(bforget[:, :], b_forget.rearrange("a n -> n a"))
            load(gnorm[:, :], g_norm_a.broadcast_to([P, P]))

            copy_transposed()
            act.wait_ge(small_in, 96)
            act.activation(wnh[:, :, :], wnraw[:, :, :], ACT.Copy).then_inc(narrow_hi, 1)
            upper()
            upper()
            act.activation(kiT[:, :], step_out()[:, 0:T], ACT.Copy).then_inc(step_evac, 1)
            act.activation(nt[:, :], step_out()[0:24, 0:T], ACT.Copy).then_inc(step_evac, 1)
            act.activation(wi[:, :, :], step_out()[:, 0:48].rearrange("p (t n) -> p t n", t=2)[:, :, 16:24], ACT.Copy)\
               .then_inc(step_evac, 1)
            copy_step(ta[:, 0:2, :])
            upper()
            copy_step(ta[:, 2:4, :])
            upper()
            log_sigmoid_parts(step_out().rearrange("p (t n) -> p t n", t=2), gz[:, :, :], ga_[:, :, :])
            for i in range(3):
                act.activation(relrow[:, i, :], step_out()[0:8, 0:REL], ACT.Copy).then_inc(step_evac, 1)
            for i in range(8):
                t, n = i // 4, P * (i // 4 + 1)
                act.wait_ge(idx_scores, i + 1)
                if i >= 2:
                    act.wait_ge(idx_acc, i - 1)
                act.activation(lg[:, i % 2, :].rearrange("p (h s) -> p h s", h=2)[:, :, 0:n],
                               pair_banks(i, n), ACT.Relu)\
                   .then_inc(idx_relu, 1)
            copy_step(tb[:, 0:2, :], scale=HD ** -0.5)
            upper()
            copy_step(tb[:, 2:4, :])
            upper()
            copy_step(gT[:, :, :], scale=1.0 / 16.0)
            act.wait_ge(step_evac, steps[0])
            act.wait_ge(gla_neg, 1)
            for c in range(2):
                for j in range(4):
                    s_ = slice(64 * j, 64 * j + 64)
                    mid = 64 * j + 31
                    act.activation(gq[:, c, s_], gT[:, c, s_], ACT.Exp, bias=ngc[:, c, j:j + 1])
                    last = act.activation(gk[:, c, s_], gT[:, c, s_], ACT.Exp, bias=gT[:, c, mid:mid + 1], scale=-1.0)
                    if j > 0:
                        b_ = 64 * j - 1
                        act.activation(gqo[:, c, s_], gT[:, c, s_], ACT.Exp, bias=ngc[:, c, 3 + j:4 + j])
                        o = 64 * (j * (j - 1) // 2)
                        last = act.activation(gko[:, c, o:o + 64 * j], gT[:, c, 0:64 * j], ACT.Exp,
                                              bias=gT[:, c, b_:b_ + 1], scale=-1.0)
                last.then_inc(gla_exp, 1)
                copy_step(nw[:, :, c * 256:(c + 1) * 256])
                upper()
            for c in range(2):
                copy_step(nr[:, :, c * 256:(c + 1) * 256], ACT.Silu)
                upper()
            copy_step(tq[:, 0:2, :], scale=HD ** -0.5)
            upper()
            act.wait_ge(gla_o, 1)
            for t in range(TT):
                act.activation(y[:, t, 0:512], bank[4 + t][:, :], ACT.Square).then_inc(gla_sq, 1)
            copy_step(tq[:, 2:4, :], scale=HD ** -0.5)
            upper()
            for dst in (tk[:, 0:2, :], tk[:, 2:4, :], nv[:, :, 0:256], nv[:, :, 256:512]):
                copy_step(dst)
                upper()
            attention(0)
            copy_transposed()
            upper()
            upper()
            upper()
            upper(sums_done, 1)
            copy_transposed()
            ffn(0)

            copy_transposed()
            act.wait_ge(consts_in, CONSTS)
            act.activation(nt[0:8, :], step_out()[0:8, 0:T], ACT.Identity, bias=bforget[:, 0:1]).then_inc(step_evac, 1)
            log_sigmoid_parts(step_out()[:, 0:16], flz, fla)
            for q, k, v in ((tq, tk, nv), (ta, tb, nw)):
                for i in range(2):
                    copy_step(q[:, 2 * i:2 * i + 2, :], scale=HD ** -0.5)
                    upper()
                for dst in (k[:, 0:2, :], k[:, 2:4, :], v[:, :, 0:256], v[:, :, 256:512]):
                    copy_step(dst)
                    upper()
                if q is tq:
                    act.activation(nfT, step_out()[0:8, 0:T], ACT.Copy, scale=-1.0).then_inc(step_evac, 1)
            attention(1)
            attention(2)
            copy_transposed()
            upper()
            upper()
            upper()
            upper(sums_done, 2)
            copy_transposed()
            act.activation(nt[0:8, :], step_out()[0:8, 0:T], ACT.Copy).then_inc(step_evac, 1)
            act.activation(rl, step_out()[:, 0:16], ACT.Copy).then_inc(step_evac, 1)
            act.wait_ge(gate_ask, 1)
            act.activation(e2[:, 2:4], e2[:, 0:2], ACT.Exp).then_inc(gate_got, 1)
            ps = step_out()
            link(act.activation(slot, ps[:, 0:16], ACT.Copy))
            act.activation(oh2[0:1, 0:8], ps[0:1, 16:24], ACT.Copy).then_inc(step_evac, 1)

            def gathered(n):
                for i in range(2):
                    act.wait_ge(xe_done, n * 2 + (i - 1))
                    act.activation(xTh[:, 4 * i:4 * i + 4, 0:P], bank[6 + i].rearrange("p (k t) -> p k t", k=4),
                                   ACT.Copy).then_inc(xe_ready, 1)

            def turned(n):
                act.wait_ge(pt_done, n)
                act.activation(dispT[:, :], bank[6][:, 0:T], ACT.Copy)
                act.activation(slotg[:, :], bank[7][:, 0:1], ACT.Copy).then_inc(pt_ready, 1)

            gathered(1)
            turned(1)
            act.wait_ge(trip_ready, 1)
            trips = act.value_load(trip_i[0:1, 0:1], min_val=NE, max_val=2 * NE)

            def expert_silu(c, e):
                act.wait_ge(m_up, e * NCH_M + (c + 1))
                if c >= 2:
                    act.wait_ge(m_gate, e * NCH_M + (c - 1))
                act.activation(hs[:, c % 2, :], bank[c % 2][:, 0:FC], ACT.Silu).then_inc(m_silu, 1)

            def expert_copy(c, e):
                act.wait_ge(m_tr, e * NCH_M + (c + 1))
                if c >= 2:
                    act.wait_ge(m_down, e * NCH_M + (c - 1))
                act.activation(hT[:, c % 2, :, 0:P], bank[2 + c % 2][:, 0:FC].rearrange("p (f t) -> p f t", f=2),
                               ACT.Copy).then_inc(m_hT, 1)

            assert halves.i == C_ALL + 2
            with act.Fori(0, trips) as e:
                halves.i = C_ALL + 2
                halves.round(e * C_BODY, e * (L_BODY // UNITS))
                upper()
                for c in range(NCH_M - 1):
                    expert_silu(c, e)
                    upper()
                    expert_copy(c, e)
                    upper()
                expert_silu(NCH_M - 1, e)
                upper()
                gathered(e + 2)
                expert_copy(NCH_M - 1, e)
                turned(e + 2)
            halves.second()

            def squares(sem_, value):
                act.wait_ge(sem_, value)
                for t in range(TT):
                    act.activation(y[:, t, :], x[:, t, :], ACT.Square, accum_out=ms[:, t:t + 1]).then_inc(rms_sq, 1)

            squares(x_ready, 4)
            copy_transposed()
            act.activation(cw[:, :, :], step_out()[:, 0:P].rearrange("p (c j) -> p c j", c=4), ACT.Copy)\
               .then_inc(step_evac, 1)
            used_up = trips * C_BODY + (C_ALL + 1)
            copy_step(ta[:, 0:2, :])
            upper(split_used[0], used_up)
            copy_step(ta[:, 2:4, :])
            upper(split_used[0], used_up + 1)
            copy_step(tb[:, 0:2, :], ACT.Sigmoid)
            upper()
            copy_step(tb[:, 2:4, :], ACT.Sigmoid)
            act.wait_ge(step_evac, steps[0])
            act.nop().then_inc(conv_in, 1)
            upper()
            for i in range(2):
                copy_step(tq[:, 2 * i:2 * i + 2, :], scale=HD ** -0.5)
                upper()
            for dst in (tk[:, 0:2, :], tk[:, 2:4, :], nv[:, :, 0:256], nv[:, :, 256:512]):
                copy_step(dst)
                upper()
            attention(3)
            for t in range(TT):
                act.activation(nr[:, t, :], step_out()[:, :], ACT.Copy).then_inc(step_evac, 1)
            for t in range(TT):
                act.wait_ge(conv_n, t + 1)
                act.activation(u[:, t, 512:1024], nr[:, t, :], ACT.Silu).then_inc(conv_out, 1)
            copy_transposed()
            upper()
            upper()
            upper()
            upper(sums_done, 3)
            squares(x2_ready, 1)
            copy_transposed()
            ffn(1)
            squares(x2_ready, 2)

        @block.vector
        def _(dve):
            chain = [0]
            norms = [0]

            def link(ins):
                chain[0] += 1
                ins.then_inc(v_chain, 1)
                dve.wait_ge(v_chain, chain[0])

            norms_asked = [0]

            def ask(ins):
                ins.then_inc(rs_ask, 1)
                norms_asked[0] += 1
                dve.wait_ge(rs_got, norms_asked[0])

            def norm_weights(n):
                dve.wait_ge(ln_in, LN_AT[n])

            halves = Split()

            def lower():
                u_, _, i, n = halves.place()
                s_ = halves.s
                dve.wait_ge(hi_ready[s_], n + 1)
                dve.tensor_tensor(wl[:, i, :], ring[:, u_, :], wh[:, i, :].bitcast(F32), ALU.subtract)\
                   .then_inc(taken[s_][u_], 1)

            trs = [0]

            def lower_transposed():
                for g in range(4):
                    trs[0] += 1
                    dve.wait_ge(tr_evac, trs[0])
                    k = slice(2 * g, 2 * g + 2)
                    dve.tensor_tensor(xTl[:, k, :], bank[g].rearrange("p (k t) -> p k t", k=2),
                                      xTh[:, k, :].bitcast(F32), ALU.subtract).then_inc(tr_low, 1)

            def add_residual(dst, alpha, done, n):
                dve.wait_ge(done, n)
                for t in range(TT):
                    for n in range(2):
                        s_ = slice(n * 512, (n + 1) * 512)
                        last = dve.scalar_tensor_tensor(dst[:, t, s_], x[:, t, s_], alpha, bank[4 + 2 * t + n][:, :],
                                                        ALU.mult, ALU.add)
                link(last)
                dve.nop().then_inc(sums_evac, 1)

            def moments(src, tiles, width):
                for t in tiles:
                    for j in range(width // 512):
                        last = dve.bn_stats(stat[:, t * 12 + 6 * j:t * 12 + 6 * j + 6], src(t)[:, j * 512:(j + 1) * 512])
                    link(last)
                    link(dve.bn_aggr(mv[:, 2 * t:2 * t + 2], stat[:, t * 12:t * 12 + 6 * (width // 512)]))
                ask(dve.tensor_scalar(e2[:, 0:2], mv[:, 1:4:2], LN_EPS, None, ALU.add))

            def layer_norm(src):
                n = norms[0]
                norms[0] += 1
                moments(lambda t: src[:, t, :], range(TT), D)
                norm_weights(n)
                w = lnw
                for t in range(TT):
                    link(dve.scalar_tensor_tensor(src[:, t, :], src[:, t, :], mv[:, 2 * t:2 * t + 1], w[:, 0, :],
                                                  ALU.subtract, ALU.mult))
                for t in range(TT):
                    last = dve.scalar_tensor_tensor(x[:, t, :], src[:, t, :], rstd[:, t:t + 1], w[:, 1, :],
                                                    ALU.mult, ALU.add)
                last.then_inc(x_ready, 1)
                dve.wait_ge(x_ready, norms[0])

            def rms_norm(dst, n_sq, signal):
                n = norms[0]
                norms[0] += 1
                dve.wait_ge(rms_sq, 2 * n_sq + 2)
                ask(dve.tensor_scalar(e2[:, 0:2], ms[:, 0:2], 1.0 / D, RMS_EPS, ALU.mult, ALU.add))
                norm_weights(n)
                w = lnw[:, 0, :] if n_sq > 0 else mixg
                for t in range(TT):
                    last = dve.scalar_tensor_tensor(dst[:, t, :], x[:, t, :], rstd[:, t:t + 1], w,
                                                    ALU.mult, ALU.mult)
                    if signal is fin:
                        last.then_inc(fin, 1)
                if signal is not fin:
                    last.then_inc(signal, 1)

            def pairs(ap, n):
                return ap.rearrange("p (h s) -> p h s", h=2)[:, :, 0:n]

            def attention(a, add, v_off):
                for g in range(8 * a, 8 * a + 8):
                    t, hp, n = (g - 8 * a) // 4, (g - 8 * a) % 4, P * ((g - 8 * a) // 4 + 1)
                    dve.wait_ge(a_scores, g + 1)
                    if g >= 2:
                        dve.wait_ge(a_exp, g - 1)
                    link(dve.tensor_tensor(pairs(lg[:, g % 2, :], n), pair_banks(g, n),
                                           add(hp, T - n), ALU.add))
                    dve.tensor_reduce(negmax[:, 2 * (g % 2):2 * (g % 2) + 2], pairs(lg[:, g % 2, :], n),
                                      AX.X, ALU.max, negate=True).then_inc(a_max, 1)
                for t in range(TT):
                    dve.wait_ge(a_pv, 8 * a + 4 * (t + 1))
                    r0 = (a % 2) * 16 + t * 8
                    link(dve.reciprocal(rinv[:, t * 8:t * 8 + 8], rsum[:, r0:r0 + 8]))
                    dve.tensor_tensor(u[:, t, v_off:v_off + 512].rearrange("p (h d) -> p h d", h=8),
                                      bank[4 + t].rearrange("p (h d) -> p h d", h=8),
                                      rinv[:, t * 8:t * 8 + 8].unsqueeze(2).broadcast_to([P, 8, HD]),
                                      ALU.mult).then_inc(a_done, 1)

            def relative():
                return lambda hp, lo: bias[:, 2 * hp:2 * hp + 2, lo:T]

            def gates(s, ft, shift=0, more=True):
                if more:
                    lower()
                c = ft // 2
                for f in range(2):
                    dve.wait_ge(silu_done[s], ft + f + 1 + shift)
                    if c >= 2 and f == 0:
                        dve.wait_ge(down_done[s], c - 1 + shift_half[0])
                    dve.tensor_tensor(hT[:, c % 2, f, :], hs[:, (ft + f) % 2, :], bank[(ft + f) % 4][:, T:2 * T],
                                      ALU.mult).then_inc(h_ready[s], 1)
                if more:
                    lower()

            shift_half = [0]

            def ffn(s):
                gates(s, 0)
                gates(s, 2)
                i0 = halves.i
                with dve.Fori(0, 4) as r:
                    shift_half[0] = r * 2
                    halves.round(r * 4, r)
                    gates(s, 4, r * 4)
                    gates(s, 6, r * 4)
                shift_half[0] = 0
                halves.round(0, 0)
                halves.i = i0 + 16
                gates(s, 20, more=s == 0)

            dve.memset(ones[:, :], 1.0).then_inc(filled, 1)
            dve.memset(half[:, :], -0.5).then_inc(filled, 1)
            dve.memset(table[:, :, :], 0.0).then_inc(filled, 1)

            def log_sigmoid(z, a, dst, n):
                dve.wait_ge(ls_a, n)
                dve.scalar_tensor_tensor(dst, z, 0.0, a, ALU.min, ALU.subtract).then_inc(ls_b, 1)

            lower_transposed()
            dve.wait_ge(narrow_hi, 1)
            dve.tensor_tensor(wnl[:, :, :], wnraw[:, :, :], wnh[:, :, :].bitcast(F32), ALU.subtract).then_inc(narrow_lo, 1)
            for _ in range(4):
                lower()
            log_sigmoid(gz[:, :, :], ga_[:, :, :], gnat[:, :, :], 1)
            for i in range(8):
                t, hp, n = i // 4, i % 4, P * (i // 4 + 1)
                dve.wait_ge(idx_relu, i + 1)
                for hh in range(2):
                    r = lg[:, i % 2, hh * T:hh * T + n]
                    w = wi[:, t, 2 * hp + hh:2 * hp + hh + 1]
                    if hp == 0 and hh == 0:
                        last = dve.tensor_scalar(score[:, t, 0:n], r, w, None, ALU.mult)
                    else:
                        last = dve.scalar_tensor_tensor(score[:, t, 0:n], r, w, score[:, t, 0:n], ALU.mult, ALU.add)
                    link(last)
                dve.nop().then_inc(idx_acc, 1)
            def top_keys(t, first, final):
                n = P * (t + 1)
                if first == 0:
                    link(dve.tensor_tensor(score[:, t, 0:n], score[:, t, 0:n], causal[:, T - n:T], ALU.add))
                for _ in range(first, final):
                    link(dve.max(top8, score[:, t, 0:n]))
                    link(dve.match_replace(score[:, t, 0:n], top8, score[:, t, 0:n], TAKEN))
                if final == TOPK // 8:
                    link(dve.tensor_scalar(score[:, t, 0:n], score[:, t, 0:n], 10.0 * NEG * 1e7, NEG, ALU.is_gt, ALU.mult))

            lower()
            top_keys(0, 0, 8)
            lower()
            dve.wait_ge(step_evac, 12)
            for c in range(2):
                dve.tensor_scalar(ngc[:, c, 0:4], gT[:, c, 31:T:64], -1.0, None, ALU.mult)
                last = dve.tensor_scalar(ngc[:, c, 4:7], gT[:, c, 63:T - 64:64], -1.0, None, ALU.mult)
            last.then_inc(gla_neg, 1)
            top_keys(1, 0, 4)
            lower()
            top_keys(1, 4, 8)
            dve.nop().then_inc(mask_ready, 1)
            lower()
            dve.wait_ge(gla_exp, 2)
            dve.wait_ge(step_evac, 12)
            dve.tensor_tensor(gq[:, :, :], gq[:, :, :], tb[:, 0:2, :], ALU.mult)
            dve.tensor_tensor(gk[:, :, :], gk[:, :, :], tb[:, 2:4, :], ALU.mult)
            dve.tensor_tensor(gqo[:, :, 64:T], gqo[:, :, 64:T], tb[:, 0:2, 64:T], ALU.mult)
            for j in (1, 2, 3):
                o = 64 * (j * (j - 1) // 2)
                last = dve.tensor_tensor(gko[:, :, o:o + 64 * j], gko[:, :, o:o + 64 * j], tb[:, 2:4, 0:64 * j], ALU.mult)
            last.then_inc(gla_ops, 1)
            lower()
            for h in range(4):
                dve.wait_ge(gla_A, h + 1)
                dve.tensor_tensor(gA[:, h, 0:T], bank[h][:, 0:T], cum[:, 0, :], ALU.mult)
                dve.tensor_tensor(gA[:, h, T:384], bank[h][:, T:384], cum[:, 1, P:T], ALU.mult).then_inc(gla_Am, 1)
            lower()
            dve.wait_ge(step_evac, 16)
            for t in range(TT):
                v4 = nr[:, t, :].rearrange("p (h d) -> p h d", h=4)
                link(dve.tensor_tensor(v4, v4, gnorm[:, :].unsqueeze(1).broadcast_to([P, 4, P]), ALU.mult))
            lower()
            for t in range(TT):
                dve.wait_ge(gla_sq, t + 1)
                link(dve.tensor_reduce(ms[:, 4 * t:4 * t + 4], y[:, t, 0:512].rearrange("p (h d) -> p h d", h=4),
                                       AX.X, ALU.add))
            lower()
            ask(dve.tensor_scalar(e2[:, 0:8], ms[:, 0:8], 1.0 / P, LN_EPS, ALU.mult, ALU.add))
            dve.wait_ge(rel_out, 48)
            for t in range(TT):
                v4 = nr[:, t, :].rearrange("p (h d) -> p h d", h=4)
                link(dve.tensor_tensor(v4, v4, rstd8[:, 4 * t:4 * t + 4].unsqueeze(2).broadcast_to([P, 4, P]), ALU.mult))
                last = dve.tensor_tensor(u[:, t, 0:512], nr[:, t, :], bank[4 + t][:, :], ALU.mult)
            last.then_inc(gla_done, 1)
            for _ in range(4):
                lower()
            dve.wait_ge(rel_in[0], 16)
            attention(0, relative(), 512)
            lower_transposed()
            for _ in range(3):
                lower()
            add_residual(y, ALPHA, sums_done, 1)
            layer_norm(y)
            lower()
            lower_transposed()
            ffn(0)
            add_residual(y, ALPHA, down_done[0], F_DENSE // FC)
            layer_norm(y)

            lower_transposed()
            for _ in range(2):
                lower()
            log_sigmoid(flz, fla, lf, 2)
            for _ in range(10):
                lower()
            attention(1, lambda hp, lo: causal[:, lo:T].unsqueeze(1).broadcast_to([P, 2, T - lo]), 0)
            dve.wait_ge(rel_in[1], 16)
            attention(2, relative(), 512)
            lower_transposed()
            for _ in range(3):
                lower()
            add_residual(y, ALPHA, sums_done, 2)
            layer_norm(y)
            lower()

            lower_transposed()
            dve.wait_ge(step_evac, STEPS_ROUTER)
            for t in range(TT):
                s8 = slice(8 * t, 8 * t + 8)
                link(dve.max(top8, rl[:, s8]))
                link(dve.max_index(topi[:, :], top8, rl[:, s8]))
                link(dve.tensor_copy(topf, topi[:, :]))
                link(dve.tensor_scalar(e2[:, t:t + 1], top8[:, 1:2], top8[:, 0:1], None, ALU.subtract))
                link(dve.tensor_scalar(chosen[:, s8], iota[:, 0:8], topf[:, 0:1], None, ALU.is_equal))
                link(dve.tensor_scalar(oh2[:, s8], iota[:, 0:8], topf[:, 1:2], None, ALU.is_equal))
            dve.nop().then_inc(gate_ask, 1)
            dve.wait_ge(gate_got, 1)
            link(dve.tensor_scalar(ms[:, 0:2], e2[:, 2:4], 1.0, None, ALU.add))
            link(dve.reciprocal(ms[:, 2:4], ms[:, 0:2]))
            link(dve.tensor_tensor(ms[:, 4:6], e2[:, 2:4], ms[:, 2:4], ALU.mult))
            for t in range(TT):
                s8 = slice(8 * t, 8 * t + 8)
                link(dve.tensor_scalar(comb[:, s8], chosen[:, s8], ms[:, 2 + t:3 + t], None, ALU.mult))
                link(dve.scalar_tensor_tensor(comb[:, s8], oh2[:, s8], ms[:, 4 + t:5 + t], comb[:, s8], ALU.mult, ALU.add))
                link(dve.tensor_tensor(chosen[:, s8], chosen[:, s8], oh2[:, s8], ALU.add))
            for t in range(TT):
                for r in range(2):
                    e_ = slice(r * 8, r * 8 + 8)
                    s8 = slice(8 * t, 8 * t + 8)
                    dve.tensor_copy(table[:, e_, 2 + t], chosen[:, s8])
                    link(dve.tensor_copy(table[:, e_, 4 + t], comb[:, s8]))
            dve.nop().then_inc(route_ready, 1)
            dve.wait_ge(step_evac, STEPS_ROUTER + 1)
            for t in range(TT):
                for r in range(2):
                    link(dve.tensor_scalar(table[:, r * 8:r * 8 + 8, t], slot[:, 8 * t:8 * t + 8], -1.0 - P * r, None, ALU.add))
            link(dve.tensor_reduce(trip_f[0:1, 0:1], oh2[0:1, 0:8], AX.X, ALU.max))
            link(dve.tensor_scalar(trip_f[0:1, 1:2], trip_f[0:1, 0:1], P + 0.5, float(NE), ALU.is_gt, ALU.mult))
            dve.tensor_scalar(trip_i[:, :], trip_f[0:1, 1:2], float(NE), None, ALU.add).then_inc(trip_ready, 1)
            for t in range(TT):
                link(dve.tensor_scalar(u[:, t, :], x[:, t, :], ALPHA, None, ALU.mult))

            def dispatch(e):
                dve.tensor_copy(cur[:, :], table[:, bass.ds(e, 1), :].rearrange("p a n -> p (a n)")).then_inc(cur_ready, 1)
                dve.wait_ge(cur_ready, e + 1)
                for t in range(TT):
                    last = dve.tensor_scalar(disp[:, t, :], iota[:, :], cur[:, t:t + 1], cur[:, 2 + t:3 + t],
                                             ALU.is_equal, ALU.mult)
                last.then_inc(disp_ready, 1)

            def lower_gathered(n):
                for i in range(2):
                    dve.wait_ge(xe_ready, n * 2 + (i - 1))
                    k = slice(4 * i, 4 * i + 4)
                    dve.tensor_tensor(xTl[:, k, 0:P], bank[6 + i].rearrange("p (k t) -> p k t", k=4),
                                      xTh[:, k, 0:P].bitcast(F32), ALU.subtract).then_inc(xe_low, 1)

            def expert_gate(c, e):
                dve.wait_ge(m_silu, e * NCH_M + (c + 1))
                if c >= 2:
                    dve.wait_ge(m_tr, e * NCH_M + (c - 1))
                dve.tensor_tensor(hn[:, c % 2, :], hs[:, c % 2, :], bank[c % 2][:, FC:2 * FC], ALU.mult)\
                   .then_inc(m_gate, 1)

            dispatch(0)
            lower_gathered(1)
            dve.wait_ge(trip_ready, 1)
            trips = dve.value_load(trip_i[0:1, 0:1], min_val=NE, max_val=2 * NE)
            with dve.Fori(0, trips) as e:
                halves.i = C_ALL + 2
                halves.round(e * C_BODY, e * (L_BODY // UNITS))
                lower()
                for c in range(NCH_M - 1):
                    expert_gate(c, e)
                    lower()
                    if c == 1:
                        dve.wait_ge(pt_done, e + 1)
                        dispatch(e + 1)
                    lower()
                expert_gate(NCH_M - 1, e)
                lower()
                lower_gathered(e + 2)
                dve.wait_ge(m_down, e * NCH_M + NCH_M)
                dve.tensor_scalar(y[:, 0, 0:512], bank[4][:, :], slotg[:, 0:1], None, ALU.mult)
                dve.tensor_scalar(y[:, 0, 512:1024], bank[5][:, :], slotg[:, 0:1], None, ALU.mult).then_inc(ye_ready, 1)
                for t in range(TT):
                    for n in range(2):
                        dve.wait_ge(sc_done, e * 4 + (2 * t + n + 1))
                        s_ = u[:, t, n * 512:(n + 1) * 512]
                        dve.tensor_tensor(s_, s_, bank[2 * t + n][:, :], ALU.add).then_inc(sc_added, 1)
            halves.second()
            dve.wait_ge(sc_added, trips * 4)
            layer_norm(u)

            rms_norm(u, 0, x_ready)
            upad = gA[:, :, 0:CONV - 1 + T]
            dve.memset(upad[:, :, 0:CONV - 1], 0.0)
            lower_transposed()
            for _ in range(3):
                lower()
            dve.wait_ge(conv_in, 1)
            link(dve.tensor_tensor(upad[:, :, CONV - 1:], ta[:, :, :], tb[:, :, :], ALU.mult))
            for j in range(CONV):
                for c in range(4):
                    if j == 0:
                        last = dve.tensor_scalar(ta[:, c, :], upad[:, c, 0:T], cw[:, c, 0:1], cw[:, c, 31:32], ALU.mult, ALU.add)
                    else:
                        last = dve.scalar_tensor_tensor(ta[:, c, :], upad[:, c, j:j + T], cw[:, c, j:j + 1], ta[:, c, :],
                                                        ALU.mult, ALU.add)
                link(last)
                if j % 3 == 2 and j < 21:
                    lower()
            dve.nop().then_inc(conv_done, 1)
            dve.wait_ge(rel_in[2], 16)
            attention(3, relative(), 0)
            dve.wait_ge(step_evac, STEPS_CONV)
            dve.wait_ge(late_in, 80)
            moments(lambda t: nr[:, t, :], range(TT), 512)
            for t in range(TT):
                link(dve.scalar_tensor_tensor(nr[:, t, :], nr[:, t, :], mv[:, 2 * t:2 * t + 1], convg,
                                              ALU.subtract, ALU.mult))
                dve.scalar_tensor_tensor(nr[:, t, :], nr[:, t, :], rstd[:, t:t + 1], convb,
                                         ALU.mult, ALU.add).then_inc(conv_n, 1)
            lower_transposed()
            for _ in range(3):
                lower()
            add_residual(x, 1.0, sums_done, 3)
            dve.nop().then_inc(x2_ready, 1)
            rms_norm(u, 1, x_ready)
            lower()
            lower_transposed()
            ffn(1)
            add_residual(x, 1.0, down_done[1], F_DENSE // FC)
            dve.nop().then_inc(x2_ready, 1)
            rms_norm(u, 2, fin)

        @block.gpsimd
        def _(pool):
            def weights(n, rows):
                if n >= 1:
                    pool.wait_ge(x_ready, n)
                for i, r in enumerate(rows):
                    pool.dma_start(lnw[:, i, :], r.broadcast_to([P, D])).then_inc(ln_in, 16)

            def bias_table(i):
                src = bass.AP(rel_dram.tensor, i * P * H * REL + P - 1, [[H * REL - 1, P], [REL, H], [1, T]])
                pool.dma_start(bias[:, :, :], src).then_inc(rel_in[i], 16)

            def rstd_of(n):
                asked[0] += 1
                pool.wait_ge(rs_ask, asked[0])
                pool.tensor_tensor(rstd8[:, 0:n], e2[:, 0:n], half[:, 0:n], ALU.pow).then_inc(rs_got, 1)

            asked = [0]
            weights(0, (ln_g[0, 0:1, :], ln_b[0, 0:1, :]))
            for i in range(3):
                pool.wait_ge(step_evac, 7 + i)
                pool.dma_start(rel_dram[i].rearrange("t h j -> h t j"),
                               relrow[:, i, :].unsqueeze(1).broadcast_to([H, P, REL])).then_inc(rel_out, 16)
            pool.wait_ge(rel_out, 48)
            bias_table(0)
            pool.wait_ge(filled, 3)
            rstd_of(8)
            pool.wait_ge(a_done, 2)
            bias_table(1)
            rstd_of(2)
            weights(1, (ln_g[0, 1:2, :], ln_b[0, 1:2, :]))
            pool.dma_start(rowsel[:, :, :], c_rowsel).then_inc(late_in, 16)
            rstd_of(2)
            weights(2, (ln_g[1, 0:1, :], ln_b[1, 0:1, :]))
            pool.wait_ge(a_done, 6)
            bias_table(2)
            pool.wait_ge(late_in, 16)
            pool.dma_start(convw[0:31, :], conv_w_2[0]).then_inc(late_in, 16)
            pool.dma_start(convw[31:32, :], conv_b_2).then_inc(late_in, 16)
            pool.dma_start(convg[:, :], conv_ln_g_2.broadcast_to([P, 512])).then_inc(late_in, 16)
            pool.dma_start(convb[:, :], conv_ln_b_2.broadcast_to([P, 512])).then_inc(late_in, 16)
            rstd_of(2)
            weights(3, (ln_g[1, 1:2, :], ln_b[1, 1:2, :]))
            pool.dma_start(mixg, mix_norm_g_2.broadcast_to([P, D])).then_inc(ln_in, 16)
            rstd_of(2)
            rstd_of(2)
            weights(5, (ffn_norm_g_2,))
            rstd_of(2)
            rstd_of(2)
            weights(6, (final_norm_g_2.rearrange("(a d) -> a d", a=1),))
            rstd_of(2)


def constants():
    import numpy as np

    t = np.arange(T)
    cum = (t[:, None] <= t[None, :]).astype(np.float32).reshape(TT, P, T).transpose(1, 0, 2)
    dist = np.arange(255, 255 - REL, -1)

    def bucket(furthest):
        d = np.maximum(dist, 1).astype(np.float32)
        far = 16 + (np.log(d / np.float32(16)) / np.float32(np.log(furthest / 16)) * np.float32(16)).astype(np.int32)
        return np.where(dist < 16, np.maximum(dist, 0), np.minimum(far, 31))

    onehot = np.stack([(bucket(f)[None, :] == np.arange(32)[:, None]) for f in (2048, 128)], 1).astype(np.float32)
    times = (dist <= 128).astype(int) + (dist % 4 == 0) + (dist % 16 == 0)
    past = dist >= 0
    plain = np.where(past, 0.0, NEG)
    dilated = np.where(past & (times > 0), np.log(np.maximum(times, 1)), NEG)
    rowadd = np.stack([plain, dilated, plain])[None].astype(np.float32)
    rowsel = np.zeros((8, 8, P), np.float32)
    for h in range(8):
        rowsel[h, h] = 1
    q = P + np.arange(P)
    return {
        "c_ident": np.eye(P, dtype=np.float32),
        "c_cum": np.ascontiguousarray(cum),
        "c_causal": np.where(t[None, :] <= q[:, None], 0.0, NEG).astype(np.float32),
        "c_iota": np.broadcast_to(np.arange(P, dtype=np.float32), (P, P)).copy(),
        "c_onehot": onehot,
        "c_rowadd": rowadd,
        "c_rowsel": rowsel,
    }


INS = ["x", "ln_g", "ln_b", "rel_table", "w_in_ab", "w_gate_a", "b_gate_a", "g_norm_a", "w_out_ab", "w_in_cd",
       "b_forget", "w_out_cd", "w1_dense", "w3_dense", "w2_dense", "w_router", "w1_moe", "w3_moe", "w2_moe",
       "mix_norm_g_2", "w_in_2", "rel_bias_2", "conv_w_2", "conv_b_2", "conv_ln_g_2", "conv_ln_b_2", "w_out_2",
       "ffn_norm_g_2", "w_gate_2", "w_up_2", "w_down_2", "final_norm_g_2"]


def kernel(**inputs):
    import numpy as np
    import concourse.bacc as bacc
    from concourse.bass_utils import run_bass_kernel_spmd

    nc = bacc.Bacc("TRN2", target_bir_lowering=False, num_devices=1)
    arrays, args = {}, []
    for name, a in [(n, np.ascontiguousarray(inputs[n])) for n in INS] + list(constants().items()):
        arrays[f"in_{name}"] = a
        args.append(nc.dram_tensor(f"in_{name}", a.shape, mybir.dt.from_np(a.dtype), kind="ExternalInput").ap())
    args.append(nc.dram_tensor("out_0", (1, T, D), F32, kind="ExternalOutput").ap())
    build(nc, *args)
    r = run_bass_kernel_spmd(nc, [arrays], core_ids=[0])
    return r.results[0]["out_0"]
```

```python
import concourse.bass as bass
from concourse import mybir
from contextlib import ExitStack

F32 = mybir.dt.float32
F32R = mybir.dt.float32r
I32 = mybir.dt.int32
U32 = mybir.dt.uint32
ALU = mybir.AluOpType
ACT = mybir.ActivationFunctionType
AX = mybir.AxisListType

P = 128
T = 256
TT = T // P
D = 1024
KT = D // P
H = 8
HD = 64
TOPK = 64
F_DENSE = 2816
F_MOE = 3584
FC = 256
NE = 8
UNITS = 6
UW = 2048
ALPHA = 4.0 ** 0.25
NEG = -1e30
TAKEN = -3e38
REL = 384
CONV = 31
LN_EPS = 1e-5
RMS_EPS = 1e-6
LN_AT = [32, 64, 96, 144, 144, 160, 176]
STEPS_ROUTER = 39
STEPS_CONV = 53
CONSTS = 16 * 11
NARROW = 168
NCH_D = F_DENSE // FC
NCH_M = F_MOE // FC
L_BODY = 3 * NCH_M
PIECES = 2 * L_BODY


LENGTHS = [18 + 3 * NCH_D + 16, 12 + 3 * NCH_D]

def silu_at(c):
    return 6 * c + 5 if c > 0 else 7


def copy_at(c):
    return (6 * c + 9 if c < NCH_M - 1 else PIECES) if c > 0 else 10


ADDED_AT = [8, 8, 9, 9]
TURNED_AT = 10
GATHERED_AT = PIECES


AB = dict(qa=0, ka=256, va=512, ra=1024, ga=1536, qb=1552, kb=2064, vb=2576, qi=3088, ki=3600, wi=3664)
CD = dict(qc=0, kc=512, vc=1024, fc=1536, qd=1544, kd=2056, vd=2568)
B2 = dict(q=0, k=512, v=1024, a=1536, g=2048)
AB_ORDER = [AB["qi"], AB["qi"] + 256, AB["qa"], AB["ka"], AB["va"], AB["va"] + 256, AB["ra"], AB["ra"] + 256,
            AB["qb"], AB["qb"] + 256, AB["kb"], AB["kb"] + 256, AB["vb"], AB["vb"] + 256]
CD_ORDER = [CD[n] + 256 * i for n in ("qc", "kc", "vc", "qd", "kd", "vd") for i in range(2)]
B2_ORDER = [B2[n] + 256 * i for n in ("a", "g", "q", "k", "v") for i in range(2)]


def build(nc, x_in, ln_g, ln_b, rel_table, w_in_ab, w_gate_a, b_gate_a, g_norm_a, w_out_ab, w_in_cd,
          b_forget, w_out_cd, w1_dense, w3_dense, w2_dense, w_router, w1_moe, w3_moe, w2_moe,
          mix_norm_g_2, w_in_2, rel_bias_2, conv_w_2, conv_b_2, conv_ln_g_2, conv_ln_b_2, w_out_2,
          ffn_norm_g_2, w_gate_2, w_up_2, w_down_2, final_norm_g_2,
          c_ident, c_cum, c_causal, c_iota, c_onehot, c_rowadd, c_rowsel, out):
    ctx = ExitStack()
    with ctx:
        def sb(name, shape, dt=F32):
            return ctx.enter_context(nc.sbuf_tensor(name, shape, dt))

        def sem(name):
            return ctx.enter_context(nc.semaphore(name))

        ring = sb("ring", [P, UNITS, UW])
        x = sb("x", [P, TT, D])
        u = sb("u", [P, TT, D])
        wh = sb("wh", [P, 2, UW], F32R)
        wl = sb("wl", [P, 2, UW], F32R)
        xTh = sb("xTh", [P, KT, T], F32R)
        xTl = sb("xTl", [P, KT, T], F32R)
        wnh = sb("wnh", [P, KT * NARROW], F32R)
        wnl = sb("wnl", [P, KT * NARROW], F32R)
        lnw = sb("lnw", [P, 2, D])
        y = sb("y", [P, TT, D])
        ident = sb("ident", [P, P])
        cum = sb("cum", [P, TT, T])
        causal = sb("causal", [P, T])
        iota = sb("iota", [P, P])
        ones = sb("ones", [P, P])
        rel = sb("rel", [32, 2, H])
        bias = sb("bias", [P, H, T])
        bforget = sb("bforget", [8, 1])
        gnorm = sb("gnorm", [P, P])
        cw = sb("cw", [P, 4, 32])
        tq = sb("tq", [P, 4, T])
        tk = sb("tk", [P, 4, T])
        nv = sb("nv", [P, TT, 512])
        ta = sb("ta", [P, 4, T])
        tb = sb("tb", [P, 4, T])
        nw = sb("nw", [P, TT, 512])
        nr = sb("nr", [P, TT, 512])
        wgate = nw[0:16, 0, 0:256]
        bgate = nw[0:1, 1, 0:256]
        nt = tb[0:24, 0, :]
        kiT = sb("kiT", [P, T])
        wi = sb("wi", [P, TT, 8])
        score = sb("score", [P, TT, T])
        lg = sb("lg", [P, 2, 512])
        pr = sb("pr", [P, 2, 512])
        pT = sb("pT", [P, 2, 512])
        gnat = sb("gnat", [P, TT, T])
        gT = sb("gT", [P, 2, T])
        ngc = sb("ngc", [P, 2, 8])
        gA = sb("gA", [P, 4, 384])
        small = sb("small", [P, 256])
        rstd_t = sb("rstd", [P, 8])
        topi = sb("topi", [P, 16], U32)
        trip_i = sb("trip_i", [1, 1], I32)
        half = sb("half", [P, 8])
        table = sb("table", [P, 2 * NE + 1, 6])
        cur = sb("cur", [P, 6])
        slotg = sb("slotg", [P, 1])
        psum = ctx.enter_context(nc.psum_tensor("psum", [P, 8, 512], F32))
        bank = [psum[:, i, :] for i in range(8)]

        def pair_banks(i, n):
            return psum[:, 2 * (i % 2):2 * (i % 2) + 2, 0:n]

        rel_dram = nc.dram_tensor("rel_scratch", (3, P, H, REL), F32, kind="Internal").ap()

        uf = u.rearrange("p t d -> p (t d)")
        onehot = uf[0:32, 0:2 * REL].rearrange("p (a n) -> p a n", a=2)
        relrow = uf[0:8, 2 * REL:5 * REL].rearrange("p (a n) -> p a n", a=3)
        rowadd = gA.rearrange("p h n -> p (h n)")[0:1, 0:3 * REL].rearrange("p (a n) -> p a n", a=3)
        gz = pr[:, 0, :].rearrange("p (t n) -> p t n", t=2)
        ga_ = pr[:, 1, :].rearrange("p (t n) -> p t n", t=2)
        yf = y.rearrange("p t d -> p (t d)")
        gq, gk, gqo = (yf[:, 512 * i:512 * i + 512].rearrange("p (c t) -> p c t", c=2) for i in range(3))
        nvf = nv.rearrange("p t n -> p (t n)")
        gko = nvf[:, 0:768].rearrange("p (c t) -> p c t", c=2)
        wnraw = yf[:, 0:KT * NARROW]

        def early(w):
            return w[:, 0:KT * 152].rearrange("p (k n) -> p k n", k=KT)

        def later(w):
            return w[:, KT * 152:KT * NARROW].rearrange("p (k n) -> p k n", k=KT)

        hTh, hTl = (w[:, 0:4 * T].rearrange("p (c f t) -> p c f t", c=2, f=2) for w in (wnh, wnl))
        gaf = gA.rearrange("p h n -> p (h n)")
        rowsel = gaf[0:8, 0:8 * P].rearrange("p (h t) -> p h t", h=8)
        convw = gT.rearrange("p c t -> p (c t)")[0:32, :]
        convg = score.rearrange("p t n -> p (t n)")
        convb = gnat.rearrange("p t n -> p (t n)")
        mixg = lg.rearrange("p a n -> p (a n)")
        hs = tk[:, 0:2, :]
        hn = tk[:, 2:4, :]
        disp = nv[:, 0, 0:T].rearrange("p (t j) -> p t j", t=TT)
        dispT = nv[:, 1, 0:T]

        negmax = small[:, 0:4]
        rsum = small[:, 8:40]
        rinv = small[:, 240:256]
        stat = small[:, 40:64]
        mv = small[:, 64:72]
        top8 = small[:, 76:84]
        ms = small[:, 84:92]
        e2 = small[:, 92:100]
        rstd8 = rstd_t[:, 0:8]
        rstd = rstd_t[:, 0:2]
        comb = small[:, 100:116]
        chosen = small[:, 116:132]
        slot = small[:, 132:148]
        oh2 = small[:, 148:164]
        rl = small[:, 164:180]
        trip_f = small[:, 188:190]
        lf = small[:, 192:208]
        flz = small[:, 208:224]
        fla = small[:, 224:240]
        best = rsum[:, 0:16]
        oh1 = rsum[:, 16:32]
        besti = rinv
        counts = fla[:, 0:8]
        nfT = gnat[0:8, 0, :]

        landed = [[sem(f"unit{i}_landed_{s}") for i in range(UNITS)] for s in range(2)]
        taken = [[sem(f"unit{i}_taken_{s}") for i in range(UNITS)] for s in range(2)]
        hi_ready = [sem("upper_halves_0"), sem("upper_halves_1")]
        split_used = [sem("halves_used_0"), sem("halves_used_1")]
        narrow_hi = sem("narrow_upper")
        narrow_lo = sem("narrow_lower")
        consts_in = sem("consts_in")
        filled = sem("fills_done")
        ident_in = sem("ident_in")
        x_in_sem = [sem("x_in_0"), sem("x_in_1")]
        small_in = sem("small_in")
        ln_in = sem("norm_weights")
        late_in = sem("late_constants")
        rel_out = sem("rel_rows_out")
        rel_in = [sem(f"rel_bias_in_{i}") for i in range(3)]
        tr_done = sem("transposed")
        tr_evac = sem("transposed_upper")
        tr_low = sem("transposed_lower")
        step_done = sem("step_done")
        step_evac = sem("step_copied")
        idx_scores = sem("indexer_scores")
        idx_relu = sem("indexer_relu")
        idx_acc = sem("indexer_summed")
        mask_ready = sem("key_mask_ready")
        ls_a = sem("log_sigmoid_parts")
        ls_b = sem("log_sigmoid_ready")
        gla_neg = sem("gla_negated")
        gla_exp = sem("gla_exponentials")
        gla_ops = sem("gla_operands")
        gla_A = sem("gla_products")
        gla_Am = sem("gla_products_masked")
        gla_o = sem("gla_out")
        gla_sq = sem("gla_squares")
        gla_done = sem("gla_normed")
        a_scores = sem("scores_ready")
        a_max = sem("max_ready")
        a_exp = sem("probs_ready")
        a_tr = sem("probs_transposed")
        a_pT = sem("probs_copied")
        a_pv = sem("probs_used")
        a_done = sem("heads_normed")
        sums_done = sem("sums_ready")
        sums_evac = sem("sums_copied")
        x_half = sem("norm_first_tile_ready")
        x_ready = sem("norm_ready")
        sums_first = sem("sums_first_tile_ready")
        rs_ask = sem("variance_ready")
        rs_got = sem("rstd_ready")
        m_up = sem("expert_hidden")
        m_silu = sem("expert_silu")
        m_gate = sem("expert_gated")
        m_tr = sem("expert_hidden_transposed")
        m_high = sem("expert_hidden_upper")
        m_low = sem("expert_hidden_lower")
        piece_high = sem("piece_upper")
        first_low = sem("first_piece_lower")
        piece_used = sem("piece_used")
        m_down = sem("expert_down_done")
        xe_low = sem("gathered_lower")
        up_done = [sem("hidden_ready_0"), sem("hidden_ready_1")]
        silu_done = [sem("silu_ready_0"), sem("silu_ready_1")]
        gated = [sem("gated_0"), sem("gated_1")]
        h_high = [sem("gated_upper_0"), sem("gated_upper_1")]
        h_low = [sem("gated_lower_0"), sem("gated_lower_1")]
        down_done = [sem("down_done_0"), sem("down_done_1")]
        route_ready = sem("routes_ready")
        trip_ready = sem("trip_ready")
        cur_ready = sem("expert_columns_ready")
        disp_ready = sem("dispatch_ready")
        xe_done = sem("gathered")
        xe_ready = sem("gathered_copied")
        ye_ready = sem("expert_out_scaled")
        sc_done = sem("scattered")
        sc_added = sem("scattered_added")
        pt_done = sem("dispatch_transposed")
        pt_ready = sem("dispatch_copied")
        rms_sq = sem("squares_ready")
        x2_ready = sem("residual_ready")
        gate_ask = sem("gate_logits_ready")
        gate_got = sem("gate_exps_ready")
        conv_in = sem("conv_in_ready")
        conv_done = sem("conv_done")
        conv_n = sem("conv_normed")
        conv_out = sem("conv_out")
        fin = sem("final_ready")
        stored = sem("stored")
        v_chain = sem("vector_chain")
        a_chain = sem("scalar_chain")
        g_chain = sem("pool_chain")

        def by_rows(w):
            return w.rearrange("(k p) n -> p k n", p=P)

        win = [by_rows(w_in_ab[0]), by_rows(w_in_cd[0]), by_rows(w_in_2[0])]
        wout = [by_rows(w_out_ab[0]), by_rows(w_out_cd[0]), by_rows(w_out_2[0])]

        def as_cols(i):
            return ring[:, i, :].rearrange("p (k n) -> p k n", k=KT)

        def as_rows(i):
            return ring[:, i, :].rearrange("p (k n) -> p k n", k=2)

        N0 = [0, LENGTHS[0] + 2]

        class Split:
            def __init__(self):
                self.s, self.n, self.more, self.rounds = 0, 0, 0, 0

            def skip(self):
                self.n += 1

            def place(self):
                n = self.n
                self.n += 1
                return ((n + N0[self.s]) % UNITS, self.rounds + (n // UNITS + 1), (n + N0[self.s]) % 2, n + self.more)

            def at(self, s, n, more=0, rounds=0):
                self.s, self.n, self.more, self.rounds = s, n, more, rounds

        upad = gA[:, :, 0:CONV - 1 + T]

        block = ctx.enter_context(nc.Block())

        @block.sync
        def _(sp):
            at = [0]
            st = [0]

            def load(dst_of, src, j=0, rounds=0):
                s_, n = st[0], at[0] + j
                i = (n + N0[s_]) % UNITS
                if n >= UNITS:
                    sp.wait_ge(taken[s_][i], rounds + n // UNITS)
                elif s_ == 1:
                    last = N0[1] - 1 - (N0[1] - 1 - i) % UNITS
                    sp.wait_ge(taken[0][i], trips * (L_BODY // UNITS) + (last // UNITS + 1))
                sp.dma_start(dst_of(i), src).then_inc(landed[s_][i], 16)

            def load_all(units, rounds=None):
                for j, (form, src) in enumerate(units):
                    if rounds is None:
                        load(form, src)
                        at[0] += 1
                    else:
                        load(form, src, j, rounds)

            def cols(w, c):
                return as_cols, w[:, :, bass.ds(c, 256)]

            def rows(w, k):
                return as_rows, w[:, bass.ds(k, 2), :]

            def ffn(w1, w3, w2):
                w1, w3, w2 = by_rows(w1), by_rows(w3), by_rows(w2)

                def up(c):
                    return [cols(w1, c * FC), cols(w3, c * FC)]

                def down(c):
                    return [rows(w2, c * 2)]

                load_all(up(0) + up(1) + down(0))
                with sp.Fori(0, 4) as r_:
                    load_all(up(r_ * 2 + 2) + down(r_ * 2 + 1) + up(r_ * 2 + 3) + down(r_ * 2 + 2), r_)
                at[0] += 6 * 4
                load_all(up(10) + down(9) + down(10))

            sp.dma_start(ident[:, :], c_ident).then_inc(ident_in, 16)
            for t in range(TT):
                sp.dma_start(x[:, t, :], x_in[0, t * P:(t + 1) * P, :]).then_inc(x_in_sem[t], 16)
            for part, c, src in ((early, 0, win[0][:, :, AB["ga"]:AB["ga"] + 16]),
                                 (early, 16, win[0][:, :, AB["wi"]:AB["wi"] + 8]),
                                 (early, 24, win[0][:, :, AB["ki"]:AB["ki"] + 64]),
                                 (early, 88, win[0][:, :, AB["ki"]:AB["ki"] + 64]),
                                 (later, 0, win[1][:, :, CD["fc"]:CD["fc"] + 8]), (later, 8, by_rows(w_router[0]))):
                sp.dma_start(part(wnraw)[:, :, c:c + src.shape[2]], src).then_inc(small_in, 16)
            load_all([cols(win[0], c) for c in AB_ORDER])
            load_all([rows(wout[0], 2 * j) for j in range(4)])
            ffn(w1_dense[0], w3_dense[0], w2_dense[0])
            load_all([cols(win[1], c) for c in CD_ORDER])
            load_all([rows(wout[1], 2 * j) for j in range(4)])

            m1 = w1_moe[0].rearrange("e (k p) n -> e p k n", p=P)
            m3 = w3_moe[0].rearrange("e (k p) n -> e p k n", p=P)
            m2 = w2_moe[0].rearrange("e (k p) n -> e p k n", p=P)

            def expert(e, passes):
                def part(form, w, k, n):
                    return form, w[bass.ds(e, 1), :, k, n].rearrange("a p k n -> p (a k) n")

                units = []
                for c in range(NCH_M + 1):
                    if c < NCH_M:
                        n = slice(c * FC, (c + 1) * FC)
                        units += [part(as_cols, m1, slice(0, KT), n), part(as_cols, m3, slice(0, KT), n)]
                    if c > 0:
                        units += [part(as_rows, m2, slice(2 * c - 2, 2 * c), slice(0, D))]
                load_all(units, passes * (L_BODY // UNITS))

            with sp.Fori(0, NE) as e:
                expert(e, e)
            sp.wait_ge(trip_ready, 1)
            trips = sp.value_load(trip_i[0:1, 0:1], min_val=NE, max_val=2 * NE)
            with sp.If(trips > NE):
                with sp.Fori(0, NE) as e:
                    expert(e, e + NE)
            for j in range(2):
                load(*cols(win[2], B2_ORDER[j]), j, trips * (L_BODY // UNITS))
            st[0], at[0] = 1, 0
            load_all([cols(win[2], c) for c in B2_ORDER[2:]])
            load_all([rows(wout[2], 2 * j) for j in range(4)])
            ffn(w_gate_2[0], w_up_2[0], w_down_2[0])
            for t in range(TT):
                sp.wait_ge(fin, t + 1)
                sp.dma_start(out[0, t * P:(t + 1) * P, :], u[:, t, :]).then_inc(stored, 16)
            sp.wait_ge(stored, 32)

        @block.tensor
        def _(pe):
            halves = Split()
            steps = [0]
            trs = [0]
            fresh = []
            sums = [0]
            freed = []

            def first_of(ins):
                if freed:
                    ins.then_inc(freed.pop(), 1)

            def split_unit(form):
                u_, loads, i, n = halves.place()
                pe.wait_ge(taken[halves.s][u_], loads)
                w_h, w_l = wh[:, i, :], wl[:, i, :]
                if form == "cols":
                    return (w_h.rearrange("p (k n) -> p k n", k=KT), w_l.rearrange("p (k n) -> p k n", k=KT))
                return (w_h.rearrange("p (k n) -> p k n", k=2), w_l.rearrange("p (k n) -> p k n", k=2))

            def split_done():
                freed.append(split_used[halves.s])

            def thirds(o, ws, xs, first, final, turned=False):
                a, b_ = (ws, xs) if not turned else (xs, ws)
                last = pe.matmul(o, a[0], b_[0], start=first, stop=False)
                first_of(last)
                pe.matmul(o, a[0], b_[1], start=False, stop=False)
                return pe.matmul(o, a[1], b_[0], start=False, stop=final)

            def step_bank():
                j = steps[0]
                steps[0] += 1
                if j >= 2:
                    pe.wait_ge(step_evac, j - 1)
                return bank[6 + j % 2]

            def proj_transposed():
                ps = step_bank()
                h_, l_ = split_unit("cols")
                for c in range(2):
                    n = slice(c * P, (c + 1) * P)
                    for k in range(KT):
                        need(k)
                        last = thirds(ps[:, c * T:(c + 1) * T], (h_[:, k, n], l_[:, k, n]), (xTh[:, k, :], xTl[:, k, :]),
                                      k == 0, k == KT - 1)
                last.then_inc(step_done, 1)
                split_done()

            def proj_natural():
                ps = step_bank()
                h_, l_ = split_unit("cols")
                for t in range(TT):
                    m = slice(t * P, (t + 1) * P)
                    for k in range(KT):
                        last = thirds(ps[:, t * 256:(t + 1) * 256], (h_[:, k, :], l_[:, k, :]), (xTh[:, k, m], xTl[:, k, m]),
                                      k == 0, k == KT - 1, turned=True)
                last.then_inc(step_done, 1)
                split_done()

            def narrow(part, c0, n):
                ps = step_bank()
                for k in range(KT):
                    need(k)
                    last = thirds(ps[0:n, 0:T], (part(wnh)[:, k, c0:c0 + n], part(wnl)[:, k, c0:c0 + n]), (xTh[:, k, :], xTl[:, k, :]),
                                  k == 0, k == KT - 1)
                last.then_inc(step_done, 1)
                pe.wait_ge(step_evac, steps[0])
                ps = step_bank()
                for t in range(TT):
                    last = pe.transpose(ps[:, t * n:(t + 1) * n], nt[0:n, t * P:(t + 1) * P], ident[0:n, 0:n])
                last.then_inc(step_done, 1)

            def transposes(src, n=None, ks=range(KT)):
                for t in range(TT):
                    if n == 0:
                        pe.wait_ge(x_in_sem[t], 16)
                    elif n is not None:
                        pe.wait_ge(x_ready if t else x_half, n)
                    for k in ks:
                        last = pe.transpose(bank[k // 2][:, (k % 2) * T + t * P:(k % 2) * T + (t + 1) * P],
                                            src[:, t, k * P:(k + 1) * P], ident[:, :])
                        first_of(last)
                        if t == 1 and k % 2 == 1:
                            last.then_inc(tr_done, 1)
                fresh.append((trs[0], ks))
                trs[0] += len(ks) // 2

            def need(k):
                if fresh and k % 2 == 0:
                    before, ks = fresh[0]
                    pe.wait_ge(tr_low, before + (k - ks[0]) // 2 + 1)
                    if k == ks[-1] - 1:
                        fresh.clear()

            def attention(a, q, k, v, between=None, masked=False, forget=False):
                def scores(g):
                    i = g - 8 * a
                    t, hp, n = i // 4, i % 4, P * (i // 4 + 1)
                    if g >= 2:
                        pe.wait_ge(a_max, g - 1)
                    for hh in range(2):
                        rows = slice(HD * hh, HD * hh + HD)
                        o = bank[2 * (g % 2) + hh][:, 0:n]
                        more = masked or forget
                        last = pe.matmul(o, q[rows, hp, t * P:(t + 1) * P], k[rows, hp, 0:n],
                                         start=True, stop=not more)
                        if g == 8 * a and hh == 0:
                            first_of(last)
                        if masked:
                            last = pe.matmul(o, ident[:, :], score[:, t, 0:n], start=False, stop=True)
                        if forget:
                            last = pe.matmul(o, rowsel[:, 2 * hp + hh, :], nfT[:, 0:n], start=False, stop=True)
                    last.then_inc(a_scores, 1)

                def turn(g):
                    t = (g - 8 * a) // 4
                    pe.wait_ge(a_exp, g + 1)
                    if g >= 2:
                        pe.wait_ge(a_pT, g - 1)
                    for hh in range(2):
                        for s in range(t + 1):
                            last = pe.transpose(bank[6 + g % 2][:, (2 * hh + s) * P:(2 * hh + s + 1) * P],
                                                pr[:, g % 2, hh * T + s * P:hh * T + (s + 1) * P], ident[:, :])
                            if g == 8 * a and hh == 0:
                                first_of(last)
                    last.then_inc(a_tr, 1)

                def values(g):
                    i = g - 8 * a
                    t, hp = i // 4, i % 4
                    pe.wait_ge(a_pT, g + 1)
                    if hp == 0 and a > 0:
                        pe.wait_ge(a_done, 2 * (a - 1) + t + 1)
                    for hh in range(2):
                        h = 2 * hp + hh
                        for s in range(t + 1):
                            last = pe.matmul(bank[4 + t][:, h * HD:(h + 1) * HD],
                                             pT[:, g % 2, (2 * hh + s) * P:(2 * hh + s + 1) * P],
                                             v[:, s, h * HD:(h + 1) * HD], start=(s == 0), stop=(s == t))
                    last.then_inc(a_pv, 1)

                for g in range(8 * a, 8 * a + 10):
                    if g < 8 * a + 8:
                        scores(g)
                    if g == 8 * a + 1 and between is not None:
                        between()
                        pe.wait_ge(step_evac, steps[0])
                    if 8 * a < g <= 8 * a + 8:
                        turn(g - 1)
                    if g >= 8 * a + 2:
                        values(g - 2)

            def out_projection(js=range(4)):
                pe.wait_ge(step_evac, steps[0])
                for j in js:
                    h_, l_ = split_unit("rows")
                    for kk, t in ([(kk, t) for kk in range(2) for t in range(TT)] if j < 3 else
                                  [(kk, t) for t in range(TT) for kk in range(2)]):
                        k = 2 * j + kk
                        if t == 0:
                            need(k)
                        m = slice(t * P, (t + 1) * P)
                        for n in range(2):
                            c = slice(n * 512, (n + 1) * 512)
                            last = thirds(bank[4 + 2 * t + n][:, :], (h_[:, kk, c], l_[:, kk, c]),
                                          (xTh[:, k, m], xTl[:, k, m]), k == 0, k == KT - 1, turned=True)
                        if k == KT - 1:
                            last.then_inc(sums_done if t else sums_first, 1)
                    split_done()
                sums[0] += 3 in js

            def up(s, ft, shift=0):
                for w in range(2):
                    h_, l_ = split_unit("cols")
                    for f in range(2):
                        ps = bank[(ft + f) % 4]
                        if w == 0 and ft + f >= 4:
                            pe.wait_ge(gated[s], ft + f - 3 + shift)
                        m = slice(f * P, (f + 1) * P)
                        for k in range(KT):
                            need(k)
                            last = thirds(ps[:, w * T:(w + 1) * T], (h_[:, k, m], l_[:, k, m]), (xTh[:, k, :], xTl[:, k, :]),
                                          k == 0, k == KT - 1)
                        if w == 1:
                            last.then_inc(up_done[s], 1)
                    split_done()

            def down(s, c, first, final, shift=0):
                h_, l_ = split_unit("rows")
                pe.wait_ge(h_low[s], 2 * c + 2 + shift)
                for f, t in ([(f, t) for t in range(TT) for f in range(2)] if final else
                             [(f, t) for f in range(2) for t in range(TT)]):
                    m = slice(t * P, (t + 1) * P)
                    for n in range(2):
                        n_ = slice(n * 512, (n + 1) * 512)
                        last = thirds(bank[4 + 2 * t + n][:, :], (h_[:, f, n_], l_[:, f, n_]),
                                      (hTh[:, c % 2, f, m], hTl[:, c % 2, f, m]),
                                      first and f == 0, final and f == 1, turned=True)
                    if final and t == 0 and f == 1:
                        last.then_inc(sums_first, 1)
                last.then_inc(down_done[s], 1)
                split_done()

            def ffn(s):
                pe.wait_ge(sums_evac, sums[0])
                up(s, 0)
                up(s, 2)
                down(s, 0, True, False)
                n0 = halves.n
                with pe.Fori(0, 4) as r:
                    halves.at(s, n0, r * 6, r)
                    up(s, 4, r * 4)
                    down(s, 1, False, False, r * 4)
                    up(s, 6, r * 4)
                    down(s, 2, False, False, r * 4)
                halves.at(s, n0 + 24)
                up(s, 20)
                down(s, 9, False, False)
                down(s, 10, False, True)
                sums[0] += 1

            pe.wait_ge(filled, 3)
            pe.wait_ge(ident_in, 16)
            transposes(x, 0)
            pe.wait_ge(narrow_lo, 1)
            ps = step_bank()
            for k in range(KT):
                need(k)
                last = thirds(ps[:, 0:T], (early(wnh)[:, k, 24:152], early(wnl)[:, k, 24:152]), (xTh[:, k, :], xTl[:, k, :]),
                              k == 0, k == KT - 1)
            last.then_inc(step_done, 1)
            narrow(early, 0, 24)
            proj_transposed()
            proj_transposed()
            pe.wait_ge(consts_in, CONSTS)
            ps = step_bank()
            for t in range(TT):
                first_of(pe.matmul(ps[:, t * T:(t + 1) * T], nt[0:16, t * P:(t + 1) * P], wgate[:, :],
                                   start=True, stop=False))
                last = pe.matmul(ps[:, t * T:(t + 1) * T], ones[0:1, :], bgate[:, :], start=False, stop=True)
            last.then_inc(step_done, 1)
            for i, w in enumerate((0, 0, 1)):
                ps = step_bank()
                pe.matmul(ps[0:8, 0:REL], rel[:, w, :], onehot[:, w, :], start=True, stop=False)
                pe.matmul(ps[0:8, 0:REL], ones[0:1, 0:8], rowadd[:, i, :], start=False, stop=True).then_inc(step_done, 1)
            for i in range(8):
                t, hp, n = i // 4, i % 4, P * (i // 4 + 1)
                if i == 0:
                    pe.wait_ge(step_evac, 5)
                if i >= 2:
                    pe.wait_ge(idx_relu, i - 1)
                for hh in range(2):
                    rows = slice(HD * hh, HD * hh + HD)
                    last = pe.matmul(bank[2 * (i % 2) + hh][:, 0:n], ta[rows, hp, t * P:(t + 1) * P],
                                     kiT[rows, 0:n], start=True, stop=True)
                last.then_inc(idx_scores, 1)
            proj_transposed()
            proj_transposed()
            pe.wait_ge(ls_b, 1)
            ps = step_bank()
            for c in range(2):
                for t in range(TT):
                    last = pe.matmul(ps[:, c * T:(c + 1) * T], gnat[:, t, c * P:(c + 1) * P], cum[:, t, :],
                                     start=(t == 0), stop=(t == 1))
                    first_of(last)
            last.then_inc(step_done, 1)
            for _ in range(4):
                proj_natural()
            pe.wait_ge(idx_relu, 8)
            pe.wait_ge(gla_ops, 1)
            for h in range(4):
                r, c = slice(HD * (h % 2), HD * (h % 2) + HD), h // 2
                b_ = bank[h]
                for o, m, kk, qq in (
                    (b_[0:P, 0:64], P, gk[r, c, 0:P], gq[r, c, 0:64]),
                    (b_[64:P, 64:P], 64, gk[r, c, 64:P], gq[r, c, 64:P]),
                    (b_[0:64, 64:P], 64, gko[r, c, 0:64], gqo[r, c, 64:P]),
                    (b_[0:P, P:192], P, gko[r, c, 64:192], gqo[r, c, P:192]),
                    (b_[0:P, 192:T], P, gko[r, c, 192:320], gqo[r, c, 192:T]),
                    (b_[0:P, T:T + 64], P, gk[r, c, P:T], gq[r, c, P:192]),
                    (b_[64:P, T + 64:384], 64, gk[r, c, 192:T], gq[r, c, 192:T]),
                    (b_[0:64, T + 64:384], 64, gko[r, c, 320:384], gqo[r, c, 192:T]),
                ):
                    last = pe.matmul(o, kk, qq, start=True, stop=True)
                    first_of(last)
                last.then_inc(gla_A, 1)
            proj_transposed()
            pe.wait_ge(gla_Am, 4)
            pe.wait_ge(step_evac, 14)
            for h in range(4):
                v_ = slice(h * P, (h + 1) * P)
                first_of(pe.matmul(bank[4][:, v_], gA[:, h, 0:P], nw[:, 0, v_], start=True, stop=True))
                pe.matmul(bank[5][:, v_], gA[:, h, P:T], nw[:, 0, v_], start=True, stop=False)
                last = pe.matmul(bank[5][:, v_], gA[:, h, T:384], nw[:, 1, v_], start=False, stop=True)
            last.then_inc(gla_o, 1)
            for _ in range(3):
                proj_transposed()

            def values_projected():
                proj_natural()
                proj_natural()

            def values_projected_0():
                values_projected()
                pe.wait_ge(gla_done, 1)

            pe.wait_ge(step_evac, steps[0])
            pe.wait_ge(mask_ready, 1)
            attention(0, tq, tk, nv, values_projected_0, masked=True)
            pe.wait_ge(a_done, 2)
            transposes(u)
            out_projection()
            transposes(x, 1)
            ffn(0)

            transposes(x, 2)
            narrow(later, 0, 8)
            for _ in range(4):
                proj_transposed()
            for _ in range(2):
                proj_natural()
            pe.wait_ge(ls_b, 2)
            ps = step_bank()
            for t in range(TT):
                last = pe.matmul(ps[0:8, 0:T], lf[:, t * 8:(t + 1) * 8], cum[:, t, :], start=(t == 0), stop=(t == 1))
                if t == 0:
                    first_of(last)
            last.then_inc(step_done, 1)
            for _ in range(4):
                proj_transposed()
            pe.wait_ge(step_evac, steps[0])
            pe.wait_ge(late_in, 16)
            attention(1, tq, tk, nv, values_projected, forget=True)
            attention(2, ta, tb, nw)
            pe.wait_ge(a_done, 6)
            transposes(u)
            out_projection()

            transposes(x, 3)
            pe.wait_ge(sums_evac, sums[0])
            narrow(later, 8, 8)
            pe.wait_ge(route_ready, 1)
            ps = step_bank()
            pe.matmul(ps[:, 0:8], cum[:, 0, 0:P], chosen[:, 0:8], start=True, stop=True)
            pe.matmul(ps[:, 8:16], cum[:, 0, P:T], chosen[:, 0:8], start=True, stop=False)
            pe.matmul(ps[:, 8:16], cum[:, 1, P:T], chosen[:, 8:16], start=False, stop=True)
            pe.matmul(ps[0:1, 16:24], ones[:, 0:1], chosen[:, 0:8], start=True, stop=False)
            pe.matmul(ps[0:1, 16:24], ones[:, 0:1], chosen[:, 8:16], start=False, stop=True).then_inc(step_done, 1)

            def gather(n):
                pe.wait_ge(disp_ready, n)
                for k in range(KT):
                    for t in range(TT):
                        last = pe.matmul(bank[6 + k // 4][:, (k % 4) * P:(k % 4 + 1) * P], x[:, t, k * P:(k + 1) * P],
                                         disp[:, t, :], start=(t == 0), stop=(t == 1))
                        first_of(last)
                    if k % 4 == 3:
                        last.then_inc(xe_done, 1)

            def turn_dispatch(n):
                pe.wait_ge(sc_added, n * 4 - 2)
                for t in range(TT):
                    pe.transpose(bank[6][:, t * P:(t + 1) * P], disp[:, t, :], ident[:, :])
                for t in range(TT):
                    last = pe.matmul(bank[7][:, 0:1], disp[:, t, :], cur[:, 4 + t:5 + t], start=(t == 0), stop=(t == 1))
                last.then_inc(pt_done, 1)

            pe.wait_ge(step_evac, steps[0])
            gather(1)
            pe.wait_ge(trip_ready, 1)
            trips = pe.value_load(trip_i[0:1, 0:1], min_val=NE, max_val=2 * NE)

            def pieces(form, e):
                u_, loads, i, n = halves.place()
                for j in range(2):
                    if j == 0 and halves.n > LENGTHS[0] + 2:
                        pe.wait_ge(first_low, n - (LENGTHS[0] + 1))
                    elif j == 1 or halves.n <= LENGTHS[0] + 2:
                        pe.wait_ge(taken[0][u_], loads)
                    h_, l_ = ((w[:, i, j * 1024:(j + 1) * 1024]).rearrange("p (k n) -> p k n", k=4 if form == "cols" else 1)
                              for w in (wh, wl))
                    yield j, h_, l_
                    freed.append(piece_used)

            def expert_up(c, w, e, between=()):
                if w == 0 and c >= 2:
                    pe.wait_ge(m_gate, e * NCH_M + (c - 1))
                for j, h_, l_ in pieces("cols", e):
                    for kk in range(4):
                        k = 4 * j + kk
                        if k == (4 if c == 1 else 0):
                            for f, arguments in between:
                                f(*arguments)
                        last = thirds(bank[c % 2][:, w * FC:(w + 1) * FC], (h_[:, kk, :], l_[:, kk, :]),
                                      (xTh[:, k, 0:P], xTl[:, k, 0:P]), k == 0, k == KT - 1, turned=True)
                    if w == 1 and j == 1:
                        last.then_inc(m_up, 1)

            def expert_turn(c, e):
                pe.wait_ge(m_gate, e * NCH_M + (c + 1))
                if c == 0:
                    pe.wait_ge(sc_added, e * 4 + 4)
                if c >= 2:
                    pe.wait_ge(m_low, e * NCH_M + (c - 1))
                for f in range(2):
                    last = pe.transpose(bank[2 + c % 2][:, f * P:(f + 1) * P], hn[:, c % 2, f * P:(f + 1) * P], ident[:, :])
                last.then_inc(m_tr, 1)

            def expert_down(c, e):
                for f, h_, l_ in pieces("rows", e):
                    if f == 0:
                        pe.wait_ge(m_low, e * NCH_M + (c + 1))
                    for n in range(2):
                        n_ = slice(n * 512, (n + 1) * 512)
                        last = thirds(bank[4 + n][:, :], (h_[:, 0, n_], l_[:, 0, n_]), (hTh[:, c % 2, f, 0:P], hTl[:, c % 2, f, 0:P]),
                                      c == 0 and f == 0, c == NCH_M - 1 and f == 1, turned=True)
                    if f == 1:
                        last.then_inc(m_down, 1)

            def scatter(n):
                pe.wait_ge(ye_ready, 2 * n - 1)
                for t in range(TT):
                    for h_ in range(2):
                        last = pe.matmul(bank[(6, 2)[t] + h_][:, :], dispT[:, t * P:(t + 1) * P],
                                         y[:, 0, h_ * 512:(h_ + 1) * 512], start=True, stop=True)
                        last.then_inc(sc_done, 1)

            assert halves.n == LENGTHS[0]
            assert not freed
            freed.append(piece_used)
            with pe.Fori(0, trips) as e:
                halves.at(0, LENGTHS[0], e * L_BODY, e * (L_BODY // UNITS))
                pe.wait_ge(xe_low, e * 2 + 2)
                for c in range(NCH_M):
                    expert_up(c, 0, e, [(scatter, (e + 1,))] if c == 1 else [])
                    expert_up(c, 1, e, ([(turn_dispatch, (e + 1,))] if c == 1 else []) +
                              ([(expert_turn, (c - 1, e))] if c > 0 else []))
                    if 0 < c < NCH_M - 1:
                        expert_down(c - 1, e)
                pe.wait_ge(pt_ready, e + 1)
                gather(e + 2)
                expert_turn(NCH_M - 1, e)
                expert_down(NCH_M - 2, e)
                expert_down(NCH_M - 1, e)
            first_of(pe.transpose(bank[0][:, 0:P], ident[:, :], ident[:, :]))
            scatter(trips + 1)

            transposes(u, 5)
            pe.wait_ge(late_in, 80)
            for i in range(4):
                if i == 0:
                    ps = step_bank()
                last = pe.transpose(ps[:, i * 32:(i + 1) * 32], convw[:, i * P:(i + 1) * P], ident[0:32, 0:32])
            last.then_inc(step_done, 1)
            halves.at(0, LENGTHS[0], trips * L_BODY, trips * (L_BODY // UNITS))
            for _ in range(2):
                proj_transposed()
            halves.at(1, 0)
            for _ in range(6):
                proj_transposed()
            pe.wait_ge(step_evac, steps[0])
            attention(3, tq, tk, nv, values_projected)
            pe.wait_ge(conv_done, 2)
            for t in range(TT):
                ps = step_bank()
                for c in range(4):
                    last = pe.transpose(ps[:, c * P:(c + 1) * P], ta[:, c, t * P:(t + 1) * P], ident[:, :])
                last.then_inc(step_done, 1)
            pe.wait_ge(a_done, 8)
            transposes(u, ks=range(4))
            out_projection(range(2))
            pe.wait_ge(conv_out, 2)
            transposes(u, ks=range(4, KT))
            out_projection(range(2, 4))
            transposes(u, 6)
            ffn(1)

        @block.scalar
        def _(act):
            steps = [0]
            trs = [0]
            chain = [0]

            def link(ins):
                chain[0] += 1
                ins.then_inc(a_chain, 1)
                act.wait_ge(a_chain, chain[0])

            def load(dst, src):
                act.dma_start(dst, src).then_inc(consts_in, 16)

            halves = Split()

            def upper(after=None, count=0):
                u_, loads, i, n = halves.place()
                s_ = halves.s
                act.wait_ge(landed[s_][u_], loads * 16)
                if after is not None:
                    act.wait_ge(after, count)
                elif not isinstance(n, int) or n >= 2:
                    act.wait_ge(split_used[s_], n - 1)
                act.activation(wh[:, i, :], ring[:, u_, :], ACT.Copy).then_inc(hi_ready[s_], 1)

            def copy_transposed(gs=range(4)):
                for g in gs:
                    trs[0] += 1
                    act.wait_ge(tr_done, trs[0])
                    act.activation(xTh[:, 2 * g:2 * g + 2, :], bank[g].rearrange("p (k t) -> p k t", k=2),
                                   ACT.Copy).then_inc(tr_evac, 1)

            def step_out():
                j = steps[0]
                steps[0] += 1
                act.wait_ge(step_done, j + 1)
                return bank[6 + j % 2]

            def copy_step(dst, func=ACT.Copy, scale=1.0):
                act.activation(dst, step_out().rearrange("p (k t) -> p k t", k=2), func,
                               scale=scale).then_inc(step_evac, 1)

            def log_sigmoid_parts(ps, z, a):
                link(act.activation(z, ps, ACT.Copy))
                act.activation(a, z, ACT.Abs).then_inc(step_evac, 1)
                act.wait_ge(step_evac, steps[0])
                link(act.activation(a, a, ACT.Exp, scale=-1.0))
                act.activation(a, a, ACT.Ln, bias=1.0).then_inc(ls_a, 1)

            def attention(a, between=None):
                def exps(g):
                    t, hp, n = (g - 8 * a) // 4, (g - 8 * a) % 4, P * ((g - 8 * a) // 4 + 1)
                    act.wait_ge(a_max, g + 1)
                    if g >= 2:
                        act.wait_ge(a_tr, g - 1)
                    for hh in range(2):
                        col = (a % 2) * 16 + t * 8 + 2 * hp + hh
                        last = act.activation(pr[:, g % 2, hh * T:hh * T + n], lg[:, g % 2, hh * T:hh * T + n],
                                              ACT.Exp, bias=negmax[:, 2 * (g % 2) + hh:2 * (g % 2) + hh + 1],
                                              accum_out=rsum[:, col:col + 1])
                    last.then_inc(a_exp, 1)

                def copy(g):
                    t = (g - 8 * a) // 4
                    act.wait_ge(a_tr, g + 1)
                    if g >= 2:
                        act.wait_ge(a_pv, g - 1)
                    dst = pT[:, g % 2, :].rearrange("p (h s t) -> p h s t", h=2, s=2)[:, :, 0:t + 1, :]
                    src = bank[6 + g % 2].rearrange("p (h s t) -> p h s t", h=2, s=2)[:, :, 0:t + 1, :]
                    act.activation(dst, src, ACT.Copy).then_inc(a_pT, 1)

                if a >= 2:
                    act.wait_ge(a_done, 2 * (a - 1))
                for g in range(8 * a, 8 * a + 9):
                    if g < 8 * a + 8:
                        exps(g)
                    if g == 8 * a + 1 and between is not None:
                        between()
                    if g > 8 * a:
                        copy(g - 1)

            def silus(s, c, before, shift=0):
                for _ in range(before):
                    upper()
                ft = 2 * c
                for f in range(2):
                    act.wait_ge(up_done[s], ft + f + 1 + shift)
                    if ft + f >= 2:
                        act.wait_ge(gated[s], ft + f - 1 + shift)
                    act.activation(hs[:, f, :], bank[(ft + f) % 4][:, 0:T], ACT.Silu).then_inc(silu_done[s], 1)
                upper()
                for f in range(2):
                    act.wait_ge(gated[s], ft + f + 1 + shift)
                    if c >= 2 and f == 0:
                        act.wait_ge(down_done[s], c - 1 + shift_half[0])
                    act.activation(hTh[:, c % 2, f, :], hn[:, f, :], ACT.Copy).then_inc(h_high[s], 1)

            shift_half = [0]

            def ffn(s):
                silus(s, 0, 1)
                silus(s, 1, 1)
                n0 = halves.n
                with act.Fori(0, 4) as r:
                    shift_half[0] = r * 2
                    halves.at(s, n0, r * 6, r)
                    silus(s, 2, 2, r * 4)
                    silus(s, 3, 2, r * 4)
                shift_half[0] = 0
                halves.at(s, n0 + 24)
                silus(s, 10, 2)
                if s == 0:
                    upper()
                    upper(down_done[s], NCH_D)

            copy_transposed()
            act.wait_ge(small_in, 96)
            act.activation(wnh[:, :], wnraw, ACT.Copy).then_inc(narrow_hi, 1)
            load(cum[:, :, :], c_cum)
            load(causal[:, :], c_causal)
            load(iota[:, :], c_iota)
            load(onehot[:, :, :], c_onehot)
            load(rowadd[:, :, :], c_rowadd)
            load(rel[:, 0, :], rel_table)
            load(rel[:, 1, :], rel_bias_2)
            load(wgate[:, :], w_gate_a[0])
            load(bgate[:, :], b_gate_a)
            load(bforget[:, :], b_forget.rearrange("a n -> n a"))
            load(gnorm[:, :], g_norm_a.broadcast_to([P, P]))
            upper()
            upper()
            act.activation(kiT[:, :], step_out()[:, 0:T], ACT.Copy).then_inc(step_evac, 1)
            act.activation(nt[:, :], step_out()[0:24, 0:T], ACT.Copy).then_inc(step_evac, 1)
            act.activation(wi[:, :, :], step_out()[:, 0:48].rearrange("p (t n) -> p t n", t=2)[:, :, 16:24], ACT.Copy)\
               .then_inc(step_evac, 1)
            copy_step(ta[:, 0:2, :])
            upper()
            copy_step(ta[:, 2:4, :])
            upper()
            log_sigmoid_parts(step_out().rearrange("p (t n) -> p t n", t=2), gz[:, :, :], ga_[:, :, :])
            for i in range(3):
                act.activation(relrow[:, i, :], step_out()[0:8, 0:REL], ACT.Copy).then_inc(step_evac, 1)
            for i in range(8):
                t, n = i // 4, P * (i // 4 + 1)
                act.wait_ge(idx_scores, i + 1)
                if i >= 2:
                    act.wait_ge(idx_acc, i - 1)
                act.activation(lg[:, i % 2, :].rearrange("p (h s) -> p h s", h=2)[:, :, 0:n],
                               pair_banks(i, n), ACT.Relu)\
                   .then_inc(idx_relu, 1)
            copy_step(tb[:, 0:2, :], scale=HD ** -0.5)
            upper()
            copy_step(tb[:, 2:4, :])
            upper()
            copy_step(gT[:, :, :], scale=1.0 / 16.0)
            act.wait_ge(step_evac, steps[0])
            for c in range(2):
                copy_step(nw[:, :, c * 256:(c + 1) * 256])
                upper()
                act.wait_ge(gla_neg, 1)
                for j in range(4):
                    s_ = slice(64 * j, 64 * j + 64)
                    mid = 64 * j + 31
                    act.activation(gq[:, c, s_], gT[:, c, s_], ACT.Exp, bias=ngc[:, c, j:j + 1])
                    last = act.activation(gk[:, c, s_], gT[:, c, s_], ACT.Exp, bias=gT[:, c, mid:mid + 1], scale=-1.0)
                    if j > 0:
                        b_ = 64 * j - 1
                        act.activation(gqo[:, c, s_], gT[:, c, s_], ACT.Exp, bias=ngc[:, c, 3 + j:4 + j])
                        o = 64 * (j * (j - 1) // 2)
                        last = act.activation(gko[:, c, o:o + 64 * j], gT[:, c, 0:64 * j], ACT.Exp,
                                              bias=gT[:, c, b_:b_ + 1], scale=-1.0)
                last.then_inc(gla_exp, 1)
            for c in range(2):
                copy_step(nr[:, :, c * 256:(c + 1) * 256], ACT.Silu)
                upper()
            copy_step(tq[:, 0:2, :], scale=HD ** -0.5)
            upper()
            act.wait_ge(gla_o, 1)
            for t in range(TT):
                act.activation(y[:, t, 0:512], bank[4 + t][:, :], ACT.Square).then_inc(gla_sq, 1)
            copy_step(tq[:, 2:4, :], scale=HD ** -0.5)
            upper()

            def copies(*dsts):
                for dst in dsts:
                    copy_step(dst)
                    upper()

            copies(tk[:, 0:2, :], tk[:, 2:4, :])
            attention(0, lambda: copies(nv[:, :, 0:256], nv[:, :, 256:512]))
            copy_transposed()
            upper()
            upper()
            upper()
            upper(sums_done, 1)
            copy_transposed()
            ffn(0)

            copy_transposed()
            act.wait_ge(consts_in, CONSTS)
            act.activation(nt[0:8, :], step_out()[0:8, 0:T], ACT.Identity, bias=bforget[:, 0:1]).then_inc(step_evac, 1)
            log_sigmoid_parts(step_out()[:, 0:16], flz, fla)
            for q, k, v in ((tq, tk, nv), (ta, tb, nw)):
                for i in range(2):
                    copy_step(q[:, 2 * i:2 * i + 2, :], scale=HD ** -0.5)
                    upper()
                copies(k[:, 0:2, :], k[:, 2:4, :])
                if q is tq:
                    copies(v[:, :, 0:256], v[:, :, 256:512])
                    act.activation(nfT, step_out()[0:8, 0:T], ACT.Copy, scale=-1.0).then_inc(step_evac, 1)
            attention(1, lambda: copies(nw[:, :, 0:256], nw[:, :, 256:512]))
            attention(2)
            copy_transposed()
            upper()
            upper()
            upper()
            upper(sums_done, 2)
            copy_transposed()
            act.activation(nt[0:8, :], step_out()[0:8, 0:T], ACT.Copy).then_inc(step_evac, 1)
            act.activation(rl, step_out()[:, 0:16], ACT.Copy).then_inc(step_evac, 1)
            act.wait_ge(gate_ask, 1)
            act.activation(e2[:, 2:4], e2[:, 0:2], ACT.Exp).then_inc(gate_got, 1)
            ps = step_out()
            link(act.activation(slot, ps[:, 0:16], ACT.Copy))
            act.activation(counts[0:1, :], ps[0:1, 16:24], ACT.Copy).then_inc(step_evac, 1)

            def gathered(n):
                for i in range(2):
                    act.wait_ge(xe_done, n * 2 + (i - 1))
                    act.activation(xTh[:, 4 * i:4 * i + 4, 0:P], bank[6 + i].rearrange("p (k t) -> p k t", k=4),
                                   ACT.Copy).then_inc(xe_ready, 1)

            def turned(n):
                act.wait_ge(pt_done, n)
                act.activation(dispT[:, :], bank[6][:, 0:T], ACT.Copy)
                act.activation(slotg[:, :], bank[7][:, 0:1], ACT.Copy).then_inc(pt_ready, 1)

            gathered(1)
            act.wait_ge(trip_ready, 1)
            trips = act.value_load(trip_i[0:1, 0:1], min_val=NE, max_val=2 * NE)

            def expert_silu(c, e):
                act.wait_ge(m_up, e * NCH_M + (c + 1))
                if c >= 2:
                    act.wait_ge(m_gate, e * NCH_M + (c - 1))
                act.activation(hs[:, c % 2, :], bank[c % 2][:, 0:FC], ACT.Silu).then_inc(m_silu, 1)

            def expert_copy(c, e):
                act.wait_ge(m_tr, e * NCH_M + (c + 1))
                if c >= 2:
                    act.wait_ge(m_down, e * NCH_M + (c - 1))
                act.activation(hTh[:, c % 2, :, 0:P], bank[2 + c % 2][:, 0:FC].rearrange("p (f t) -> p f t", f=2),
                               ACT.Copy).then_inc(m_high, 1)

            def upper_piece(e, p):
                j = p % 2
                if j == 0:
                    here[0] = halves.place()
                u_, loads, i, n = here[0]
                if j == 0:
                    act.wait_ge(landed[0][u_], loads * 16)
                act.wait_ge(piece_used, e * PIECES + (p - 2))
                c = slice(j * 1024, (j + 1) * 1024)
                act.activation(wh[:, i, c], ring[:, u_, c], ACT.Copy).then_inc(piece_high, 1)

            here = [None]
            assert halves.n == LENGTHS[0] + 2
            with act.Fori(0, trips) as e:
                halves.at(0, LENGTHS[0] + 2, e * L_BODY, e * (L_BODY // UNITS))
                for p in range(4, PIECES + 4):
                    for c in range(NCH_M):
                        if p == silu_at(c):
                            expert_silu(c, e)
                        if p == copy_at(c):
                            expert_copy(c, e)
                    if p == GATHERED_AT:
                        gathered(e + 2)
                    if p == TURNED_AT:
                        turned(e + 1)
                    upper_piece(e, p)
                act.wait_ge(m_down, e * NCH_M + NCH_M)
                act.activation(y[:, 0, 0:512], bank[4][:, :], ACT.Copy, scale=slotg[:, 0:1]).then_inc(ye_ready, 1)
            halves.at(1, 0)

            def squares(waits):
                for t in range(TT):
                    act.wait_ge(*waits[t])
                    act.activation(y[:, t, :], x[:, t, :], ACT.Square, accum_out=ms[:, t:t + 1]).then_inc(rms_sq, 1)

            squares([(x_half, 4), (x_ready, 4)])
            copy_transposed()
            act.activation(cw[:, :, :], step_out()[:, 0:P].rearrange("p (c j) -> p c j", c=4), ACT.Copy)\
               .then_inc(step_evac, 1)
            copy_step(ta[:, 0:2, :])
            upper(split_used[0], LENGTHS[0] + 1)
            copy_step(ta[:, 2:4, :])
            upper(split_used[0], LENGTHS[0] + 2)
            copy_step(tb[:, 0:2, :], ACT.Sigmoid)
            upper()
            copy_step(tb[:, 2:4, :], ACT.Sigmoid)
            act.wait_ge(step_evac, steps[0])
            act.nop().then_inc(conv_in, 1)
            upper()
            for i in range(2):
                copy_step(tq[:, 2 * i:2 * i + 2, :], scale=HD ** -0.5)
                upper()
            copies(tk[:, 0:2, :], tk[:, 2:4, :])
            attention(3, lambda: copies(nv[:, :, 0:256], nv[:, :, 256:512]))
            for t in range(TT):
                act.activation(nr[:, t, :], step_out()[:, :], ACT.Copy).then_inc(step_evac, 1)
            copy_transposed(range(2))
            for t in range(TT):
                act.wait_ge(conv_n, t + 1)
                act.activation(u[:, t, 512:1024], nr[:, t, :], ACT.Silu).then_inc(conv_out, 1)
            upper()
            copy_transposed(range(2, 4))
            upper()
            upper()
            upper(sums_done, 3)
            squares([(x2_ready, 1), (x2_ready, 2)])
            copy_transposed()
            ffn(1)
            squares([(x2_ready, 3), (x2_ready, 4)])

        @block.vector
        def _(dve):
            chain = [0]
            norms = [0]

            def link(ins):
                chain[0] += 1
                ins.then_inc(v_chain, 1)
                dve.wait_ge(v_chain, chain[0])

            norms_asked = [0]

            def ask(ins):
                ins.then_inc(rs_ask, 1)
                norms_asked[0] += 1
                dve.wait_ge(rs_got, norms_asked[0])

            def norm_weights(n):
                dve.wait_ge(ln_in, LN_AT[n])

            halves = Split()

            def lower():
                u_, _, i, n = halves.place()
                s_ = halves.s
                dve.wait_ge(hi_ready[s_], n + 1)
                dve.tensor_tensor(wl[:, i, :], ring[:, u_, :], wh[:, i, :].bitcast(F32), ALU.subtract)\
                   .then_inc(taken[s_][u_], 1)

            trs = [0]

            def lower_transposed(gs=range(4)):
                for g in gs:
                    trs[0] += 1
                    dve.wait_ge(tr_evac, trs[0])
                    k = slice(2 * g, 2 * g + 2)
                    dve.tensor_tensor(xTl[:, k, :], bank[g].rearrange("p (k t) -> p k t", k=2),
                                      xTh[:, k, :].bitcast(F32), ALU.subtract).then_inc(tr_low, 1)

            events = [0]

            def residual(t, dst, alpha, done, n):
                if t == 0:
                    events[0] += 1
                    dve.wait_ge(sums_first, events[0])
                else:
                    dve.wait_ge(done, n)
                for h_ in range(2):
                    s_ = slice(h_ * 512, (h_ + 1) * 512)
                    last = dve.scalar_tensor_tensor(dst[:, t, s_], x[:, t, s_], alpha, bank[4 + 2 * t + h_][:, :],
                                                    ALU.mult, ALU.add)
                link(last)
                if t == 1:
                    dve.nop().then_inc(sums_evac, 1)

            def ask_for(t, ins):
                ins.then_inc(rs_ask, 1)
                norms_asked[0] += 1
                return norms_asked[0]

            def moments(src, tiles, width):
                for t in tiles:
                    for j in range(width // 512):
                        last = dve.bn_stats(stat[:, t * 12 + 6 * j:t * 12 + 6 * j + 6], src(t)[:, j * 512:(j + 1) * 512])
                    link(last)
                    link(dve.bn_aggr(mv[:, 2 * t:2 * t + 2], stat[:, t * 12:t * 12 + 6 * (width // 512)]))
                ask(dve.tensor_scalar(e2[:, 0:2], mv[:, 1:4:2], LN_EPS, None, ALU.add))

            def layer_norm(src, *sums):
                n = norms[0]
                norms[0] += 1
                asked = []
                for t in range(TT):
                    if sums:
                        residual(t, src, ALPHA, *sums)
                    for j in range(2):
                        last = dve.bn_stats(stat[:, t * 12 + 6 * j:t * 12 + 6 * j + 6], src[:, t, j * 512:(j + 1) * 512])
                    link(last)
                    link(dve.bn_aggr(mv[:, 2 * t:2 * t + 2], stat[:, t * 12:t * 12 + 12]))
                    asked.append(ask_for(t, dve.tensor_scalar(e2[:, t:t + 1], mv[:, 2 * t + 1:2 * t + 2], LN_EPS, None, ALU.add)))
                norm_weights(n)
                w = lnw
                for t in range(TT):
                    dve.wait_ge(rs_got, asked[t])
                    link(dve.scalar_tensor_tensor(src[:, t, :], src[:, t, :], mv[:, 2 * t:2 * t + 1], w[:, 0, :],
                                                  ALU.subtract, ALU.mult))
                    dve.scalar_tensor_tensor(x[:, t, :], src[:, t, :], rstd[:, t:t + 1], w[:, 1, :],
                                             ALU.mult, ALU.add).then_inc(x_ready if t else x_half, 1)
                dve.wait_ge(x_ready, norms[0])
                dve.wait_ge(x_half, norms[0])

            def rms_norm(dst, n_sq, signals, *sums):
                n = norms[0]
                norms[0] += 1
                if sums:
                    for t in range(TT):
                        residual(t, x, 1.0, *sums)
                        dve.nop().then_inc(x2_ready, 1)
                asked = []
                for t in range(TT):
                    dve.wait_ge(rms_sq, 2 * n_sq + t + 1)
                    asked.append(ask_for(t, dve.tensor_scalar(e2[:, t:t + 1], ms[:, t:t + 1], 1.0 / D, RMS_EPS, ALU.mult, ALU.add)))
                norm_weights(n)
                w = lnw[:, 0, :] if n_sq > 0 else mixg
                for t in range(TT):
                    dve.wait_ge(rs_got, asked[t])
                    dve.scalar_tensor_tensor(dst[:, t, :], x[:, t, :], rstd[:, t:t + 1], w,
                                             ALU.mult, ALU.mult).then_inc(signals[t], 1)

            def pairs(ap, n):
                return ap.rearrange("p (h s) -> p h s", h=2)[:, :, 0:n]

            def attention(a, add, v_off, between=None, taps=0):
                for g in range(8 * a, 8 * a + 8):
                    if g == 8 * a + 2 and between is not None:
                        between()
                    t, hp, n = (g - 8 * a) // 4, (g - 8 * a) % 4, P * ((g - 8 * a) // 4 + 1)
                    dve.wait_ge(a_scores, g + 1)
                    if g >= 2:
                        dve.wait_ge(a_exp, g - 1)
                    link(dve.tensor_tensor(pairs(lg[:, g % 2, :], n), pair_banks(g, n),
                                           add(hp, T - n), ALU.add))
                    dve.tensor_reduce(negmax[:, 2 * (g % 2):2 * (g % 2) + 2], pairs(lg[:, g % 2, :], n),
                                      AX.X, ALU.max, negate=True).then_inc(a_max, 1)
                    for _ in range(taps):
                        next_tap()
                for t in range(TT):
                    dve.wait_ge(a_pv, 8 * a + 4 * (t + 1))
                    r0 = (a % 2) * 16 + t * 8
                    link(dve.reciprocal(rinv[:, t * 8:t * 8 + 8], rsum[:, r0:r0 + 8]))
                    dve.tensor_tensor(u[:, t, v_off:v_off + 512].rearrange("p (h d) -> p h d", h=8),
                                      bank[4 + t].rearrange("p (h d) -> p h d", h=8),
                                      rinv[:, t * 8:t * 8 + 8].unsqueeze(2).broadcast_to([P, 8, HD]),
                                      ALU.mult).then_inc(a_done, 1)

            def relative():
                return lambda hp, lo: bias[:, 2 * hp:2 * hp + 2, lo:T]

            def gates(s, c, before, shift=0):
                for _ in range(before):
                    lower()
                ft = 2 * c
                for f in range(2):
                    dve.wait_ge(silu_done[s], ft + f + 1 + shift)
                    if c >= 1:
                        dve.wait_ge(h_low[s], ft + f - 1 + shift)
                    dve.tensor_tensor(hn[:, f, :], hs[:, f, :], bank[(ft + f) % 4][:, T:2 * T], ALU.mult)\
                       .then_inc(gated[s], 1)
                lower()
                for f in range(2):
                    dve.wait_ge(h_high[s], ft + f + 1 + shift)
                    dve.tensor_tensor(hTl[:, c % 2, f, :], hn[:, f, :], hTh[:, c % 2, f, :].bitcast(F32), ALU.subtract)\
                       .then_inc(h_low[s], 1)

            def ffn(s):
                gates(s, 0, 1)
                gates(s, 1, 1)
                n0 = halves.n
                with dve.Fori(0, 4) as r:
                    halves.at(s, n0, r * 6, r)
                    gates(s, 2, 2, r * 4)
                    gates(s, 3, 2, r * 4)
                halves.at(s, n0 + 24)
                gates(s, 10, 2)
                if s == 0:
                    halves.skip()

            dve.memset(ones[:, :], 1.0).then_inc(filled, 1)
            dve.memset(half[:, :], -0.5).then_inc(filled, 1)
            dve.memset(table[:, :, :], 0.0).then_inc(filled, 1)

            def log_sigmoid(z, a, dst, n):
                dve.wait_ge(ls_a, n)
                dve.scalar_tensor_tensor(dst, z, 0.0, a, ALU.min, ALU.subtract).then_inc(ls_b, 1)

            lower_transposed()
            dve.wait_ge(narrow_hi, 1)
            dve.tensor_tensor(wnl[:, :], wnraw, wnh[:, :].bitcast(F32), ALU.subtract).then_inc(narrow_lo, 1)
            for _ in range(4):
                lower()
            log_sigmoid(gz[:, :, :], ga_[:, :, :], gnat[:, :, :], 1)
            for i in range(8):
                t, hp, n = i // 4, i % 4, P * (i // 4 + 1)
                dve.wait_ge(idx_relu, i + 1)
                for hh in range(2):
                    r = lg[:, i % 2, hh * T:hh * T + n]
                    w = wi[:, t, 2 * hp + hh:2 * hp + hh + 1]
                    if hp == 0 and hh == 0:
                        last = dve.tensor_scalar(score[:, t, 0:n], r, w, None, ALU.mult)
                    else:
                        last = dve.scalar_tensor_tensor(score[:, t, 0:n], r, w, score[:, t, 0:n], ALU.mult, ALU.add)
                    link(last)
                dve.nop().then_inc(idx_acc, 1)
            def top_keys(t, first, final):
                n = P * (t + 1)
                if first == 0:
                    link(dve.tensor_tensor(score[:, t, 0:n], score[:, t, 0:n], causal[:, T - n:T], ALU.add))
                for _ in range(first, final):
                    link(dve.max(top8, score[:, t, 0:n]))
                    link(dve.match_replace(score[:, t, 0:n], top8, score[:, t, 0:n], TAKEN))
                if final == TOPK // 8:
                    link(dve.tensor_scalar(score[:, t, 0:n], score[:, t, 0:n], 10.0 * NEG * 1e7, NEG, ALU.is_gt, ALU.mult))

            lower()
            top_keys(0, 0, 8)
            lower()
            dve.wait_ge(step_evac, 12)
            for c in range(2):
                dve.tensor_scalar(ngc[:, c, 0:4], gT[:, c, 31:T:64], -1.0, None, ALU.mult)
                last = dve.tensor_scalar(ngc[:, c, 4:7], gT[:, c, 63:T - 64:64], -1.0, None, ALU.mult)
            last.then_inc(gla_neg, 1)
            top_keys(1, 0, 4)
            lower()
            top_keys(1, 4, 8)
            dve.nop().then_inc(mask_ready, 1)
            lower()
            dve.wait_ge(gla_exp, 2)
            dve.wait_ge(step_evac, 12)
            dve.tensor_tensor(gq[:, :, :], gq[:, :, :], tb[:, 0:2, :], ALU.mult)
            dve.tensor_tensor(gk[:, :, :], gk[:, :, :], tb[:, 2:4, :], ALU.mult)
            dve.tensor_tensor(gqo[:, :, 64:T], gqo[:, :, 64:T], tb[:, 0:2, 64:T], ALU.mult)
            for j in (1, 2, 3):
                o = 64 * (j * (j - 1) // 2)
                last = dve.tensor_tensor(gko[:, :, o:o + 64 * j], gko[:, :, o:o + 64 * j], tb[:, 2:4, 0:64 * j], ALU.mult)
            last.then_inc(gla_ops, 1)
            lower()
            for h in range(4):
                dve.wait_ge(gla_A, h + 1)
                dve.tensor_tensor(gA[:, h, 0:T], bank[h][:, 0:T], cum[:, 0, :], ALU.mult)
                dve.tensor_tensor(gA[:, h, T:384], bank[h][:, T:384], cum[:, 1, P:T], ALU.mult).then_inc(gla_Am, 1)
            lower()
            dve.wait_ge(step_evac, 16)
            for t in range(TT):
                v4 = nr[:, t, :].rearrange("p (h d) -> p h d", h=4)
                link(dve.tensor_tensor(v4, v4, gnorm[:, :].unsqueeze(1).broadcast_to([P, 4, P]), ALU.mult))
            lower()
            for t in range(TT):
                dve.wait_ge(gla_sq, t + 1)
                link(dve.tensor_reduce(ms[:, 4 * t:4 * t + 4], y[:, t, 0:512].rearrange("p (h d) -> p h d", h=4),
                                       AX.X, ALU.add))
            lower()
            ask(dve.tensor_scalar(e2[:, 0:8], ms[:, 0:8], 1.0 / P, LN_EPS, ALU.mult, ALU.add))
            dve.wait_ge(rel_out, 48)
            for t in range(TT):
                v4 = nr[:, t, :].rearrange("p (h d) -> p h d", h=4)
                link(dve.tensor_tensor(v4, v4, rstd8[:, 4 * t:4 * t + 4].unsqueeze(2).broadcast_to([P, 4, P]), ALU.mult))
                last = dve.tensor_tensor(u[:, t, 0:512], nr[:, t, :], bank[4 + t][:, :], ALU.mult)
            last.then_inc(gla_done, 1)

            def two_units():
                lower()
                lower()

            two_units()
            dve.wait_ge(rel_in[0], 16)
            attention(0, relative(), 512, two_units)
            lower_transposed()
            two_units()
            halves.skip()
            layer_norm(y, sums_done, 1)
            lower_transposed()
            lower()
            ffn(0)
            layer_norm(y, down_done[0], NCH_D)

            lower_transposed()
            for _ in range(3):
                lower()
            log_sigmoid(flz, fla, lf, 2)
            for _ in range(8):
                lower()
            attention(1, lambda hp, lo: causal[:, lo:T].unsqueeze(1).broadcast_to([P, 2, T - lo]), 0, two_units)
            dve.wait_ge(rel_in[1], 16)
            attention(2, relative(), 512)
            lower_transposed()
            two_units()
            halves.skip()
            layer_norm(y, sums_done, 2)

            lower_transposed()
            lower()
            dve.wait_ge(step_evac, STEPS_ROUTER)
            tiles = [slice(8 * t, 8 * t + 8) for t in range(TT)]

            def both(step):
                for t, s8 in enumerate(tiles):
                    last = step(t, s8)
                link(last)

            both(lambda t, s8: dve.max(best[:, s8], rl[:, s8]))
            both(lambda t, s8: dve.max_index(topi[:, s8], best[:, s8], rl[:, s8]))
            dve.tensor_tensor(e2[:, 0:2], best[:, 1:16:8], best[:, 0:16:8], ALU.subtract).then_inc(gate_ask, 1)
            link(dve.tensor_copy(besti, topi[:, :]))
            both(lambda t, s8: dve.tensor_scalar(oh1[:, s8], iota[:, 0:8], besti[:, 8 * t:8 * t + 1], None, ALU.is_equal))
            both(lambda t, s8: dve.tensor_scalar(oh2[:, s8], iota[:, 0:8], besti[:, 8 * t + 1:8 * t + 2], None, ALU.is_equal))
            dve.tensor_tensor(chosen, oh1, oh2, ALU.add).then_inc(route_ready, 1)
            dve.wait_ge(gate_got, 1)
            link(dve.tensor_scalar(ms[:, 0:2], e2[:, 2:4], 1.0, None, ALU.add))
            link(dve.reciprocal(ms[:, 2:4], ms[:, 0:2]))
            link(dve.tensor_tensor(ms[:, 4:6], e2[:, 2:4], ms[:, 2:4], ALU.mult))
            both(lambda t, s8: dve.tensor_scalar(comb[:, s8], oh1[:, s8], ms[:, 2 + t:3 + t], None, ALU.mult))
            both(lambda t, s8: dve.scalar_tensor_tensor(comb[:, s8], oh2[:, s8], ms[:, 4 + t:5 + t], comb[:, s8],
                                                        ALU.mult, ALU.add))
            for r in range(2):
                e_ = slice(r * 8, r * 8 + 8)
                both(lambda t, s8: dve.tensor_copy(table[:, e_, 2 + t], chosen[:, s8]))
                both(lambda t, s8: dve.tensor_copy(table[:, e_, 4 + t], comb[:, s8]))
            dve.wait_ge(step_evac, STEPS_ROUTER + 1)
            for r in range(2):
                both(lambda t, s8: dve.tensor_scalar(table[:, r * 8:r * 8 + 8, t], slot[:, s8], -1.0 - P * r, None, ALU.add))
            def dispatch(e):
                dve.tensor_copy(cur[:, :], table[:, bass.ds(e, 1), :].rearrange("p a n -> p (a n)")).then_inc(cur_ready, 1)
                dve.wait_ge(cur_ready, e + 1)
                for t in range(TT):
                    last = dve.tensor_scalar(disp[:, t, :], iota[:, :], cur[:, t:t + 1], cur[:, 2 + t:3 + t],
                                             ALU.is_equal, ALU.mult)
                last.then_inc(disp_ready, 1)

            def lower_gathered(n):
                for i in range(2):
                    dve.wait_ge(xe_ready, n * 2 + (i - 1))
                    k = slice(4 * i, 4 * i + 4)
                    dve.tensor_tensor(xTl[:, k, 0:P], bank[6 + i].rearrange("p (k t) -> p k t", k=4),
                                      xTh[:, k, 0:P].bitcast(F32), ALU.subtract).then_inc(xe_low, 1)

            def expert_gate(c, e):
                dve.wait_ge(m_silu, e * NCH_M + (c + 1))
                if c >= 2:
                    dve.wait_ge(m_tr, e * NCH_M + (c - 1))
                dve.tensor_tensor(hn[:, c % 2, :], hs[:, c % 2, :], bank[c % 2][:, FC:2 * FC], ALU.mult)\
                   .then_inc(m_gate, 1)

            dispatch(0)
            link(dve.tensor_reduce(trip_f[0:1, 0:1], counts[0:1, :], AX.X, ALU.max))
            link(dve.tensor_scalar(trip_f[0:1, 1:2], trip_f[0:1, 0:1], P + 0.5, float(NE), ALU.is_gt, ALU.mult))
            dve.tensor_scalar(trip_i[:, :], trip_f[0:1, 1:2], float(NE), None, ALU.add).then_inc(trip_ready, 1)
            link(dve.memset(dispT[:, :], 0.0))
            dve.memset(y[:, 0, :], 0.0).then_inc(ye_ready, 1)
            lower_gathered(1)
            for t in range(TT):
                link(dve.tensor_scalar(u[:, t, :], x[:, t, :], ALPHA, None, ALU.mult))
            dve.wait_ge(trip_ready, 1)
            trips = dve.value_load(trip_i[0:1, 0:1], min_val=NE, max_val=2 * NE)
            def scatter_add(e, i):
                t, n = i // 2, i % 2
                dve.wait_ge(sc_done, e * 4 + (i + 1))
                s_ = u[:, t, n * 512:(n + 1) * 512]
                dve.tensor_tensor(s_, s_, bank[(6, 2)[t] + n][:, :], ALU.add).then_inc(sc_added, 1)

            def lower_piece(e, p):
                j = p % 2
                if j == 0:
                    here[0] = halves.place()
                u_, _, i, n = here[0]
                dve.wait_ge(piece_high, e * PIECES + (p - 3))
                c = slice(j * 1024, (j + 1) * 1024)
                dve.tensor_tensor(wl[:, i, c], ring[:, u_, c], wh[:, i, c].bitcast(F32), ALU.subtract)\
                   .then_inc(taken[0][u_] if j == 1 else first_low, 1)

            def expert_low(c, e):
                dve.wait_ge(m_high, e * NCH_M + (c + 1))
                dve.tensor_tensor(hTl[:, c % 2, :, 0:P], bank[2 + c % 2][:, 0:FC].rearrange("p (f t) -> p f t", f=2),
                                  hTh[:, c % 2, :, 0:P].bitcast(F32), ALU.subtract).then_inc(m_low, 1)

            here = [None]
            with dve.Fori(0, trips) as e:
                halves.at(0, LENGTHS[0] + 2, e * L_BODY, e * (L_BODY // UNITS))
                for p in range(4, PIECES + 4):
                    for c in range(NCH_M):
                        if p == silu_at(c):
                            expert_gate(c, e)
                        if p == copy_at(c):
                            expert_low(c, e)
                    for i, at_ in enumerate(ADDED_AT):
                        if p == at_:
                            scatter_add(e, i)
                    if p == 16:
                        dve.wait_ge(pt_done, e + 1)
                        dispatch(e + 1)
                    if p == GATHERED_AT:
                        lower_gathered(e + 2)
                    lower_piece(e, p)
                dve.wait_ge(m_down, e * NCH_M + NCH_M)
                dve.tensor_scalar(y[:, 0, 512:1024], bank[5][:, :], slotg[:, 0:1], None, ALU.mult).then_inc(ye_ready, 1)
            for i in range(4):
                scatter_add(trips, i)
            halves.at(1, 0)
            dve.wait_ge(sc_added, trips * 4 + 4)
            layer_norm(u)

            rms_norm(u, 0, (x_half, x_ready))
            dve.memset(upad[:, 0:3, 0:CONV - 1], 0.0)
            lower_transposed()
            for _ in range(3):
                lower()
            dve.wait_ge(conv_in, 1)
            link(dve.tensor_tensor(upad[:, 0:3, CONV - 1:], ta[:, 0:3, :], tb[:, 0:3, :], ALU.mult))
            taps = [0]

            def next_tap():
                j = taps[0]
                taps[0] += 1
                for c in range(3):
                    if j == 0:
                        last = dve.tensor_scalar(ta[:, c, :], upad[:, c, 0:T], cw[:, c, 0:1], cw[:, c, 31:32], ALU.mult, ALU.add)
                    else:
                        last = dve.scalar_tensor_tensor(ta[:, c, :], upad[:, c, j:j + T], cw[:, c, j:j + 1], ta[:, c, :],
                                                        ALU.mult, ALU.add)
                link(last)

            while taps[0] < CONV - 16:
                next_tap()
                if taps[0] % 3 == 0:
                    lower()
            dve.wait_ge(rel_in[2], 16)
            attention(3, relative(), 0, two_units, taps=2)
            assert taps[0] == CONV
            dve.nop().then_inc(conv_done, 1)
            lower_transposed(range(2))
            dve.wait_ge(step_evac, STEPS_CONV)
            dve.wait_ge(late_in, 80)
            moments(lambda t: nr[:, t, :], range(TT), 512)
            for t in range(TT):
                link(dve.scalar_tensor_tensor(nr[:, t, :], nr[:, t, :], mv[:, 2 * t:2 * t + 1], convg,
                                              ALU.subtract, ALU.mult))
                dve.scalar_tensor_tensor(nr[:, t, :], nr[:, t, :], rstd[:, t:t + 1], convb,
                                         ALU.mult, ALU.add).then_inc(conv_n, 1)
            lower()
            lower_transposed(range(2, 4))
            lower()
            halves.skip()
            rms_norm(u, 1, (x_half, x_ready), sums_done, 3)
            lower_transposed()
            lower()
            ffn(1)
            rms_norm(u, 2, (fin, fin), down_done[1], NCH_D)

        @block.gpsimd
        def _(pool):
            def weights(n, rows):
                if n >= 1:
                    pool.wait_ge(x_ready, n)
                for i, r in enumerate(rows):
                    pool.dma_start(lnw[:, i, :], r.broadcast_to([P, D])).then_inc(ln_in, 16)

            def bias_table(i):
                src = bass.AP(rel_dram.tensor, i * P * H * REL + P - 1, [[H * REL - 1, P], [REL, H], [1, T]])
                pool.dma_start(bias[:, :, :], src).then_inc(rel_in[i], 16)

            def rstd_of(n):
                asked[0] += 1
                pool.wait_ge(rs_ask, asked[0])
                pool.tensor_tensor(rstd8[:, 0:n], e2[:, 0:n], half[:, 0:n], ALU.pow).then_inc(rs_got, 1)

            def rstd_tiles():
                for t in range(TT):
                    asked[0] += 1
                    pool.wait_ge(rs_ask, asked[0])
                    pool.tensor_tensor(rstd8[:, t:t + 1], e2[:, t:t + 1], half[:, 0:1], ALU.pow).then_inc(rs_got, 1)

            halves = Split()

            def lower(s_, n):
                halves.at(s_, n)
                u_, _, i, n = halves.place()
                pool.wait_ge(hi_ready[s_], n + 1)
                pool.tensor_tensor(wl[:, i, :], ring[:, u_, :], wh[:, i, :].bitcast(F32), ALU.subtract)\
                    .then_inc(taken[s_][u_], 1)

            def link(ins):
                chain[0] += 1
                ins.then_inc(g_chain, 1)
                pool.wait_ge(g_chain, chain[0])

            chain = [0]
            asked = [0]
            weights(0, (ln_g[0, 0:1, :], ln_b[0, 0:1, :]))
            for i in range(3):
                pool.wait_ge(step_evac, 7 + i)
                pool.dma_start(rel_dram[i].rearrange("t h j -> h t j"),
                               relrow[:, i, :].unsqueeze(1).broadcast_to([H, P, REL])).then_inc(rel_out, 16)
            pool.wait_ge(rel_out, 48)
            bias_table(0)
            pool.wait_ge(filled, 3)
            rstd_of(8)
            pool.wait_ge(a_done, 2)
            bias_table(1)
            lower(0, 18)
            rstd_tiles()
            weights(1, (ln_g[0, 1:2, :], ln_b[0, 1:2, :]))
            pool.dma_start(rowsel[:, :, :], c_rowsel).then_inc(late_in, 16)
            lower(0, 18 + 3 * NCH_D)
            rstd_tiles()
            weights(2, (ln_g[1, 0:1, :], ln_b[1, 0:1, :]))
            pool.wait_ge(a_done, 6)
            bias_table(2)
            pool.wait_ge(late_in, 16)
            pool.dma_start(convw[0:31, :], conv_w_2[0]).then_inc(late_in, 16)
            pool.dma_start(convw[31:32, :], conv_b_2).then_inc(late_in, 16)
            pool.dma_start(convg[:, :], conv_ln_g_2.broadcast_to([P, 512])).then_inc(late_in, 16)
            pool.dma_start(convb[:, :], conv_ln_b_2.broadcast_to([P, 512])).then_inc(late_in, 16)
            lower(0, LENGTHS[0])
            rstd_tiles()
            weights(3, (ln_g[1, 1:2, :], ln_b[1, 1:2, :]))
            pool.dma_start(mixg, mix_norm_g_2.broadcast_to([P, D])).then_inc(ln_in, 16)
            rstd_tiles()
            rstd_tiles()
            weights(5, (ffn_norm_g_2,))
            product = nw[:, 0, 0:T]
            pool.memset(upad[:, 3, 0:CONV - 1], 0.0)
            pool.wait_ge(conv_in, 1)
            link(pool.tensor_tensor(upad[:, 3, CONV - 1:], ta[:, 3, :], tb[:, 3, :], ALU.mult))
            for j in range(CONV):
                factor = cw[:, 3, j:j + 1].broadcast_to([P, T])
                if j == 0:
                    link(pool.tensor_tensor(ta[:, 3, :], upad[:, 3, 0:T], factor, ALU.mult))
                    link(pool.tensor_tensor(ta[:, 3, :], ta[:, 3, :], cw[:, 3, 31:32].broadcast_to([P, T]), ALU.add))
                else:
                    link(pool.tensor_tensor(product, upad[:, 3, j:j + T], factor, ALU.mult))
                    link(pool.tensor_tensor(ta[:, 3, :], ta[:, 3, :], product, ALU.add))
            pool.nop().then_inc(conv_done, 1)
            rstd_of(2)
            lower(1, 12)
            rstd_tiles()
            weights(6, (final_norm_g_2.rearrange("(a d) -> a d", a=1),))
            rstd_tiles()


def constants():
    import numpy as np

    t = np.arange(T)
    cum = (t[:, None] <= t[None, :]).astype(np.float32).reshape(TT, P, T).transpose(1, 0, 2)
    dist = np.arange(255, 255 - REL, -1)

    def bucket(furthest):
        d = np.maximum(dist, 1).astype(np.float32)
        far = 16 + (np.log(d / np.float32(16)) / np.float32(np.log(furthest / 16)) * np.float32(16)).astype(np.int32)
        return np.where(dist < 16, np.maximum(dist, 0), np.minimum(far, 31))

    onehot = np.stack([(bucket(f)[None, :] == np.arange(32)[:, None]) for f in (2048, 128)], 1).astype(np.float32)
    times = (dist <= 128).astype(int) + (dist % 4 == 0) + (dist % 16 == 0)
    past = dist >= 0
    plain = np.where(past, 0.0, NEG)
    dilated = np.where(past & (times > 0), np.log(np.maximum(times, 1)), NEG)
    rowadd = np.stack([plain, dilated, plain])[None].astype(np.float32)
    rowsel = np.zeros((8, 8, P), np.float32)
    for h in range(8):
        rowsel[h, h] = 1
    q = P + np.arange(P)
    return {
        "c_ident": np.eye(P, dtype=np.float32),
        "c_cum": np.ascontiguousarray(cum),
        "c_causal": np.where(t[None, :] <= q[:, None], 0.0, NEG).astype(np.float32),
        "c_iota": np.broadcast_to(np.arange(P, dtype=np.float32), (P, P)).copy(),
        "c_onehot": onehot,
        "c_rowadd": rowadd,
        "c_rowsel": rowsel,
    }


INS = ["x", "ln_g", "ln_b", "rel_table", "w_in_ab", "w_gate_a", "b_gate_a", "g_norm_a", "w_out_ab", "w_in_cd",
       "b_forget", "w_out_cd", "w1_dense", "w3_dense", "w2_dense", "w_router", "w1_moe", "w3_moe", "w2_moe",
       "mix_norm_g_2", "w_in_2", "rel_bias_2", "conv_w_2", "conv_b_2", "conv_ln_g_2", "conv_ln_b_2", "w_out_2",
       "ffn_norm_g_2", "w_gate_2", "w_up_2", "w_down_2", "final_norm_g_2"]


def kernel(**inputs):
    import numpy as np
    import concourse.bacc as bacc
    from concourse.bass_utils import run_bass_kernel_spmd

    nc = bacc.Bacc("TRN2", target_bir_lowering=False, num_devices=1)
    arrays, args = {}, []
    for name, a in [(n, np.ascontiguousarray(inputs[n])) for n in INS] + list(constants().items()):
        arrays[f"in_{name}"] = a
        args.append(nc.dram_tensor(f"in_{name}", a.shape, mybir.dt.from_np(a.dtype), kind="ExternalInput").ap())
    args.append(nc.dram_tensor("out_0", (1, T, D), F32, kind="ExternalOutput").ap())
    build(nc, *args)
    r = run_bass_kernel_spmd(nc, [arrays], core_ids=[0])
    return r.results[0]["out_0"]
```
